# Optimizing a Trainium2 kernel written in Bass

```python
import math
import jax, jax.numpy as jnp
from jax import lax
import numpy as np

D_MODEL = 1024
BATCH = 1
SEQ = 512
DEPTH = 1
DEC_BATCH = 8
DEC_SEQ = 4
PAST_LEN = 4096
PAGE_SIZE = 128

MIX_WIDTH = D_MODEL
ATTN_WIDTH = D_MODEL // 2
POOL_WIDTH = MIX_WIDTH - ATTN_WIDTH
HEAD_DIM = 64
N_HEADS = ATTN_WIDTH // HEAD_DIM
IN_WIDTH = 3 * ATTN_WIDTH + POOL_WIDTH
POOL_WINDOWS = (2, 4, 8, 16)
N_POOL_GROUPS = len(POOL_WINDOWS)
POOL_GROUP = POOL_WIDTH // N_POOL_GROUPS
POOL_STATE = max(POOL_WINDOWS) - 1
MOBA_BLOCK = 256
MOBA_TOPK = 3
N_BUCKETS = 32
MAX_DISTANCE = 128
D_FF = 4 * D_MODEL
N_MOD = 6
QCHUNK = 64
EPS = 1e-6
NEG = -1e30
SCALE = HEAD_DIM ** -0.5

kernel_name = 'hymba_moba_pool_adaln_decode_step'

def rms_norm(x, g):
    xf = x.astype(jnp.float32)
    y = xf * lax.rsqrt(jnp.mean(xf * xf, axis=-1, keepdims=True) + EPS)
    return (y * g.astype(jnp.float32)).astype(x.dtype)

def ada_modulation(c, w_ada, b_ada):
    m = jax.nn.silu(c) @ w_ada + b_ada
    return jnp.split(m[:, None, :], N_MOD, axis=-1)

def t5_bucket(rel):
    n = jnp.maximum(rel, 0)
    max_exact = N_BUCKETS // 2
    nf = jnp.maximum(n, max_exact).astype(jnp.float32)
    large = max_exact + (jnp.log(nf / max_exact) / math.log(MAX_DISTANCE / max_exact)
                         * (N_BUCKETS - max_exact)).astype(jnp.int32)
    large = jnp.minimum(large, N_BUCKETS - 1)
    return jnp.where(n < max_exact, n, large)

def moba_attend(qc, qpos, rel_bias, k_own, v_own, kpos_own, sel_part):
    bias_tab = rel_bias.T.astype(jnp.float32)
    rel = qpos[:, None] - kpos_own[None, :]
    s_own = (jnp.einsum('bhcd,bhkd->bhck', qc, k_own, preferred_element_type=jnp.float32) * SCALE
             + bias_tab[:, t5_bucket(rel)])
    s_own = jnp.where(rel >= 0, s_own, NEG)
    if sel_part is None:
        p = jax.nn.softmax(s_own, axis=-1).astype(v_own.dtype)
        return jnp.einsum('bhck,bhkd->bhcd', p, v_own)
    k_sel, v_sel, kpos_sel, sel_ok = sel_part
    B, H, C, n, K = kpos_sel.shape
    h_ix = jnp.arange(H)[None, :, None, None, None]
    rel_s = qpos[None, None, :, None, None] - kpos_sel
    s_sel = (jnp.einsum('bhcd,bhcnkd->bhcnk', qc, k_sel, preferred_element_type=jnp.float32) * SCALE
             + bias_tab[h_ix, t5_bucket(rel_s)])
    if sel_ok is not None:
        s_sel = jnp.where(sel_ok[..., None], s_sel, NEG)
    logits = jnp.concatenate([s_sel.reshape(B, H, C, n * K), s_own], axis=-1)
    p = jax.nn.softmax(logits, axis=-1).astype(v_own.dtype)
    p_sel = p[..., :n * K].reshape(B, H, C, n, K)
    return (jnp.einsum('bhcnk,bhcnkd->bhcd', p_sel, v_sel)
            + jnp.einsum('bhck,bhkd->bhcd', p[..., n * K:], v_own))

def moba_prompt(q, k, v, rel_bias):
    B, S = q.shape[:2]
    nb = -(-S // MOBA_BLOCK)
    pad = nb * MOBA_BLOCK - S

    def blocks(t):
        t = jnp.pad(t, ((0, 0), (0, pad), (0, 0), (0, 0)))
        return t.reshape(B, nb, MOBA_BLOCK, N_HEADS, HEAD_DIM).transpose(0, 3, 1, 2, 4)

    kb, vb = blocks(k), blocks(v)
    kmean = jnp.mean(kb.astype(jnp.float32), axis=3)
    n_sel = min(MOBA_TOPK, nb - 1)
    qh = q.transpose(0, 2, 1, 3)
    b_ix = jnp.arange(B)[:, None, None, None]
    h_ix = jnp.arange(N_HEADS)[None, :, None, None]
    blk_off = jnp.arange(MOBA_BLOCK)

    def chunk(ci):
        start = ci * QCHUNK
        qc = lax.dynamic_slice_in_dim(qh, start, QCHUNK, axis=2)
        qpos = start + jnp.arange(QCHUNK)
        own = start // MOBA_BLOCK
        k_own = lax.dynamic_index_in_dim(kb, own, axis=2, keepdims=False)
        v_own = lax.dynamic_index_in_dim(vb, own, axis=2, keepdims=False)
        kpos_own = own * MOBA_BLOCK + blk_off
        if n_sel == 0:
            return moba_attend(qc, qpos, rel_bias, k_own, v_own, kpos_own, None)
        gate = jnp.einsum('bhcd,bhnd->bhcn', qc.astype(jnp.float32), kmean)
        gate = jnp.where(jnp.arange(nb) < own, gate, NEG)
        _, sel = lax.top_k(gate, n_sel)
        k_sel = kb[b_ix, h_ix, sel]
        v_sel = vb[b_ix, h_ix, sel]
        kpos_sel = sel[..., None] * MOBA_BLOCK + blk_off
        return moba_attend(qc, qpos, rel_bias, k_own, v_own, kpos_own,
                           (k_sel, v_sel, kpos_sel, sel < own))

    out = lax.map(chunk, jnp.arange(S // QCHUNK))
    return out.transpose(1, 0, 3, 2, 4).reshape(B, S, ATTN_WIDTH)

def moba_sample(q, k, v, cache_k, cache_v, layer, page_table, rel_bias):
    DB, T = q.shape[:2]
    ppb = MOBA_BLOCK // PAGE_SIZE
    own = PAST_LEN // MOBA_BLOCK
    n_sel = min(MOBA_TOPK, own)
    r_pages = PAST_LEN // PAGE_SIZE - own * ppb
    qh = q.transpose(0, 2, 1, 3)
    qpos = PAST_LEN + jnp.arange(T)
    own_pages = page_table[:, own * ppb: own * ppb + r_pages]

    def own_rows(cache, new):
        past = cache[layer, own_pages].reshape(DB, r_pages * PAGE_SIZE, N_HEADS, HEAD_DIM)
        return jnp.concatenate([past.astype(new.dtype), new], axis=1).transpose(0, 2, 1, 3)

    k_own, v_own = own_rows(cache_k, k), own_rows(cache_v, v)
    kpos_own = own * MOBA_BLOCK + jnp.arange(r_pages * PAGE_SIZE + T)
    sel_part = None
    if n_sel > 0:
        past = cache_k[layer, page_table[:, :own * ppb]].astype(jnp.float32)
        kmean = jnp.mean(past.reshape(DB, own, MOBA_BLOCK, N_HEADS, HEAD_DIM), axis=2).transpose(0, 2, 1, 3)
        gate = jnp.einsum('bhtd,bhnd->bhtn', qh.astype(jnp.float32), kmean)
        _, sel = lax.top_k(gate, n_sel)
        b_ix = jnp.arange(DB)[:, None, None, None, None]
        phys = page_table[b_ix, sel[..., None] * ppb + jnp.arange(ppb)]
        h_ix = jnp.arange(N_HEADS)[None, :, None, None, None, None]

        def gather(cache):
            g = cache[layer, phys[..., None], jnp.arange(PAGE_SIZE), h_ix]
            return g.reshape(DB, N_HEADS, T, n_sel, MOBA_BLOCK, HEAD_DIM).astype(q.dtype)

        kpos_sel = sel[..., None] * MOBA_BLOCK + jnp.arange(MOBA_BLOCK)
        sel_part = (gather(cache_k), gather(cache_v), kpos_sel, None)
    out = moba_attend(qh, qpos, rel_bias, k_own, v_own, kpos_own, sel_part)
    return out.transpose(0, 2, 1, 3).reshape(DB, T, ATTN_WIDTH)

def multi_pool(u_full, first_pos, w_pool, pool_scale):
    B, L, _ = u_full.shape
    uf = u_full.astype(jnp.float32)
    cs = jnp.pad(jnp.cumsum(uf, axis=1), ((0, 0), (1, 0), (0, 0)))
    pos = first_pos + jnp.arange(L)
    diffs = []
    for g, w in enumerate(POOL_WINDOWS):
        sl = slice(g * POOL_GROUP, (g + 1) * POOL_GROUP)
        cg = cs[..., sl]
        lower = jnp.pad(cg, ((0, 0), (w - 1, 0), (0, 0)))[:, :L]
        cnt = jnp.minimum(pos + 1, w).astype(jnp.float32)[None, :, None]
        diffs.append((cg[:, 1:] - lower) / cnt - uf[..., sl])
    d = jnp.stack(diffs, axis=2).astype(u_full.dtype)
    y = jnp.einsum('blgc,gcd->blgd', d, w_pool).reshape(B, L, POOL_WIDTH)
    return y * pool_scale

def layer_in(x, c, w_ada, b_ada, norm_mix, w_in):
    mods = ada_modulation(c, w_ada, b_ada)
    h = rms_norm(x, norm_mix) * (1 + mods[1]) + mods[0]
    B, L, _ = x.shape
    q, k, v, u = jnp.split(h @ w_in, [ATTN_WIDTH, 2 * ATTN_WIDTH, 3 * ATTN_WIDTH], axis=-1)
    heads = lambda t: t.reshape(B, L, N_HEADS, HEAD_DIM)
    return mods, heads(q), heads(k), heads(v), u

def layer_out(x, attn, pool, mods, w_out, norm_mlp, w_up, w_down):
    _, _, g1, sh2, sc2, g2 = mods
    x = x + g1 * (jnp.concatenate([attn, pool], axis=-1) @ w_out)
    h = rms_norm(x, norm_mlp) * (1 + sc2) + sh2
    return x + g2 * (jnp.square(jax.nn.relu(h @ w_up)) @ w_down)

def setup_inputs(seed: int = 0) -> dict:
    key = jax.random.key(seed)
    ks = jax.random.split(key, 24)
    n_pages = PAST_LEN // PAGE_SIZE
    n_phys = (DEC_BATCH * n_pages * 5) // 4
    f32 = jnp.float32

    def nrm(k, shape, s):
        return jax.random.normal(k, shape, f32) * s

    page_table = jax.random.permutation(ks[5], n_phys)[:DEC_BATCH * n_pages]
    page_table = page_table.reshape(DEC_BATCH, n_pages).astype(jnp.int32)
    return {
        'x_prompt': nrm(ks[0], (BATCH, SEQ, D_MODEL), 1.0),
        'x_sample': nrm(ks[1], (DEC_BATCH, DEC_SEQ, D_MODEL), 1.0),
        'cache_k': nrm(ks[2], (DEPTH, n_phys, PAGE_SIZE, N_HEADS, HEAD_DIM), 1.0),
        'cache_v': nrm(ks[3], (DEPTH, n_phys, PAGE_SIZE, N_HEADS, HEAD_DIM), 1.0),
        'state_pool': nrm(ks[4], (DEPTH, DEC_BATCH, POOL_STATE, POOL_WIDTH), 1.0),
        'page_table': page_table,
        'c_prompt': nrm(ks[6], (BATCH, D_MODEL), 1.0),
        'c_sample': nrm(ks[7], (DEC_BATCH, D_MODEL), 1.0),
        'w_ada': nrm(ks[8], (DEPTH, D_MODEL, N_MOD * D_MODEL), 0.02),
        'b_ada': nrm(ks[9], (DEPTH, N_MOD * D_MODEL), 0.01),
        'norm_mix': 1.0 + nrm(ks[10], (DEPTH, D_MODEL), 0.1),
        'w_in': nrm(ks[11], (DEPTH, D_MODEL, IN_WIDTH), D_MODEL ** -0.5),
        'rel_bias': nrm(ks[12], (N_BUCKETS, N_HEADS), 0.5),
        'w_pool': nrm(ks[13], (DEPTH, N_POOL_GROUPS, POOL_GROUP, POOL_GROUP), POOL_GROUP ** -0.5),
        'pool_scale': 1.0 + nrm(ks[14], (DEPTH, POOL_WIDTH), 0.1),
        'w_out': nrm(ks[15], (DEPTH, MIX_WIDTH, D_MODEL), MIX_WIDTH ** -0.5),
        'norm_mlp': 1.0 + nrm(ks[16], (DEPTH, D_MODEL), 0.1),
        'w_up': nrm(ks[17], (DEPTH, D_MODEL, D_FF), D_MODEL ** -0.5),
        'w_down': nrm(ks[18], (DEPTH, D_FF, D_MODEL), D_FF ** -0.5),
        'norm_final': 1.0 + nrm(ks[19], (D_MODEL,), 0.1),
    }

def reference(x_prompt, x_sample, cache_k, cache_v, state_pool, page_table, c_prompt, c_sample,
              w_ada, b_ada, norm_mix, w_in, rel_bias, w_pool, pool_scale, w_out, norm_mlp,
              w_up, w_down, norm_final):
    xp, xs = x_prompt, x_sample
    kp, vp, pp, ksm, vsm, psm = [], [], [], [], [], []
    for l in range(DEPTH):
        mods, q, k, v, u = layer_in(xp, c_prompt, w_ada[l], b_ada[l], norm_mix[l], w_in[l])
        attn = moba_prompt(q, k, v, rel_bias)
        pool = multi_pool(u, 0, w_pool[l], pool_scale[l])
        xp = layer_out(xp, attn, pool, mods, w_out[l], norm_mlp[l], w_up[l], w_down[l])
        kp.append(k)
        vp.append(v)
        pp.append(u[:, -POOL_STATE:])
        mods, q, k, v, u = layer_in(xs, c_sample, w_ada[l], b_ada[l], norm_mix[l], w_in[l])
        attn = moba_sample(q, k, v, cache_k, cache_v, l, page_table, rel_bias)
        u_full = jnp.concatenate([state_pool[l].astype(u.dtype), u], axis=1)
        pool = multi_pool(u_full, PAST_LEN - POOL_STATE, w_pool[l], pool_scale[l])[:, POOL_STATE:]
        xs = layer_out(xs, attn, pool, mods, w_out[l], norm_mlp[l], w_up[l], w_down[l])
        ksm.append(k)
        vsm.append(v)
        psm.append(u_full[:, -POOL_STATE:])
    y_prompt = rms_norm(xp, norm_final)
    y_sample = rms_norm(xs, norm_final)
    return (y_prompt, y_sample, jnp.stack(kp), jnp.stack(vp), jnp.stack(pp),
            jnp.stack(ksm), jnp.stack(vsm), jnp.stack(psm))


_drawn_inputs = setup_inputs


def setup_inputs(seed=0):
    import zlib

    import numpy as np

    out = dict(_drawn_inputs(seed))
    spreads = {}
    factors = {'cache_k': 3.096, 'cache_v': 2.968, 'b_ada': 3.197, 'rel_bias': 2.906}
    for name, (base, spread) in spreads.items():
        noise = np.random.default_rng([zlib.crc32(name.encode()), seed]).standard_normal(out[name].shape)
        drawn = base * np.exp(spread * noise) if base else spread * noise
        out[name] = __import__('jax').numpy.asarray(drawn.astype(out[name].dtype))
    for name, factor in factors.items():
        out[name] = (out[name] * factor).astype(out[name].dtype)
    return out
```

```python
import math
from contextlib import ExitStack

import numpy as np

import concourse.bass as bass
from concourse import mybir

F32 = mybir.dt.float32
I32 = mybir.dt.int32
ALU = mybir.AluOpType
ACT = mybir.ActivationFunctionType
AX = mybir.AxisListType

P = 128
D = 1024
FT = D // P
S = 512
TT = S // P
DB, DT = 8, 4
NS = DB * DT
NH, HD = 8, 64
AW = NH * HD
HP = AW // P
NG = 4
WINDOWS = (2, 4, 8, 16)
STATE = 15
FF = 4096
PAGE = 128
PAGES = 32
N_PHYS = 320
BLOCKS = 16
PPB = 2
TOPK = 3
HT = NH * DT
NMOD = 6 * FT
SH1, SC1, G1, SH2, SC2, G2 = (i * FT for i in range(6))
EPS = 1e-6
NEG = -1e30
SCALE = HD ** -0.5
PIECE = 512
SLOTS = 8
VEC_MIX, VEC_MLP, VEC_POOL, VECS = NMOD, NMOD + FT, NMOD + 2 * FT, NMOD + 2 * FT + NG
REV = 2 * P + P - 1
C32 = {}
_at = 0
for _name, _n in (("rev", REV + 1), ("far", P), ("last", DT * P), ("own", DT * NS), ("ownmask", NS), ("lt", 256)):
    C32[_name] = (_at, _at + _n)
    _at += _n
C32_W = _at


def bucket(n):
    n = max(n, 0)
    if n < 16:
        return n
    return min(16 + int(math.log(n / 16) / math.log(8) * 16), 31)


def shape_constants():
    c128 = np.zeros((P, 2 * P + NG * 16), np.float32)
    c128[:, :P] = np.eye(P)
    for g, w in enumerate(WINDOWS):
        c128[:, P + 16 * g:P + 16 * g + 16] = 1.0 / np.minimum(np.arange(16) + 1, w)
    c128[:, P + NG * 16:] = np.eye(P)[::-1]
    c32 = np.zeros((32, C32_W), np.float32)
    cmask = np.zeros((NH, REV), np.float32)
    o = C32["rev"][0]
    for i in range(REV):
        rel = 2 * P - 1 - i
        if rel >= 0:
            c32[bucket(rel), o + i] = 1.0
        else:
            cmask[:, i] = NEG
    c32[31, C32["far"][0]:C32["far"][1]] = 1.0
    o = C32["last"][0]
    for t in range(DT):
        for key in range(P):
            c32[bucket(P + t - key), o + t * P + key] = 1.0
    o = C32["own"][0]
    for t in range(DT):
        for r in range(NS):
            c32[bucket(t - r % DT), o + t * NS + r] = 1.0
    o = C32["ownmask"][0]
    for r in range(NS):
        for b in range(DB):
            for t in range(DT):
                if r // DT != b or r % DT > t:
                    c32[r, o + b * DT + t] = NEG
    o = C32["lt"][0]
    for n in range(BLOCKS):
        for m in range(n):
            c32[:, o + n * BLOCKS + m] = 1.0
    return c128, c32, cmask


def decoder_step(nc, x_prompt, x_sample, cache_k, cache_v, state_pool, page_table, c_prompt, c_sample, w_ada, b_ada,
                 norm_mix, w_in, rel_bias, w_pool, pool_scale, w_out, norm_mlp, w_up, w_down, norm_final,
                 c128, c32, cmask,
                 y_prompt, y_sample, k_prompt, v_prompt, pool_prompt, k_sample, v_sample, pool_sample):
    ctx = ExitStack()
    with ctx:
        def sb(name, shape, dt=F32):
            return ctx.enter_context(nc.sbuf_tensor(name, shape, dt))

        def sem(name):
            return ctx.enter_context(nc.semaphore(name))

        cst = sb("cst", [P, 2 * P + NG * 16])
        flip = cst[:, P + NG * 16:2 * P + NG * 16]
        ident = cst[:, 0:P]
        inv_count = cst[:, P:P + NG * 16].rearrange("p (g c) -> p g c", g=NG)
        ones = sb("ones", [P, P])
        eps = sb("eps", [P, 1])
        pages = sb("pages", [1, DB * PAGES], I32)
        xT = sb("xT", [P, FT, S])
        hT = sb("hT", [P, FT, S])
        mixT = sb("mixT", [P, FT, S])
        gT = sb("gT", [P, HP, S])
        W = sb("W", [P, 4, 4096])
        ring = sb("ring", [P, SLOTS, PPB, 512])
        ktb = sb("ktb", [P, 2, HP, PPB * P])
        scn = sb("scn", [P, NH * 2 * P])
        nearb = scn[:, :].rearrange("p (h n) -> p h n", h=NH)
        sc = scn[:, 0:PAGES * HT].rearrange("p (n c) -> p n c", n=PAGES)
        nfb = scn[:, D:2 * D]
        smp = sb("smp", [P, 2, PAGES + 1, HT])
        masked, probs = smp[:, 0], smp[:, 1]
        QBD = sb("QBD", [P, DB, HP, HT])
        qcur = sb("qcur", [P, HP, HT])
        xTs = sb("xTs", [P, FT, NS])
        hTs = sb("hTs", [P, FT, NS])
        mixS = sb("mixS", [P, FT, NS])
        kTs = sb("kTs", [P, HP, NS])
        vS = sb("vS", [NS, AW])
        uS = sb("uS", [P, NG, DB, STATE + DT])
        uSn = sb("uSn", [P, NG, NS])
        mods = sb("mods", [P, NMOD, 1 + DB])
        vecs = sb("vecs", [P, VECS])
        cT = sb("cT", [P, FT, 1 + DB])
        rstd = sb("rstd", [P, S])
        rstds = sb("rstds", [P, NS])
        farb = sb("farb", [P, NH])
        farbt = sb("farbt", [P, HT])
        lastb = sb("lastb", [P, HT])
        own = sb("own", [NS, DB, HT])
        ownb = sb("ownb", [NS, HT])
        ownmask = sb("ownmask", [NS, NS])
        lt = sb("lt", [HT, 256])
        kmean = sb("kmean", [P, HP, BLOCKS])
        gate = sb("gate", [HT, BLOCKS])
        cmps = sb("cmps", [P, 2 * BLOCKS * BLOCKS])
        cmpa, cmpb = (cmps[0:HT, i * 256:(i + 1) * 256].rearrange("p (n m) -> p n m", n=BLOCKS) for i in range(2))
        rank = sb("rank", [HT, BLOCKS])
        wpool = sb("wpool", [P, NG, P])
        diag = wpool[0:HT, :, :].rearrange("p g d -> p (g d)").rearrange("p (n c) -> p n c", n=BLOCKS)
        colmax = sb("colmax", [P, HT])
        rowmax = sb("rowmax", [HT, 1])
        dmax = sb("dmax", [HT, HT])
        colsum = sb("colsum", [P, HT])
        rden = sb("rden", [P, HT])
        stat = sb("stat", [P, 4])
        mod_a = sb("mod_a", [P, 2, FT, 1 + DB])
        gS = sb("gS", [P, 2, HP, NS])
        tmpS = gS[:, :, :, :].rearrange("p a m n -> p (a m) n")
        fstat = sb("fstat", [P, TT + 1, 2])

        rw = ring[:, :, :, :].rearrange("p a b c -> p (a b c)")
        x_tok = mixT[:, :, :].rearrange("p a b -> p (a b)").rearrange("p (t d) -> p t d", t=TT)
        xs_tok = probs.rearrange("p a b -> p (a b)")[0:NS, 0:D]
        flipped = mixT[:, 0:4, :]
        c_tok = rw[0:1 + DB, 0:D]
        c_sig = rw[0:1 + DB, D:2 * D]
        vec_rows = rw[0:VECS, 2 * D:2 * D + P]
        st_rows = rw[0:DB * STATE, 2304:2304 + AW]
        const32 = rw[0:32, 3072:3072 + C32_W]
        bias_rows = rw[0:NH, 4864:4864 + REV]
        mask_rows = rw[0:NH, 5376:5376 + REV]
        relb = rw[0:32, 5888:5888 + NH]
        qT = gT
        kT = ktb[:, :, :, :].rearrange("p a b c -> p (a b c)").rearrange("p (h n) -> p h n", h=HP)
        v_tok = rw[:, 0:2048].rearrange("p (t n) -> p t n", t=TT)
        logits = rw[:, 2048:3072].rearrange("p (a n) -> p a n", a=2)
        pT = rw[:, 3072:4096].rearrange("p (a n) -> p a n", a=2)
        dT = rw[:, 4096:6144].rearrange("p (g n) -> p g n", g=NG)
        UP = S + 16
        win = [rw[:, 6144:6144 + UP], rw[:, 6144 + UP:6144 + 2 * UP]]
        rows_k = hT[:, 0:TT, :]
        uT = smp[:, :, :, :].rearrange("p a b c -> p (a b c)")[:, 0:NG * UP].rearrange("p (g n) -> p g n", g=NG)
        winS = cmps[:, 0:2 * DB * (STATE + DT)].rearrange("p (a b s) -> p a b s", a=2, b=DB)
        dS = sb("dS", [P, NG, NS])
        rows_s = hT[0:NS, TT:TT + 3, :]
        junk = ring[:, 2, :, :].rearrange("p a b -> p (a b)")
        ybuf = [ring[:, 4 + i, :, :].rearrange("p a b -> p (a b)") for i in (0, 1, 2, 3, -1)]
        PS = ctx.enter_context(nc.psum_tensor("PS", [P, 8, 512], F32))

        def bank(i, parts=P, n=512, off=0):
            return PS[0:parts, i, off:off + n]

        def sems(names):
            return [sem(n) for n in names.split()]

        x_in, c_in, vec_in, cst_in, st_in, pool_in, page_in, nf_in = sems(
            "x_in c_in vec_in cst_in st_in pool_in page_in nf_in")
        w_landed = [sem(f"w_landed{i}") for i in range(4)]
        kv_landed = [sem(f"kv_landed{i}") for i in range(SLOTS)]
        bias_out, bias_back, row_out, outs, y_out = sems("bias_out bias_back row_out outs y_out")
        kv_used = sem("kv_used")
        dve_init, qbd_zero, pads, c_exp, c_ready = sems("dve_init qbd_zero pads c_exp c_ready")
        small_ps, small_ev, xt_ps, xt_ev_act, xt_ev_dve = sems("small_ps small_ev xt_ps xt_ev_act xt_ev_dve")
        sq_done, ms_ps, root_done = sems("sq_done ms_ps root_done")
        ada_ps, ada_ev, bias_ps, bias_ev, h_ready = sems("ada_ps ada_ev bias_ps bias_ev h_ready")
        proj_ps, proj_ev, projs_ps, projs_ev = sems("proj_ps proj_ev projs_ps projs_ev")
        near_ps, near_ev = sems("near_ps near_ev")
        own_ps, own_ev, row_ps, row_ev = sems("own_ps own_ev row_ps row_ev")
        win_step, win_done, pool_ps, pool_ev, pools_ps, pools_ev = sems(
            "win_step win_done pool_ps pool_ev pools_ps pools_ev")
        at_scores, at_max, at_exp, at_norm, at_pT, at_pT_ev, at_out, at_out_ev = sems(
            "at_scores at_max at_exp at_norm at_pT at_pT_ev at_out at_out_ev")
        out_ps, out_ev, sq2_done, ms2_ps, root2_done, h2_ready = sems(
            "out_ps out_ev sq2_done ms2_ps root2_done h2_ready")
        dve_chain = sem("dve_chain")
        kt_ps, kt_ev, km, qk, sc_ev, q_cur = sems("kt_ps kt_ev km qk sc_ev q_cur")
        fin_pe, fin_dve, fin_exp, fin_chain, pv, at_s = sems("fin_pe fin_dve fin_exp fin_chain pv at_s")
        up_ps, relu_ev, sqr_ev, dn_ps, dn_ev = sems("up_ps relu_ev sqr_ev dn_ps dn_ev")
        so_ps, so_ev, ssq, sms_ps, sroot, h2s_ready = sems("so_ps so_ev ssq sms_ps sroot h2s_ready")
        sup_ps, srelu, ssqr, sdn_ps, xs_done = sems("sup_ps srelu ssqr sdn_ps xs_done")
        fin_ps, fin_ss, fin_root, fin_y = sems("fin_ps fin_ss fin_root fin_y")

        scratch = nc.dram_tensor("bias_scratch", [NH, REV], F32, kind="Internal").ap()
        block = ctx.enter_context(nc.Block())

        wada = w_ada.rearrange("l (k p) n -> (l p) k n", p=P)
        win_d = w_in.rearrange("l (k p) n -> (l p) k n", p=P)
        wout_d = w_out.rearrange("l (k p) n -> (l p) k n", p=P)
        wup_d = w_up.rearrange("l (k p) n -> (l p) k n", p=P)
        wdown_d = w_down.rearrange("l (c k p) n -> (l c) p k n", p=P, k=PIECE // P)
        ck = cache_k.rearrange("l n p h d -> (l n) p (h d)")
        cv = cache_v.rearrange("l n p h d -> (l n) p (h d)")
        kpd = k_prompt.rearrange("a b (t p) h d -> (a b t) p (h d)", p=P)
        vpd = v_prompt.rearrange("a b (t p) h d -> p (a b t) (h d)", p=P)
        ksd = k_sample.rearrange("a b t h d -> (a b t) (h d)")
        vsd = v_sample.rearrange("a b t h d -> (a b t) (h d)")
        ypd = y_prompt.rearrange("b (t p) d -> (b t) p d", p=P)
        ysd = y_sample.rearrange("b t d -> (b t) d")

        N_PRE = 18
        UP_SLOT, DOWN_SLOT = 2, 3
        PRE_USES = 4
        N_CH = FF // PIECE

        def pre_piece(n):
            if n < 4:
                return wada[:, :, n * PIECE:(n + 1) * PIECE]
            if n < 8:
                return win_d[:, :, (n - 4) * PIECE:(n - 3) * PIECE]
            if n < 16:
                return wada[:, :, (n - 4) * PIECE:(n - 3) * PIECE]
            return wout_d[:, :, (n - 16) * PIECE:(n - 15) * PIECE]

        def wslot(s, cols=PIECE):
            return W[:, s, :].rearrange("p (k n) -> p k n", n=cols)

        LAST = DB - 1

        def k_seq(b, j):
            return 2 * BLOCKS * b - BLOCKS + j

        def v_seq(b, j, more):
            return 2 * BLOCKS * b + (2 * BLOCKS if more else BLOCKS) + j

        def k_landed(b, j):
            return 16 * PPB * (4 * b - 2 + j // SLOTS + 1)

        def v_landed(b, j, more):
            return 16 * PPB * (4 * b + (4 if more else 2) + j // SLOTS + 1)

        ROWS = TT + 3
        FS = 5
        FC = 9
        WIN_STEPS = 2 * sum(range(1, NG + 1)) + NG * 5

        @block.sync
        def _(sp):
            sp.dma_start(c_tok[0:1, :], c_prompt).then_inc(c_in, 16)
            sp.dma_start(c_tok[1:1 + DB, :], c_sample).then_inc(c_in, 16)
            sp.dma_start(cst[:, :], c128).then_inc(cst_in, 16)
            sp.dma_start(x_tok, x_prompt.rearrange("b (t p) d -> p (b t) d", p=P)).then_inc(x_in, 16)
            sp.dma_start(xs_tok, x_sample.rearrange("b t d -> (b t) d")).then_inc(x_in, 16)
            for lo, hi, src in ((0, NMOD, b_ada), (VEC_MIX, VEC_MLP, norm_mix), (VEC_MLP, VEC_POOL, norm_mlp),
                                (VEC_POOL, VECS, pool_scale)):
                sp.dma_start(vec_rows[lo:hi, :], src.rearrange("l (k p) -> (l k) p", p=P)).then_inc(vec_in, 16)
            sp.dma_start(st_rows, state_pool.rearrange("l b s c -> (l b s) c")).then_inc(st_in, 16)
            sp.dma_start(const32, c32).then_inc(st_in, 16)
            sp.dma_start(mask_rows, cmask).then_inc(st_in, 16)
            sp.dma_start(relb, rel_bias).then_inc(st_in, 16)
            for n in range(4):
                sp.dma_start(wslot(n), pre_piece(n)).then_inc(w_landed[n], 16)
            sp.dma_start(wpool[:, :, :], w_pool.rearrange("l g c d -> c (l g) d")).then_inc(pool_in, 16)
            sp.dma_start(pages[0:1, :], page_table.rearrange("b n -> (b n)")[None, :]).then_inc(page_in, 16)
            piece_used = ([(ada_ps, n + 1) for n in range(4)]
                          + [(projs_ps, 1), (projs_ps, 2), (proj_ps, 13), (projs_ps, 3)]
                          + [(ada_ps, n + 1) for n in range(4, 12)])
            for n in range(4, N_PRE):
                sp.wait_ge(*piece_used[n - 4])
                sp.dma_start(wslot(n % 4), pre_piece(n)).then_inc(w_landed[n % 4], 16)
                if n == 7:
                    sp.wait_ge(bias_ev, 1)
                    sp.dma_start(scratch, bias_rows).then_inc(bias_out, 16)
                    sp.wait_ge(bias_out, 16)
                    sp.dma_start(flipped.rearrange("p a (b n) -> p (a b) n", b=2),
                                 bass.AP(scratch.tensor, 0, [[1, P], [REV, NH], [1, 2 * P]])).then_inc(bias_back, 16)
            sp.wait_ge(page_in, 16)
            sp.wait_ge(at_out_ev, HP)
            sp.wait_ge(pool_ev, NG)
            sp.wait_ge(outs, 16 * 3)

            def load_block(cache, b, j, seq):
                slot = j % SLOTS
                for pg in range(PPB):
                    at = b * PAGES + PPB * j + pg
                    phys = sp.value_load(pages[0:1, bass.ds(at, 1)], min_val=0, max_val=N_PHYS - 1)
                    if pg == 0 and not (isinstance(seq, int) and seq < SLOTS):
                        sp.wait_ge(kv_used, seq - SLOTS + 1)
                    sp.dma_start(ring[:, slot, pg, :], cache[bass.ds(phys, 1), :, :].rearrange("a p n -> (a p) n"))\
                      .then_inc(kv_landed[slot], 16)

            def load_up(b):
                sp.dma_start(wslot(UP_SLOT), wup_d[:, :, bass.ds(b * PIECE, PIECE)]).then_inc(w_landed[UP_SLOT], 16)

            def load_down(b):
                sp.dma_start(wslot(DOWN_SLOT, D), wdown_d[bass.ds(b, 1), :, :, :]
                             .rearrange("a p k n -> (a p) k n")).then_inc(w_landed[DOWN_SLOT], 16)

            for j in range(BLOCKS):
                load_block(ck, 0, j, j)
            with sp.Fori(0, LAST) as b:
                for j in range(BLOCKS):
                    load_block(ck, b + 1, j, k_seq(b + 1, j))
                    if j == 1:
                        load_up(b)
                    if j == 9:
                        load_down(b)
                for j in range(BLOCKS):
                    load_block(cv, b, j, v_seq(b, j, True))
            for j in range(BLOCKS):
                load_block(cv, LAST, j, v_seq(LAST, j, False))
                if j == 1:
                    load_up(LAST)
                if j == SLOTS:
                    load_down(LAST)
            sp.dma_start(nfb, bass.AP(norm_final.tensor, 0, [[0, P], [1, D]])).then_inc(nf_in, 16)
            for i in range(2 * (N_CH - 1)):
                if i < 2:
                    sp.wait_ge(so_ps, 1)
                else:
                    sp.wait_ge((sup_ps, sdn_ps)[i % 2], (i - 4) // 2 + 2)
                if i % 2 == 0:
                    sp.dma_start(wslot(i % 4), wup_d[:, :, i // 2 * PIECE:(i // 2 + 1) * PIECE])\
                      .then_inc(w_landed[i % 4], 16)
                else:
                    sp.dma_start(wslot(i % 4, D), wdown_d[i // 2, :, :, :]).then_inc(w_landed[i % 4], 16)
            for t in range(TT):
                sp.wait_ge(fin_y, t + 1)
                sp.dma_start(ypd[t, :, :], ybuf[t]).then_inc(y_out, 16)
            sp.wait_ge(fin_y, TT + 1)
            sp.dma_start(ysd, ybuf[TT][0:NS, :]).then_inc(y_out, 16)
            sp.wait_ge(bias_out, 16)
            sp.wait_ge(row_out, 16 * ROWS)
            sp.wait_ge(outs, 16 * 3)
            sp.wait_ge(y_out, 16 * (TT + 1))

        @block.gpsimd
        def _(pool):
            pool.memset(QBD[:, :, :, :], 0.0).then_inc(qbd_zero, 1)
            pool.dma_start(pool_sample[0, :, 0:STATE - DT, :], state_pool[0, :, DT:STATE, :]).then_inc(outs, 16)
            step = [0]

            def chain(ins):
                step[0] += 1
                ins.then_inc(win_step, 1)
                pool.wait_ge(win_step, step[0])

            pool.wait_ge(proj_ev, 12)
            pool.dma_start(vpd, v_tok).then_inc(outs, 16)
            pool.wait_ge(proj_ev, 17)
            pool.dma_start(vsd, vS[:, :]).then_inc(outs, 16)
            pool.wait_ge(pads, 1)
            pool.wait_ge(bias_out, 16)
            for g, w in enumerate(WINDOWS):
                src, sh, n = uT[:, g, :], 1, 0
                while sh < w:
                    lo = 2 * sh - 1
                    chain(pool.tensor_tensor(win[n % 2][:, lo:UP], src[:, lo:UP], src[:, lo - sh:UP - sh], ALU.add))
                    src, sh, n = win[n % 2], 2 * sh, n + 1
                other = win[n % 2]
                chain(pool.tensor_scalar(other[:, 32:UP], src[:, 32:UP], 1.0 / w, None, ALU.mult))
                chain(pool.tensor_tensor(other[:, 16:32], src[:, 16:32], inv_count[:, g, :], ALU.mult))
                chain(pool.tensor_tensor(dT[:, g, :], other[:, 16:UP], uT[:, g, 16:UP], ALU.subtract))
            pool.wait_ge(projs_ev, 3)
            L = STATE + DT
            for g, w in enumerate(WINDOWS):
                src, sh, n = uS[:, g, :, :], 1, 0
                while sh < w:
                    lo = 2 * sh - 1
                    chain(pool.tensor_tensor(winS[:, n % 2, :, lo:L], src[:, :, lo:L], src[:, :, lo - sh:L - sh],
                                             ALU.add))
                    src, sh, n = winS[:, n % 2, :, :], 2 * sh, n + 1
                other = winS[:, n % 2, :, :]
                chain(pool.tensor_scalar(other[:, :, STATE:L], src[:, :, STATE:L], 1.0 / w, None, ALU.mult))
                chain(pool.tensor_tensor(dS[:, g, :].rearrange("p (b t) -> p b t", b=DB), other[:, :, STATE:L],
                                         uS[:, g, :, STATE:L], ALU.subtract))
            pool.sem_inc(win_done, 1)
            for t in range(TT):
                pool.wait_ge(row_ev, t + 1)
                pool.dma_start(kpd[t, :, :], rows_k[:, t, :]).then_inc(row_out, 16)
            pool.wait_ge(row_ev, ROWS)
            pool.dma_start(ksd, rows_s[:, 0, :]).then_inc(row_out, 16)
            pool.dma_start(pool_sample[0, :, STATE - DT:STATE, :], rows_s[:, 1, :]).then_inc(row_out, 16)
            pool.dma_start(pool_prompt[0, 0, :, :], rows_s[0:STATE, 2, :]).then_inc(row_out, 16)

            def take_queries(b, first=False):
                if first:
                    pool.wait_ge(projs_ev, 1)
                else:
                    pool.wait_ge(fin_pe, FS * (b - 1) + 1)
                    pool.wait_ge(qk, BLOCKS * b)
                pool.tensor_copy(qcur[:, :, :], QBD[:, bass.ds(b, 1), :, :].rearrange("p a h c -> p (a h) c"))\
                    .then_inc(q_cur, 1)

            def squares(b):
                for m in range(HP):
                    pool.wait_ge(relu_ev, HP * b + m + 1)
                    pool.tensor_tensor(gT[:, m, :], gT[:, m, :], gT[:, m, :], ALU.mult).then_inc(sqr_ev, 1)

            take_queries(0, first=True)
            with pool.Fori(0, LAST) as b:
                take_queries(b + 1)
                squares(b)
            squares(LAST)

        @block.scalar
        def _(act):
            act.wait_ge(c_in, 32)
            act.activation(c_sig, c_tok, ACT.Exp, scale=-1.0).then_inc(c_exp, 1)
            for f in range(0, FT, 2):
                act.wait_ge(xt_ps, f + 1)
                act.activation(xT[:, f, :], bank(f % 4), ACT.Copy).then_inc(xt_ev_act, 1)
            act.wait_ge(xt_ev_act, FT // 2)
            act.wait_ge(xt_ev_dve, FT // 2 + 1)
            for f in range(FT):
                act.activation(hT[:, f, :], xT[:, f, :], ACT.Square).then_inc(sq_done, 1)
            act.activation(hTs[:, :, :], xTs[:, :, :], ACT.Square).then_inc(sq_done, 1)
            act.wait_ge(ms_ps, 1)
            act.wait_ge(dve_init, 2)
            act.activation(rstd[:, :], bank(7), ACT.Sqrt, bias=eps[:, 0:1], scale=1.0 / D).then_inc(root_done, 1)
            act.activation(rstds[:, :], bank(5, P, NS), ACT.Sqrt, bias=eps[:, 0:1], scale=1.0 / D)\
               .then_inc(root_done, 1)
            for g in range(17):
                act.wait_ge(proj_ps, g + 1)
                src = bank(2 + g % 2)
                if g < 4:
                    act.activation(qT[:, g, :], src, ACT.Copy, scale=SCALE).then_inc(proj_ev, 1)
                elif g < 8:
                    act.activation(kT[:, g - 4, :], src, ACT.Copy).then_inc(proj_ev, 1)
                elif g < 12:
                    act.activation(v_tok[:, g - 8, :], src, ACT.Copy).then_inc(proj_ev, 1)
                elif g == 12:
                    act.activation(vS[:, :], bank(2 + g % 2, NS), ACT.Copy).then_inc(proj_ev, 1)
                else:
                    if g == 13:
                        act.wait_ge(pads, 1)
                    act.activation(uT[:, g - 13, 16:UP], src, ACT.Copy).then_inc(proj_ev, 1)

            def attention_out(hp):
                act.activation(mixT[:, hp, :], bank(4 + hp % 2), ACT.Copy).then_inc(at_out_ev, 1)

            for a in range(NH * TT):
                n = (a % TT + 1) * P
                act.wait_ge(at_max, a + 1)
                act.activation(logits[:, a % 2, 0:n], logits[:, a % 2, 0:n], ACT.Exp, bias=stat[:, a % 2:a % 2 + 1],
                               accum_out=stat[:, 2 + a % 2:3 + a % 2]).then_inc(at_exp, 1)
                act.wait_ge(at_pT, a + 1)
                if a >= 2:
                    act.wait_ge(at_out, a - 1)
                act.activation(pT[:, a % 2, 0:n], bank(a % 2, P, n), ACT.Copy).then_inc(at_pT_ev, 1)
                if a > 2 * TT and a % (2 * TT) == 1:
                    act.wait_ge(at_out, a - 1)
                    attention_out(a // (2 * TT) - 1)
            act.wait_ge(at_out, NH * TT)
            attention_out(HP - 1)
            for g in range(NG):
                act.wait_ge(pool_ps, g + 1)
                act.activation(mixT[:, HP + g, :], bank(6 + g % 2), ACT.Copy,
                               scale=vecs[:, VEC_POOL + g:VEC_POOL + g + 1]).then_inc(pool_ev, 1)
            act.wait_ge(row_out, 16 * ROWS)
            for f in range(FT):
                act.wait_ge(out_ev, f + 1)
                act.activation(hT[:, f, :], xT[:, f, :], ACT.Square).then_inc(sq2_done, 1)
            act.wait_ge(ms2_ps, 1)
            act.activation(rstd[:, :], bank(7), ACT.Sqrt, bias=eps[:, 0:1], scale=1.0 / D).then_inc(root2_done, 1)

            def keys_out(b, j, first=False):
                i = BLOCKS * b + j
                for pg in range(PPB):
                    if pg == 0:
                        act.wait_ge(kt_ps, i + 1)
                    else:
                        act.wait_ge(kv_used, (j if first else k_seq(b, j)) + 1)
                    if pg == 0 and not (first and j < 2):
                        act.wait_ge(qk, i - 1)
                        act.wait_ge(km, i - 1)
                    act.activation(ktb[:, j % 2, :, pg * P:(pg + 1) * P],
                                   bank(pg).rearrange("p (h n) -> p h n", h=HP), ACT.Copy).then_inc(kt_ev, 1)

            def exps(b):
                act.wait_ge(fin_dve, FS * b + 4)
                act.activation(probs, probs, ACT.Exp).then_inc(fin_exp, 1)

            def relu(b, m):
                act.wait_ge(up_ps, HP * b + m + 1)
                act.activation(gT[:, m, :], bank(5 + m % 2), ACT.Relu).then_inc(relu_ev, 1)

            for j in range(BLOCKS):
                keys_out(0, j, first=True)
            with act.Fori(0, LAST) as b:
                for j in range(BLOCKS):
                    keys_out(b + 1, j)
                    if j == 8:
                        exps(b)
                    if j % 4 == 3:
                        relu(b, j // 4)
            for m in range(HP - 1):
                relu(LAST, m)
            exps(LAST)
            relu(LAST, HP - 1)

            act.wait_ge(so_ev, 1)
            act.activation(hTs[:, :, :], xTs[:, :, :], ACT.Square).then_inc(ssq, 1)
            act.wait_ge(sms_ps, 1)
            act.activation(rstds[:, :], bank(1, P, NS), ACT.Sqrt, bias=eps[:, 0:1], scale=1.0 / D).then_inc(sroot, 1)

            def final_norm(t):
                n = P if t < TT else NS
                act.wait_ge(fin_ps, t + 1)
                act.activation(junk[0:n, :], PS[0:n, 4 + 2 * (t % 2):6 + 2 * (t % 2), :].rearrange("p a b -> p (a b)"),
                               ACT.Square, accum_out=fstat[0:n, t, 0:1]).then_inc(fin_ss, 1)
                act.wait_ge(fin_ss, t + 1)
                act.activation(fstat[0:n, t, 1:2], fstat[0:n, t, 0:1], ACT.Sqrt, bias=eps[0:n, 0:1], scale=1.0 / D)\
                   .then_inc(fin_root, 1)

            for i in range(N_CH):
                act.wait_ge(sup_ps, i + 1)
                if i >= 2:
                    act.wait_ge(sdn_ps, i - 1)
                act.activation(gS[:, i % 2, :, :].rearrange("p a b -> p (a b)"), bank(1 + i % 2, P, HP * NS), ACT.Relu)\
                   .then_inc(srelu, 1)
                if 1 <= i <= TT:
                    final_norm(i - 1)
            final_norm(TT)

        @block.vector
        def _(dve):
            steps = [0]

            def link(ins):
                steps[0] += 1
                ins.then_inc(dve_chain, 1)
                dve.wait_ge(dve_chain, steps[0])

            dve.memset(ones[:, :], 1.0).then_inc(dve_init, 1)
            dve.memset(eps[:, :], EPS).then_inc(dve_init, 1)
            dve.wait_ge(c_exp, 1)
            link(dve.tensor_scalar(c_sig, c_sig, 1.0, None, ALU.add))
            link(dve.reciprocal(c_sig, c_sig))
            dve.tensor_tensor(c_sig, c_sig, c_tok, ALU.mult).then_inc(c_ready, 1)
            for f in range(1, FT, 2):
                dve.wait_ge(xt_ps, f + 1)
                dve.tensor_copy(xT[:, f, :], bank(f % 4)).then_inc(xt_ev_dve, 1)
            dve.wait_ge(xt_ps, FT + 1)
            dve.tensor_copy(xTs[:, :, :].rearrange("p a b -> p (a b)"), bank(4, P, FT * NS)).then_inc(xt_ev_dve, 1)
            dve.memset(uT[:, :, 0:16], 0.0).then_inc(pads, 1)
            dve.wait_ge(small_ps, 1)
            dve.tensor_copy(cT[:, :, :].rearrange("p a b -> p (a b)"), bank(5, P, FT * (1 + DB))).then_inc(small_ev, 1)
            dve.tensor_copy(vecs[:, :], bank(5, P, VECS, 128)).then_inc(small_ev, 1)
            dve.tensor_copy(uS[:, :, :, 0:STATE], bank(6, P, NG * DB * STATE)
                            .rearrange("p (g b s) -> p g b s", g=NG, b=DB)).then_inc(small_ev, 1)
            dve.wait_ge(bias_ps, 1)
            dve.tensor_tensor(bias_rows, bank(6, NH, REV), mask_rows, ALU.add).then_inc(bias_ev, 1)
            dve.wait_ge(bias_ps, 2)
            dve.tensor_copy(farb[:, :], bank(4, P, NH)).then_inc(bias_ev, 1)
            dve.tensor_copy(farbt[:, :].rearrange("p (h t) -> p h t", t=DT),
                            bank(4, P, NH)[:, :, None].to_broadcast([P, NH, DT])).then_inc(bias_ev, 1)
            dve.tensor_copy(lastb[:, :].rearrange("p (h t) -> p h t", t=DT),
                            bank(4, P, HT, NH).rearrange("p (t h) -> p h t", t=DT)).then_inc(bias_ev, 1)
            dve.tensor_copy(ownb[:, :].rearrange("p (h t) -> p h t", t=DT),
                            bank(4, NS, HT, 64).rearrange("p (t h) -> p h t", t=DT)).then_inc(bias_ev, 1)
            dve.tensor_copy(lt[:, :], const32[:, C32["lt"][0]:C32["lt"][1]]).then_inc(bias_ev, 1)
            dve.tensor_copy(ownmask[:, :], const32[:, C32["ownmask"][0]:C32["ownmask"][1]]).then_inc(bias_ev, 1)

            def modulation(p):
                dve.wait_ge(ada_ps, p + 1)
                dve.tensor_tensor(mods[:, 4 * p:4 * p + 4, :],
                                  bank(p % 2 if p < 4 else 7, P, 4 * (1 + DB)).rearrange("p (m c) -> p m c", m=4),
                                  vecs[:, 4 * p:4 * p + 4][:, :, None].to_broadcast([P, 4, 1 + DB]), ALU.add)\
                   .then_inc(ada_ev, 1)

            def weighted(which, scale, vec):
                link(dve.tensor_scalar(mod_a[:, which, :, :], mods[:, scale:scale + FT, :], 1.0, None, ALU.add))
                link(dve.tensor_tensor(mod_a[:, which, :, :], mod_a[:, which, :, :],
                                       vecs[:, vec:vec + FT][:, :, None].to_broadcast([P, FT, 1 + DB]), ALU.mult))

            def per_token(table):
                return table[:, :, 1:1 + DB][:, :, :, None].to_broadcast([P, FT, DB, DT])

            def split(tile):
                return tile[:, :, :].rearrange("p f (b t) -> p f b t", b=DB)

            def modulate_sample(which, shift):
                link(dve.tensor_tensor(hTs[:, :, :], xTs[:, :, :], rstds[:, None, :].to_broadcast([P, FT, NS]), ALU.mult))
                link(dve.tensor_tensor(split(hTs), split(hTs), per_token(mod_a[:, which, :, :]), ALU.mult))
                return dve.tensor_tensor(split(hTs), split(hTs), per_token(mods[:, shift:shift + FT, :]), ALU.add)

            def modulate_prompt(which, shift, ready):
                for f in range(FT):
                    link(dve.tensor_tensor(hT[:, f, :], xT[:, f, :], rstd[:, :], ALU.mult))
                    dve.tensor_scalar(hT[:, f, :], hT[:, f, :], mod_a[:, which, f, 0:1], mods[:, shift + f, 0:1],
                                      ALU.mult, ALU.add).then_inc(ready, 1)

            dve.wait_ge(root_done, 2)
            link(dve.reciprocal(rstd[:, :], rstd[:, :]))
            link(dve.reciprocal(rstds[:, :], rstds[:, :]))
            for p in range(4):
                modulation(p)
            dve.wait_ge(ada_ev, 4)
            weighted(0, SC1, VEC_MIX)
            dve.wait_ge(xt_ev_act, FT // 2)
            modulate_sample(0, SH1).then_inc(h_ready, 1)
            modulate_prompt(0, SH1, h_ready)

            dve.wait_ge(projs_ps, 1)
            dve.wait_ge(qbd_zero, 1)
            for hp in range(HP):
                for half in range(2):
                    r, c = slice(HD * half, HD * half + HD), 2 * DT * hp + DT * half
                    last = dve.tensor_scalar(QBD[r, :, hp, c:c + DT],
                                             PS[r, 4, hp * NS:(hp + 1) * NS].rearrange("p (b t) -> p b t", b=DB),
                                             SCALE, None, ALU.mult)
                    if (hp, half) != (HP - 1, 1):
                        link(last)
            last.then_inc(projs_ev, 1)
            dve.wait_ge(projs_ps, 2)
            dve.tensor_copy(kTs[:, :, :].rearrange("p a b -> p (a b)"), bank(5, P, HP * NS)).then_inc(projs_ev, 1)
            dve.wait_ge(projs_ps, 3)
            link(dve.tensor_copy(uS[:, :, :, STATE:STATE + DT],
                                 bank(6, P, NG * NS).rearrange("p (g b t) -> p g b t", g=NG, b=DB)))
            dve.tensor_copy(uSn[:, :, :].rearrange("p a b -> p (a b)"), bank(6, P, NG * NS)).then_inc(projs_ev, 1)
            dve.wait_ge(own_ps, 1)
            dve.wait_ge(bias_ev, 7)
            link(dve.tensor_tensor(own[:, :, :], bank(7, NS, DB * HT).rearrange("p (b c) -> p b c", b=DB),
                                   ownb[:, None, :].to_broadcast([NS, DB, HT]), ALU.add))
            own4 = own[:, :, :].rearrange("p b (h t) -> p b h t", t=DT)
            dve.tensor_tensor(own4, own4, ownmask[:, :].rearrange("p (b t) -> p b t", b=DB)[:, :, None, :]
                              .to_broadcast([NS, DB, NH, DT]), ALU.add).then_inc(own_ev, 1)

            def logits_in(a):
                h, i = a // TT, a % TT
                n, near = (i + 1) * P, P if i == 0 else 2 * P
                dve.wait_ge(at_scores, a + 1)
                if a >= 2:
                    dve.wait_ge(at_pT, a - 1)
                src = bank(2 + a % 2)
                if n > near:
                    dve.tensor_scalar(logits[:, a % 2, 0:n - near], src[:, 0:n - near], farb[:, h:h + 1], None,
                                      ALU.add).then_inc(dve_chain, 1)
                    steps[0] += 1
                link(dve.tensor_tensor(logits[:, a % 2, n - near:n], src[:, n - near:n], nearb[:, h, 2 * P - near:2 * P],
                                       ALU.add))
                dve.tensor_reduce(stat[:, a % 2:a % 2 + 1], logits[:, a % 2, 0:n], AX.X, ALU.max, negate=True)\
                   .then_inc(at_max, 1)

            def normalize(a):
                n = (a % TT + 1) * P
                dve.wait_ge(at_exp, a + 1)
                link(dve.reciprocal(stat[:, 2 + a % 2:3 + a % 2], stat[:, 2 + a % 2:3 + a % 2]))
                dve.tensor_scalar(logits[:, a % 2, 0:n], logits[:, a % 2, 0:n], stat[:, 2 + a % 2:3 + a % 2], None,
                                  ALU.mult).then_inc(at_norm, 1)

            def rows(r):
                dve.wait_ge(row_ps, r + 1)
                if r < TT:
                    dve.tensor_copy(rows_k[:, r, :], bank(6)).then_inc(row_ev, 1)
                else:
                    n = NS if r < TT + 2 else STATE
                    dve.tensor_copy(rows_s[0:n, r - TT, :], bank(6, n)).then_inc(row_ev, 1)

            for i in range(4):
                dve.wait_ge(near_ps, i + 1)
                dve.tensor_copy(scn[:, 512 * i:512 * i + 512], bank(4 + i % 2)).then_inc(near_ev, 1)
            dve.wait_ge(near_ev, 4)
            logits_in(0)
            for a in range(NH * TT):
                if a + 1 < NH * TT:
                    logits_in(a + 1)
                normalize(a)
                if a % TT == TT - 1:
                    h = a // TT
                    if h < ROWS:
                        rows(h)
                    modulation(4 + h)
            dve.wait_ge(pools_ps, 1)
            dve.tensor_tensor(mixS[:, HP:FT, :], bank(5, P, NG * NS).rearrange("p (g n) -> p g n", g=NG),
                              vecs[:, VEC_POOL:VEC_POOL + NG][:, :, None].to_broadcast([P, NG, NS]), ALU.mult)\
               .then_inc(pools_ev, 1)
            dve.wait_ge(ada_ev, 12)
            weighted(1, SC2, VEC_MLP)
            for m in range(FT):
                dve.wait_ge(out_ps, m + 1)
                dve.scalar_tensor_tensor(xT[:, m, :], bank(2 + m % 2), mods[:, G1 + m, 0:1], xT[:, m, :],
                                         ALU.mult, ALU.add).then_inc(out_ev, 1)
            dve.wait_ge(root2_done, 1)
            link(dve.reciprocal(rstd[:, :], rstd[:, :]))
            modulate_prompt(1, SH2, h2_ready)
            dve.wait_ge(win_done, 1)
            dve.wait_ge(row_ev, ROWS)
            link(dve.memset(masked[:, PAGES, :], NEG))

            def block_sum(b, j):
                dve.wait_ge(kt_ev, PPB * (BLOCKS * b + j + 1))
                dve.tensor_reduce(kmean[:, :, j], ktb[:, j % 2, :, :], AX.X, ALU.add).then_inc(km, 1)

            def scores_out(b, j):
                dve.wait_ge(qk, BLOCKS * b + j + 1)
                g = j // 4
                src = bank(2 + g % 2, P, 8 * HT).rearrange("p (n c) -> p n c", c=HT)
                far = 8 if g < 3 else 7
                ins = dve.tensor_tensor(sc[:, 8 * g:8 * g + far, :], src[:, 0:far, :],
                                        farbt[:, None, :].to_broadcast([P, far, HT]), ALU.add)
                if g == 3:
                    ins = dve.tensor_tensor(sc[:, PAGES - 1, :], src[:, 7, :], lastb[:, :], ALU.add)
                ins.then_inc(sc_ev, 1)

            def fchain(ins, b, k):
                ins.then_inc(fin_chain, 1)
                dve.wait_ge(fin_chain, FC * b + k)

            def rank_blocks(b):
                dve.wait_ge(fin_pe, FS * b + 1)
                fchain(dve.tensor_copy(gate[:, :], bank(7, HT, BLOCKS)), b, 1)
                over_n = gate[:, None, :].to_broadcast([HT, BLOCKS, BLOCKS])
                over_m = gate[:, :, None].to_broadcast([HT, BLOCKS, BLOCKS])
                fchain(dve.tensor_tensor(cmpb, over_n, over_m, ALU.is_equal), b, 2)
                fchain(dve.tensor_tensor(cmpb, cmpb, lt[:, :].rearrange("p (n m) -> p n m", n=BLOCKS),
                                         ALU.mult), b, 3)
                fchain(dve.tensor_tensor(cmpa, over_n, over_m, ALU.is_gt), b, 4)
                fchain(dve.tensor_tensor(cmpa, cmpa, cmpb, ALU.add), b, 5)
                fchain(dve.tensor_reduce(rank[:, :], cmpa, AX.X, ALU.add), b, 6)
                fchain(dve.tensor_scalar(rank[:, :], rank[:, :], float(TOPK), NEG, ALU.is_ge, ALU.mult), b, 7)
                dve.tensor_tensor(diag, rank[:, :, None].to_broadcast([HT, BLOCKS, HT]),
                                  ident[0:HT, None, 0:HT].to_broadcast([HT, BLOCKS, HT]), ALU.mult).then_inc(fin_dve, 1)

            def mask_scores(b):
                dve.wait_ge(fin_pe, FS * b + 2)
                dve.tensor_copy(masked[0:NS, PAGES, :], own[:, bass.ds(b, 1), :].rearrange("p a c -> p (a c)"))
                fchain(dve.tensor_tensor(masked[:, 0:PAGES, :].rearrange("p (n g) c -> p n g c", g=PPB),
                                         sc[:, :, :].rearrange("p (n g) c -> p n g c", g=PPB),
                                         bank(7).rearrange("p (n c) -> p n c", c=HT)[:, :, None, :]
                                         .to_broadcast([P, BLOCKS, PPB, HT]), ALU.add), b, 8)
                dve.tensor_reduce(colmax[:, :], masked.rearrange("p g c -> p c g"), AX.X, ALU.max).then_inc(fin_dve, 1)

            def column_max(b):
                dve.wait_ge(fin_pe, FS * b + 3)
                fchain(dve.tensor_reduce(rowmax[:, :], bank(7, HT, P), AX.X, ALU.max), b, 9)
                dve.tensor_scalar(dmax[:, :], ident[0:HT, 0:HT], rowmax[:, 0:1], None, ALU.mult).then_inc(fin_dve, 1)

            def less_max(b):
                dve.wait_ge(fin_pe, FS * b + 4)
                dve.tensor_tensor(probs, masked, bank(7, P, HT)[:, None, :].to_broadcast([P, PAGES + 1, HT]),
                                  ALU.subtract).then_inc(fin_dve, 1)

            def column_sum(b):
                dve.wait_ge(fin_exp, b + 1)
                dve.tensor_reduce(colsum[:, :], probs.rearrange("p g c -> p c g"), AX.X, ALU.add).then_inc(fin_dve, 1)

            def take_reciprocal(b):
                dve.wait_ge(fin_pe, FS * b + 5)
                dve.reciprocal(rden[:, :], bank(7, P, HT)).then_inc(at_s, 1)

            def down_out(b, m):
                dve.wait_ge(dn_ps, FT * b + m + 1)
                dve.scalar_tensor_tensor(xT[:, m, :], bank(5 + m % 2), mods[:, G2 + m, 0:1], xT[:, m, :],
                                         ALU.mult, ALU.add).then_inc(dn_ev, 1)

            def attention_sample(b):
                dve.wait_ge(pv, b + 1)
                dve.wait_ge(at_s, 3 * b + 1)
                for half in range(2):
                    r = slice(HD * half, HD * half + HD)
                    acc = PS[r, 4, 0:HT].rearrange("p (h c) -> p h c", h=HP)[:, :, DT * half:DT * half + DT]
                    den = rden[r, :].rearrange("p (h c) -> p h c", h=HP)[:, :, DT * half:DT * half + DT]
                    dve.tensor_tensor(mixS[r, 0:HP, bass.ds(DT * b, DT)], acc, den, ALU.mult).then_inc(at_s, 1)

            for j in range(BLOCKS):
                block_sum(0, j)
                if j % 4 == 3:
                    scores_out(0, j)
            with dve.Fori(0, LAST) as b:
                rank_blocks(b)
                for j in range(BLOCKS):
                    block_sum(b + 1, j)
                    if j == 1:
                        mask_scores(b)
                    if j == 3:
                        column_max(b)
                    if j == 5:
                        less_max(b)
                    if j == 9:
                        column_sum(b)
                    if j == 11:
                        take_reciprocal(b)
                    if j % 4 == 3:
                        scores_out(b + 1, j)
                for m in range(FT):
                    down_out(b, m)
                attention_sample(b)
            rank_blocks(LAST)
            mask_scores(LAST)
            column_max(LAST)
            less_max(LAST)
            column_sum(LAST)
            take_reciprocal(LAST)
            for m in range(FT):
                down_out(LAST, m)
            attention_sample(LAST)

            dve.wait_ge(so_ps, 1)
            link(dve.tensor_tensor(split(tmpS), bank(0, P, FT * NS).rearrange("p (f b t) -> p f b t", f=FT, b=DB),
                                   per_token(mods[:, G1:G1 + FT, :]), ALU.mult))
            dve.tensor_tensor(xTs[:, :, :], xTs[:, :, :], tmpS[:, :, :], ALU.add).then_inc(so_ev, 1)
            dve.wait_ge(so_ev, 1)
            dve.wait_ge(sroot, 1)
            link(dve.reciprocal(rstds[:, :], rstds[:, :]))
            modulate_sample(1, SH2).then_inc(h2s_ready, 1)

            def final_out(t):
                n = P if t < TT else NS
                dve.wait_ge(fin_root, t + 1)
                if t == 0:
                    dve.wait_ge(nf_in, 16)
                link(dve.reciprocal(fstat[0:n, t, 1:2], fstat[0:n, t, 1:2]))
                src = PS[0:n, 4 + 2 * (t % 2):6 + 2 * (t % 2), :].rearrange("p a b -> p (a b)")
                dve.scalar_tensor_tensor(ybuf[t][0:n, :], src, fstat[0:n, t, 1:2], nfb[0:n, :],
                                         ALU.mult, ALU.mult).then_inc(fin_y, 1)

            for i in range(N_CH):
                dve.wait_ge(srelu, i + 1)
                dve.tensor_tensor(gS[:, i % 2, :, :], gS[:, i % 2, :, :], gS[:, i % 2, :, :], ALU.mult)\
                   .then_inc(ssqr, 1)
                if 1 <= i <= TT:
                    final_out(i - 1)
            dve.wait_ge(sdn_ps, N_CH)
            link(dve.tensor_tensor(split(tmpS), bank(3, P, FT * NS).rearrange("p (f b t) -> p f b t", f=FT, b=DB),
                                   per_token(mods[:, G2:G2 + FT, :]), ALU.mult))
            dve.tensor_tensor(xTs[:, :, :], xTs[:, :, :], tmpS[:, :, :], ALU.add).then_inc(xs_done, 1)
            final_out(TT)

        @block.tensor
        def _(pe):
            def mm(out, lhsT, rhs, start=True, stop=True, **kw):
                return pe.matmul(out, lhsT, rhs, start=start, stop=stop, **kw)

            pe.wait_ge(cst_in, 16)
            pe.wait_ge(x_in, 32)
            for f in range(FT):
                if f >= 4:
                    pe.wait_ge((xt_ev_act, xt_ev_dve)[f % 2], (f - 4) // 2 + 1)
                for t in range(TT):
                    last = pe.transpose(bank(f % 4, P, P, t * P), x_tok[:, t, f * P:(f + 1) * P], ident)
                last.then_inc(xt_ps, 1)
            for f in range(FT):
                last = pe.transpose(bank(4, P, NS, f * NS), xs_tok[:, f * P:(f + 1) * P], ident[0:NS, 0:NS])
            last.then_inc(xt_ps, 1)
            pe.wait_ge(c_ready, 1)
            for f in range(FT):
                pe.transpose(bank(5, P, 1 + DB, f * (1 + DB)), c_sig[:, f * P:(f + 1) * P], ident[0:1 + DB, 0:1 + DB])
            pe.wait_ge(vec_in, 64)
            pe.transpose(bank(5, P, VECS, 128), vec_rows, ident[0:VECS, 0:VECS])
            pe.wait_ge(st_in, 64)
            for g in range(NG):
                last = pe.transpose(bank(6, P, DB * STATE, g * DB * STATE), st_rows[:, g * P:(g + 1) * P],
                                    ident[0:DB * STATE, 0:DB * STATE])
            last.then_inc(small_ps, 1)
            pe.wait_ge(small_ev, 3)
            pe.wait_ge(xt_ev_dve, FT // 2 + 1)
            lo, hi = C32["rev"]
            mm(bank(6, NH, REV), relb, const32[:, lo:lo + REV]).then_inc(bias_ps, 1)
            lo, hi = C32["far"]
            mm(bank(4, P, NH), const32[:, lo:hi], relb)
            for t in range(DT):
                lo = C32["last"][0] + t * P
                mm(bank(4, P, NH, NH + NH * t), const32[:, lo:lo + P], relb)
            for t in range(DT):
                lo = C32["own"][0] + t * NS
                last = mm(bank(4, NS, NH, 64 + NH * t), const32[:, lo:lo + NS], relb)
            last.then_inc(bias_ps, 1)

            def mean_squares(dst, tile, done, first):
                for f in range(FT):
                    pe.wait_ge(done, first + f + 1)
                    last = mm(dst, ones[:, :], tile[:, f, :], f == 0, f == FT - 1)
                return last

            pe.wait_ge(dve_init, 2)
            mean_squares(bank(7), hT, sq_done, 0)
            pe.wait_ge(sq_done, FT + 1)
            for f in range(FT):
                last = mm(bank(5, P, NS), ones[:, :], hTs[:, f, :], f == 0, f == FT - 1)
            last.then_inc(ms_ps, 1)

            def w_ready(n):
                pe.wait_ge(w_landed[n % 4], 16 * (n // 4 + 1))

            def modulation(p, n):
                w_ready(n)
                if p == 4:
                    pe.wait_ge(own_ev, 1)
                elif p >= 2:
                    pe.wait_ge(ada_ev, p - 1 if p < 4 else p)
                for m in range(4):
                    for k in range(FT):
                        last = mm(bank(p % 2 if p < 4 else 7, P, 1 + DB, m * (1 + DB)),
                                  wslot(n % 4)[:, k, m * P:(m + 1) * P], cT[:, k, :], k == 0, k == FT - 1)
                last.then_inc(ada_ps, 1)

            pe.wait_ge(xt_ev_act, FT // 2)
            for p in range(4):
                modulation(p, p)

            def project(g, dst, weights, tile, done, ready):
                for k in range(FT):
                    if ready:
                        pe.wait_ge(h_ready, k + 2)
                    last = mm(dst, weights[:, k, :], tile[:, k, :], k == 0, k == FT - 1)
                if done is not None:
                    last.then_inc(done, 1)

            def proj_bank(g):
                if g >= 2:
                    pe.wait_ge(proj_ev, g - 1)
                return 2 + g % 2

            for n, first, dst in ((4, 0, 4), (5, 4, 5), (6, 8, None), (7, 13, 6)):
                w_ready(n)
                if n == 6:
                    for t in range(TT + 1):
                        tile = hT[:, :, t * P:(t + 1) * P] if t < TT else hTs
                        out = bank(proj_bank(8 + t), P if t < TT else NS)
                        for k in range(FT):
                            last = mm(out, tile[:, k, :], wslot(n % 4)[:, k, :], k == 0, k == FT - 1)
                        last.then_inc(proj_ps, 1)
                    continue
                if n == 4:
                    pe.wait_ge(bias_ev, 7)
                if n == 5:
                    pe.wait_ge(root_done, 2)
                for m in range(4):
                    weights = wslot(n % 4)[:, :, m * P:(m + 1) * P]
                    out = bank(proj_bank(first + m))
                    project(first + m, out, weights, hT, proj_ps, n == 4 and m == 0)
                    pe.wait_ge(h_ready, 1)
                    project(first + m, bank(dst, P, NS, m * NS), weights, hTs, projs_ps if m == 3 else None, False)

            pe.wait_ge(projs_ev, 2)
            pe.wait_ge(root_done, 2)
            for hp in range(HP):
                last = mm(bank(7, NS, DB * HT).rearrange("p (b c) -> p b c", b=DB), kTs[:, hp, :], QBD[:, :, hp, :],
                          hp == 0, hp == HP - 1)
            last.then_inc(own_ps, 1)

            def scores(a):
                h, i = a // TT, a % TT
                r, hp = slice(HD * (h % 2), HD * (h % 2) + HD), h // 2
                if a >= 2:
                    pe.wait_ge(at_max, a - 1)
                mm(bank(2 + a % 2, P, (i + 1) * P), qT[r, hp, i * P:(i + 1) * P], kT[r, hp, 0:(i + 1) * P])\
                    .then_inc(at_scores, 1)

            def turn_probs(a):
                pe.wait_ge(at_norm, a + 1)
                if a >= 2:
                    pe.wait_ge(at_pT_ev, a - 1)
                for kt in range(a % TT + 1):
                    last = pe.transpose(bank(a % 2, P, P, kt * P), logits[:, a % 2, kt * P:(kt + 1) * P], ident)
                last.then_inc(at_pT, 1)

            def weigh(a):
                h, i = a // TT, a % TT
                r, hp = slice(HD * (h % 2), HD * (h % 2) + HD), h // 2
                pe.wait_ge(at_pT_ev, a + 1)
                if hp >= 2:
                    pe.wait_ge(at_out_ev, hp - 1)
                for kt in range(i + 1):
                    last = mm(PS[r, 4 + hp % 2, i * P:(i + 1) * P], v_tok[:, kt, HD * h:HD * h + HD],
                              pT[:, a % 2, kt * P:(kt + 1) * P], kt == 0, kt == i)
                last.then_inc(at_out, 1)

            def rows(r):
                pe.wait_ge(row_ev, r) if r else pe.wait_ge(projs_ev, 3)
                for c in range(HP):
                    if r < TT:
                        src, n = kT[:, c, r * P:(r + 1) * P], P
                    elif r == TT:
                        src, n = kTs[:, c, :], NS
                    elif r == TT + 1:
                        src, n = uSn[:, c, :], NS
                    else:
                        src, n = uT[:, c, UP - STATE:UP], STATE
                    last = pe.transpose(bank(6, n, P, c * P), src, ident)
                last.then_inc(row_ps, 1)

            pe.wait_ge(bias_back, 16)
            for i in range(4):
                if i >= 2:
                    pe.wait_ge(near_ev, i - 1)
                mm(bank(4 + i % 2), flip, flipped[:, i, :]).then_inc(near_ps, 1)
            pe.wait_ge(near_ev, 4)
            pe.wait_ge(proj_ev, 17)
            pe.wait_ge(ada_ev, 4)
            scores(0)
            for a in range(NH * TT):
                if a + 1 < NH * TT:
                    scores(a + 1)
                turn_probs(a)
                if a >= 1:
                    weigh(a - 1)
                if a % TT == TT - 1:
                    h = a // TT
                    if h < ROWS:
                        rows(h)
                    modulation(4 + h, 8 + h)
            weigh(NH * TT - 1)

            pe.wait_ge(pool_in, 16)
            pe.wait_ge(win_done, 1)
            pe.wait_ge(win_step, WIN_STEPS)
            pe.wait_ge(row_ev, ROWS)
            pe.wait_ge(ada_ev, 12)
            for g in range(NG):
                if g >= 2:
                    pe.wait_ge(pool_ev, g - 1)
                mm(bank(6 + g % 2), wpool[:, g, :], dT[:, g, :]).then_inc(pool_ps, 1)
            pe.wait_ge(at_out_ev, HP)
            for g in range(NG):
                last = mm(bank(5, P, NS, g * NS), wpool[:, g, :], dS[:, g, :])
            last.then_inc(pools_ps, 1)

            pe.wait_ge(pool_ev, NG)
            pe.wait_ge(at_max, NH * TT)
            for m in range(FT):
                if m % 4 == 0:
                    w_ready(16 + m // 4)
                if m >= 2:
                    pe.wait_ge(out_ev, m - 1)
                for k in range(FT):
                    last = mm(bank(2 + m % 2), wslot(m // 4)[:, k, m % 4 * P:(m % 4 + 1) * P], mixT[:, k, :],
                              k == 0, k == FT - 1)
                last.then_inc(out_ps, 1)
            mean_squares(bank(7), hT, sq2_done, 0).then_inc(ms2_ps, 1)

            def turn_keys(b, j, known):
                i = BLOCKS * b + j
                slot = j % SLOTS
                pe.wait_ge(kv_landed[slot], k_landed(b, j) if not known else 16 * PPB * (j // SLOTS + 1))
                for pg in range(PPB):
                    if not (known and j == 0):
                        pe.wait_ge(kt_ev, PPB * i + pg - 1)
                    for hp in range(HP):
                        last = pe.transpose(bank(pg, P, P, hp * P), ring[:, slot, pg, hp * P:(hp + 1) * P], ident)
                    last.then_inc(kt_ps if pg == 0 else kv_used, 1)

            def score_keys(b, j, known):
                i = BLOCKS * b + j
                pe.wait_ge(kt_ev, PPB * (i + 1))
                if j == 0:
                    pe.wait_ge(q_cur, b + 1)
                g = j // 4
                if j % 4 == 0 and not (known and g < 2):
                    pe.wait_ge(sc_ev, 4 * b + g - 1)
                for pg in range(PPB):
                    for hp in range(HP):
                        at = (j % 4 * PPB + pg) * HT + 2 * DT * hp
                        last = mm(bank(2 + g % 2, P, 2 * DT, at), ktb[:, j % 2, hp, pg * P:(pg + 1) * P],
                                  qcur[:, hp, 2 * DT * hp:2 * DT * (hp + 1)])
                last.then_inc(qk, 1)

            def gates(b):
                pe.wait_ge(km, BLOCKS * (b + 1))
                for hp in range(HP):
                    last = mm(bank(7, HT, BLOCKS), qcur[:, hp, :], kmean[:, hp, :], hp == 0, hp == HP - 1)
                last.then_inc(fin_pe, 1)

            def spread_mask(b):
                pe.wait_ge(fin_dve, FS * b + 1)
                mm(bank(7), ones[0:HT, :], diag.rearrange("p n c -> p (n c)")).then_inc(fin_pe, 1)

            def turn_max(b):
                pe.wait_ge(fin_dve, FS * b + 2)
                pe.transpose(bank(7, HT, P), colmax[:, :], ident).then_inc(fin_pe, 1)

            def spread_max(b):
                pe.wait_ge(fin_dve, FS * b + 3)
                mm(bank(7, P, HT), ones[0:HT, :], dmax[:, :]).then_inc(fin_pe, 1)

            def total(b):
                pe.wait_ge(fin_dve, FS * b + 5)
                mm(bank(7, P, HT), ones[:, :], colsum[:, :]).then_inc(fin_pe, 1)

            def up(b, m):
                if m == 0:
                    pe.wait_ge(w_landed[UP_SLOT], 16 * (PRE_USES + b + 1))
                if m >= 2:
                    pe.wait_ge(relu_ev, HP * b + m - 1)
                for k in range(FT):
                    last = mm(bank(5 + m % 2), wslot(UP_SLOT)[:, k, m * P:(m + 1) * P], hT[:, k, :], k == 0, k == FT - 1)
                last.then_inc(up_ps, 1)

            def down(b, m):
                if m == 0:
                    pe.wait_ge(w_landed[DOWN_SLOT], 16 * (PRE_USES + b + 1))
                    pe.wait_ge(sqr_ev, HP * (b + 1))
                if m >= 2:
                    pe.wait_ge(dn_ev, FT * b + m - 1)
                for k in range(HP):
                    last = mm(bank(5 + m % 2), wslot(DOWN_SLOT, D)[:, k, m * P:(m + 1) * P], gT[:, k, :],
                              k == 0, k == HP - 1)
                last.then_inc(dn_ps, 1)

            def weigh_values(b, more):
                pe.wait_ge(fin_exp, b + 1)
                for j in range(BLOCKS):
                    slot = j % SLOTS
                    pe.wait_ge(kv_landed[slot], v_landed(b, j, more))
                    for pg in range(PPB):
                        for hp in range(HP):
                            last = mm(bank(4, P, 2 * DT, 2 * DT * hp), ring[:, slot, pg, hp * P:(hp + 1) * P],
                                      probs[:, PPB * j + pg, 2 * DT * hp:2 * DT * (hp + 1)],
                                      j == 0 and pg == 0 and hp == 0, False, skip_group_check=True)
                    last.then_inc(kv_used, 1)
                    if j % 2 == 1:
                        down(b, j // 2)
                for hp in range(HP):
                    last = mm(bank(4, P, 2 * DT, 2 * DT * hp), vS[:, hp * P:(hp + 1) * P],
                              probs[0:NS, PAGES, 2 * DT * hp:2 * DT * (hp + 1)], False, True, skip_group_check=True)
                last.then_inc(pv, 1)

            pe.wait_ge(at_pT_ev, NH * TT)
            pe.wait_ge(out_ev, FT)
            for j in range(BLOCKS):
                turn_keys(0, j, True)
                if j >= 1:
                    score_keys(0, j - 1, True)
            score_keys(0, BLOCKS - 1, True)
            pe.wait_ge(h2_ready, FT)
            pe.wait_ge(root2_done, 1)
            pe.wait_ge(pools_ev, 1)
            with pe.Fori(0, LAST) as b:
                for j in range(BLOCKS):
                    turn_keys(b + 1, j, False)
                    if j == 0:
                        gates(b)
                    if j >= 1:
                        score_keys(b + 1, j - 1, False)
                    if j == 2:
                        spread_mask(b)
                    if j == 4:
                        turn_max(b)
                    if j == 6:
                        spread_max(b)
                    if j == 10:
                        total(b)
                    if j % 4 == 3:
                        up(b, j // 4)
                score_keys(b + 1, BLOCKS - 1, False)
                weigh_values(b, True)
            gates(LAST)
            spread_mask(LAST)
            up(LAST, 0)
            up(LAST, 1)
            turn_max(LAST)
            up(LAST, 2)
            spread_max(LAST)
            up(LAST, 3)
            total(LAST)
            weigh_values(LAST, False)

            pe.wait_ge(at_s, 3 * DB)
            for m in range(FT):
                for k in range(FT):
                    last = mm(bank(0, P, NS, m * NS), wslot(m // 4)[:, k, m % 4 * P:(m % 4 + 1) * P], mixS[:, k, :],
                              k == 0, k == FT - 1)
            last.then_inc(so_ps, 1)
            pe.wait_ge(ssq, 1)
            for f in range(FT):
                last = mm(bank(1, P, NS), ones[:, :], hTs[:, f, :], f == 0, f == FT - 1)
            last.then_inc(sms_ps, 1)

            def final_rows(t):
                pe.wait_ge(dn_ev, FT * N_CH) if t < TT else pe.wait_ge(xs_done, 1)
                if t >= 2:
                    pe.wait_ge(fin_y, t - 1)
                for f in range(FT):
                    if t < TT:
                        src, n = xT[:, f, t * P:(t + 1) * P], P
                    else:
                        src, n = xTs[:, f, :], NS
                    last = pe.transpose(bank(4 + 2 * (t % 2) + f // 4, n, P, f % 4 * P), src, ident)
                last.then_inc(fin_ps, 1)

            def tail_landed(i, half):
                if i == 0:
                    slot, uses = (UP_SLOT, DOWN_SLOT)[half], PRE_USES + N_CH
                else:
                    n = 2 * (i - 1) + half
                    slot = n % 4
                    uses = (5 if slot < 2 else PRE_USES + N_CH) + n // 4 + 1
                pe.wait_ge(w_landed[slot], 16 * uses)
                return slot

            pe.wait_ge(h2s_ready, 1)
            for i in range(N_CH):
                slot = tail_landed(i, 0)
                if i >= 2:
                    pe.wait_ge(srelu, i - 1)
                for m in range(HP):
                    for k in range(FT):
                        last = mm(bank(1 + i % 2, P, NS, m * NS), wslot(slot)[:, k, m * P:(m + 1) * P], hTs[:, k, :],
                                  k == 0, k == FT - 1)
                last.then_inc(sup_ps, 1)
                slot = tail_landed(i, 1)
                pe.wait_ge(ssqr, i + 1)
                for m in range(FT):
                    for k in range(HP):
                        last = mm(bank(3, P, NS, m * NS), wslot(slot, D)[:, k, m * P:(m + 1) * P], gS[:, i % 2, k, :],
                                  i == 0 and m == 0 and k == 0, i == N_CH - 1 and k == HP - 1, skip_group_check=True)
                last.then_inc(sdn_ps, 1)
                if 1 <= i <= TT:
                    final_rows(i - 1)
            final_rows(TT)


_INS = ["x_prompt", "x_sample", "cache_k", "cache_v", "state_pool", "page_table", "c_prompt", "c_sample", "w_ada",
        "b_ada", "norm_mix", "w_in", "rel_bias", "w_pool", "pool_scale", "w_out", "norm_mlp", "w_up", "w_down",
        "norm_final"]
_OUTS = [(1, S, D), (DB, DT, D), (1, 1, S, NH, HD), (1, 1, S, NH, HD), (1, 1, STATE, AW), (1, DB, DT, NH, HD),
         (1, DB, DT, NH, HD), (1, DB, STATE, AW)]


def kernel(**inputs):
    import numpy as _np
    import concourse.bacc as _bacc
    from concourse import mybir as _mybir
    from concourse.bass_utils import run_bass_kernel_spmd as _run

    nc = _bacc.Bacc("TRN2", target_bir_lowering=False, num_devices=1)
    arrays, args = {}, []
    host = [(name, _np.ascontiguousarray(inputs[name])) for name in _INS]
    host += list(zip(("shape_c128", "shape_c32", "shape_cmask"), shape_constants()))
    for name, a in host:
        arrays[f"in_{name}_dram"] = a
        args.append(nc.dram_tensor(f"in_{name}_dram", a.shape, _mybir.dt.from_np(a.dtype), kind="ExternalInput").ap())
    for i, shape in enumerate(_OUTS):
        args.append(nc.dram_tensor(f"out_{i}_dram", shape, F32, kind="ExternalOutput").ap())
    decoder_step(nc, *args)
    r = _run(nc, [arrays], core_ids=[0])
    return tuple(r.results[0][f"out_{i}_dram"] for i in range(len(_OUTS)))
```

```python
import math
from contextlib import ExitStack

import numpy as np

import concourse.bass as bass
from concourse import mybir

F32 = mybir.dt.float32
I32 = mybir.dt.int32
ALU = mybir.AluOpType
ACT = mybir.ActivationFunctionType
AX = mybir.AxisListType

P = 128
D = 1024
FT = D // P
S = 512
TT = S // P
DB, DT = 8, 4
NS = DB * DT
NH, HD = 8, 64
AW = NH * HD
HP = AW // P
NG = 4
WINDOWS = (2, 4, 8, 16)
STATE = 15
FF = 4096
PAGE = 128
PAGES = 32
N_PHYS = 320
BLOCKS = 16
PPB = 2
TOPK = 3
HT = NH * DT
NMOD = 6 * FT
SH1, SC1, G1, SH2, SC2, G2 = (i * FT for i in range(6))
EPS = 1e-6
NEG = -1e30
SCALE = HD ** -0.5
PIECE = 512
SLOTS = 8
VEC_MIX, VEC_MLP, VEC_POOL, VECS = NMOD, NMOD + FT, NMOD + 2 * FT, NMOD + 2 * FT + NG
REV = 2 * P + P - 1
C32 = {}
_at = 0
for _name, _n in (("ownmask", DB * NS), ("rev", REV + 1), ("far", P), ("last", DT * P), ("own", DT * NS)):
    C32[_name] = (_at, _at + _n)
    _at += _n
C32_W = _at
QUADS = P // HT
UNITS = PAGES // QUADS
C128 = {}
_at = 0
for _name, _n in (("ident", P), ("inv_count", NG * 16), ("flip", P), ("same_row", P), ("head", NH), ("token", DT),
                  ("pair", 2), ("quad", QUADS), ("lower", BLOCKS * BLOCKS)):
    C128[_name] = (_at, _at + _n)
    _at += _n
C128_W = _at


def bucket(n):
    n = max(n, 0)
    if n < 16:
        return n
    return min(16 + int(math.log(n / 16) / math.log(8) * 16), 31)


def shape_constants():
    c128 = np.zeros((P, C128_W), np.float32)
    part = {name: c128[:, lo:hi] for name, (lo, hi) in C128.items()}
    part["ident"][:] = np.eye(P)
    part["flip"][:] = np.eye(P)[::-1]
    for g, w in enumerate(WINDOWS):
        part["inv_count"][:, 16 * g:16 * g + 16] = 1.0 / np.minimum(np.arange(16) + 1, w)
    for p in range(P):
        part["same_row"][p, p % HT::HT] = 1.0
        part["head"][p, p % HT // DT] = 1.0
        part["token"][p, p % DT] = 1.0
        part["pair"][p, p // HT // PPB] = 1.0
        part["quad"][p, p // HT] = 1.0
    for n in range(BLOCKS):
        part["lower"][:, n * BLOCKS:n * BLOCKS + n] = 1.0
    c32 = np.zeros((32, C32_W), np.float32)
    cmask = np.zeros((NH, REV), np.float32)
    o = C32["rev"][0]
    for i in range(REV):
        rel = 2 * P - 1 - i
        if rel >= 0:
            c32[bucket(rel), o + i] = 1.0
        else:
            cmask[:, i] = NEG
    c32[31, C32["far"][0]:C32["far"][1]] = 1.0
    o = C32["last"][0]
    for t in range(DT):
        for key in range(P):
            c32[bucket(P + t - key), o + t * P + key] = 1.0
    o = C32["own"][0]
    for t in range(DT):
        for r in range(NS):
            c32[bucket(t - r % DT), o + t * NS + r] = 1.0
    o = C32["ownmask"][0]
    for row in range(HT):
        for b in range(DB):
            for key in range(NS):
                if key // DT != b or key % DT > row % DT:
                    c32[row, o + b * NS + key] = NEG
    return c128, c32, cmask


def decoder_step(nc, x_prompt, x_sample, cache_k, cache_v, state_pool, page_table, c_prompt, c_sample, w_ada, b_ada,
                 norm_mix, w_in, rel_bias, w_pool, pool_scale, w_out, norm_mlp, w_up, w_down, norm_final,
                 c128, c32, cmask,
                 y_prompt, y_sample, k_prompt, v_prompt, pool_prompt, k_sample, v_sample, pool_sample):
    ctx = ExitStack()
    with ctx:
        def sb(name, shape, dt=F32):
            return ctx.enter_context(nc.sbuf_tensor(name, shape, dt))

        def sem(name):
            return ctx.enter_context(nc.semaphore(name))

        cst = sb("cst", [P, C128_W])

        def const(name):
            return cst[:, C128[name][0]:C128[name][1]]

        ident, flip = const("ident"), const("flip")
        inv_count = const("inv_count").rearrange("p (g c) -> p g c", g=NG)
        same_row, own_head, own_token = const("same_row"), const("head"), const("token")
        own_pair, own_quad = const("pair"), const("quad")
        lower = const("lower").rearrange("p (n m) -> p n m", n=BLOCKS)
        ones = sb("ones", [P, P])
        eps = sb("eps", [P, 1])
        pages = sb("pages", [1, DB * PAGES], I32)
        xT = sb("xT", [P, FT, S])
        hT = sb("hT", [P, FT, S])
        mixT = sb("mixT", [P, FT, S])
        gT = sb("gT", [P, HP, S])
        W = sb("W", [P, 4, 4096])
        ring = sb("ring", [P, SLOTS, PPB, 512])
        ktb = mixT[:, :, :].rearrange("p (u h) n -> p u h n", u=2)
        kT = sb("kT", [P, HP, S])
        heads_out = kT[:, 0, :]
        folded = kT[:, 0:2, :]
        up_sums = kT[:, 2, :]
        scn = sb("scn", [P, NH * 2 * P])
        nearb = scn[:, :].rearrange("p (h n) -> p h n", h=NH)
        sc = scn[:, 0:UNITS * P]
        nfb = scn[:, D:2 * D]
        smp = sb("smp", [P, 2, UNITS * P + NS])
        probs, probsT = smp[:, 0, :], smp[:, 1, :]
        QBD = sb("QBD", [P, DB, HP, HT])
        qcur = sb("qcur", [P, HP, HT])
        xTs = sb("xTs", [P, FT, NS])
        hTs = sb("hTs", [P, FT, NS])
        mixS = sb("mixS", [P, FT, NS])
        kTs = sb("kTs", [P, HP, NS])
        vS = sb("vS", [NS, AW])
        uS = sb("uS", [P, NG, DB, STATE + DT])
        uSn = sb("uSn", [P, NG, NS])
        mods = sb("mods", [P, NMOD, 1 + DB])
        vecs = sb("vecs", [P, VECS])
        cT = sb("cT", [P, FT, HT])
        rstd = sb("rstd", [P, S])
        rstds = sb("rstds", [P, NS])
        farb = sb("farb", [P, NH])
        farr = sb("farr", [P, 1])
        lastr = sb("lastr", [P, P])
        own = sb("own", [P, DB, NS])
        owncur = sb("owncur", [P, NS])
        ownb = sb("ownb", [HT, NS])
        gsum = sb("gsum", [P, UNITS])
        gsplit = sb("gsplit", [P, UNITS, PPB])
        tops = sb("tops", [P, UNITS + 1])
        penalty = sb("penalty", [P, UNITS + 1])
        shift = sb("shift", [P, UNITS + 1])
        gate = sb("gate", [P, BLOCKS])
        cmps = sb("cmps", [P, 2 * BLOCKS * BLOCKS])
        cmpa, cmpb = (cmps[:, i * 256:(i + 1) * 256].rearrange("p (n m) -> p n m", n=BLOCKS) for i in range(2))
        rank = sb("rank", [P, UNITS, PPB])
        wpool = sb("wpool", [P, NG, P])
        rowmax = sb("rowmax", [P, 2])
        quadmax = sb("quadmax", [P, QUADS])
        rowsum = sb("rowsum", [P, 1])
        rden = sb("rden", [P, 1])
        stat = sb("stat", [P, 4])
        mod_a = sb("mod_a", [P, 2, FT, 1 + DB])
        gS = sb("gS", [P, 2, HP, NS])
        tmpS = gS[:, :, :, :].rearrange("p a m n -> p (a m) n")
        fstat = sb("fstat", [P, TT + 1, 2])

        rw = ring[:, :, :, :].rearrange("p a b c -> p (a b c)")
        x_tok = mixT[:, :, :].rearrange("p a b -> p (a b)").rearrange("p (t d) -> p t d", t=TT)
        xs_tok = probs[0:NS, 0:D]
        flipped = mixT[:, 0:4, :]
        c_tok = rw[0:1 + DB, 0:D]
        c_sig = rw[0:1 + DB, D:2 * D]
        vec_rows = rw[0:VECS, 2 * D:2 * D + P]
        st_rows = rw[0:DB * STATE, 2304:2304 + AW]
        const32 = rw[0:32, 3072:3072 + C32_W]
        bias_rows = rw[0:NH, 4864:4864 + REV]
        mask_rows = rw[0:NH, 5376:5376 + REV]
        relb = rw[0:32, 5888:5888 + NH]
        relx = rw[0:32, 6144:6144 + 6 * P].rearrange("p (s g h t) -> p s g h t", s=6, g=QUADS, h=NH)
        relrows = rw[0:32, 6144:6144 + 6 * P].rearrange("p (s r) -> p s r", s=6)
        ada_sums = rw[:, 7200:7200 + PIECE]
        qT = gT
        v_tok = rw[:, 0:2048].rearrange("p (t n) -> p t n", t=TT)
        logits = rw[:, 2048:3072].rearrange("p (a n) -> p a n", a=2)
        pT = rw[:, 3072:4096].rearrange("p (a n) -> p a n", a=2)
        dT = rw[:, 4096:6144].rearrange("p (g n) -> p g n", g=NG)
        UP = S + 16
        win = [rw[:, 6144:6144 + UP], rw[:, 6144 + UP:6144 + 2 * UP]]
        rows_k = hT[:, 0:TT, :]
        uT = smp[:, :, :].rearrange("p a b -> p (a b)")[:, 0:NG * UP].rearrange("p (g n) -> p g n", g=NG)
        winS = cmps[:, 0:2 * DB * (STATE + DT)].rearrange("p (a b s) -> p a b s", a=2, b=DB)
        dS = sb("dS", [P, NG, NS])
        rows_s = hT[0:NS, TT:TT + 3, :]
        junk = ring[:, 2, :, :].rearrange("p a b -> p (a b)")
        ybuf = [ring[:, 4 + i, :, :].rearrange("p a b -> p (a b)") for i in (0, 1, 2, 3, -1)]
        PS = ctx.enter_context(nc.psum_tensor("PS", [P, 8, 512], F32))

        def bank(i, parts=P, n=512, off=0):
            return PS[0:parts, i, off:off + n]

        def sems(names):
            return [sem(n) for n in names.split()]

        x_in, c_in, vec_in, cst_in, st_in, pool_in, page_in, nf_in = sems(
            "x_in c_in vec_in cst_in st_in pool_in page_in nf_in")
        w_landed = [sem(f"w_landed{i}") for i in range(4)]
        kv_landed = [sem(f"kv_landed{i}") for i in range(SLOTS)]
        bias_out, bias_back, row_out, outs, y_out = sems("bias_out bias_back row_out outs y_out")
        kv_used = sem("kv_used")
        dve_init, qbd_zero, pads, c_exp, c_ready = sems("dve_init qbd_zero pads c_exp c_ready")
        relx_ready, ada_part, ada_copied, neg_own = sems("relx_ready ada_part ada_copied neg_own")
        small_ps, small_ev, xt_ps, xt_ev_act, xt_ev_dve = sems("small_ps small_ev xt_ps xt_ev_act xt_ev_dve")
        sq_done, ms_ps, root_done = sems("sq_done ms_ps root_done")
        ada_ps, ada_ev, bias_ps, bias_ev, h_ready = sems("ada_ps ada_ev bias_ps bias_ev h_ready")
        proj_ps, proj_ev, projs_ps, projs_ev = sems("proj_ps proj_ev projs_ps projs_ev")
        near_ps, near_ev = sems("near_ps near_ev")
        own_ps, own_ev, row_ps, row_ev = sems("own_ps own_ev row_ps row_ev")
        win_step, pool_ps, pool_ev, pools_ps, pools_ev = sems(
            "win_step pool_ps pool_ev pools_ps pools_ev")
        at_scores, at_max, at_exp, at_norm, at_pT, at_pT_ev, at_out, at_out_ev = sems(
            "at_scores at_max at_exp at_norm at_pT at_pT_ev at_out at_out_ev")
        out_ps, out_ev, sq2_done, ms2_ps, root2_done, h2_ready = sems(
            "out_ps out_ev sq2_done ms2_ps root2_done h2_ready")
        dve_chain = sem("dve_chain")
        kt_ps, kt_ev, qk, sc_in, sc_ev, q_cur = sems("kt_ps kt_ev qk sc_in sc_ev q_cur")
        fin_pe, fin_dve, fin_exp, fin_chain, pT_out, pv, at_s = sems("fin_pe fin_dve fin_exp fin_chain pT_out pv at_s")
        up_ps, relu_ev, sqr_ev, dn_ps, dn_ev = sems("up_ps relu_ev sqr_ev dn_ps dn_ev")
        so_ps, so_ev, ssq, sms_ps, sroot, h2s_ready = sems("so_ps so_ev ssq sms_ps sroot h2s_ready")
        so_copied, so_fold, sup_copied, sup_fold, sdn_copied, sdn_fold = sems(
            "so_copied so_fold sup_copied sup_fold sdn_copied sdn_fold")
        sup_ps, srelu, ssqr, sdn_ps, xs_done = sems("sup_ps srelu ssqr sdn_ps xs_done")
        fin_ps, fin_ss, fin_root, fin_y = sems("fin_ps fin_ss fin_root fin_y")

        scratch = nc.dram_tensor("bias_scratch", [NH, REV], F32, kind="Internal").ap()
        block = ctx.enter_context(nc.Block())

        wada = w_ada.rearrange("l (k p) n -> (l p) k n", p=P)
        win_d = w_in.rearrange("l (k p) n -> (l p) k n", p=P)
        wout_d = w_out.rearrange("l (k p) n -> (l p) k n", p=P)
        wup_d = w_up.rearrange("l (k p) n -> (l p) k n", p=P)
        wdown_d = w_down.rearrange("l (c k p) n -> (l c) p k n", p=P, k=PIECE // P)
        ck = cache_k.rearrange("l n p h d -> (l n) p (h d)")
        cv = cache_v.rearrange("l n p h d -> (l n) p (h d)")
        kpd = k_prompt.rearrange("a b (t p) h d -> (a b t) p (h d)", p=P)
        vpd = v_prompt.rearrange("a b (t p) h d -> p (a b t) (h d)", p=P)
        ksd = k_sample.rearrange("a b t h d -> (a b t) (h d)")
        vsd = v_sample.rearrange("a b t h d -> (a b t) (h d)")
        ypd = y_prompt.rearrange("b (t p) d -> (b t) p d", p=P)
        ysd = y_sample.rearrange("b t d -> (b t) d")

        N_PRE = 18
        UP_SLOT, DOWN_SLOT = 2, 3
        PRE_USES = 4
        N_CH = FF // PIECE

        def pre_piece(n):
            if n < 4:
                return wada[:, :, n * PIECE:(n + 1) * PIECE]
            if n < 8:
                return win_d[:, :, (n - 4) * PIECE:(n - 3) * PIECE]
            if n < 16:
                return wada[:, :, (n - 4) * PIECE:(n - 3) * PIECE]
            return wout_d[:, :, (n - 16) * PIECE:(n - 15) * PIECE]

        def wslot(s, cols=PIECE):
            return W[:, s, :].rearrange("p (k n) -> p k n", n=cols)

        LAST = DB - 1

        def k_seq(b, j):
            return 2 * BLOCKS * b - BLOCKS + j

        def v_seq(b, j, more):
            return 2 * BLOCKS * b + (2 * BLOCKS if more else BLOCKS) + j

        def k_landed(b, j):
            return 16 * PPB * (4 * b - 2 + j // SLOTS + 1)

        def v_landed(b, j, more):
            return 16 * PPB * (4 * b + (4 if more else 2) + j // SLOTS + 1)

        ROWS = TT + 3
        FD, FP = 5, 6
        FC = 14
        WIN_STEPS = 2 * sum(range(1, NG + 1)) + NG * 5

        @block.sync
        def _(sp):
            sp.dma_start(c_tok[0:1, :], c_prompt).then_inc(c_in, 16)
            sp.dma_start(c_tok[1:1 + DB, :], c_sample).then_inc(c_in, 16)
            sp.dma_start(cst[:, :], c128).then_inc(cst_in, 16)
            sp.dma_start(x_tok, x_prompt.rearrange("b (t p) d -> p (b t) d", p=P)).then_inc(x_in, 16)
            sp.dma_start(xs_tok, x_sample.rearrange("b t d -> (b t) d")).then_inc(x_in, 16)
            for lo, hi, src in ((0, NMOD, b_ada), (VEC_MIX, VEC_MLP, norm_mix), (VEC_MLP, VEC_POOL, norm_mlp),
                                (VEC_POOL, VECS, pool_scale)):
                sp.dma_start(vec_rows[lo:hi, :], src.rearrange("l (k p) -> (l k) p", p=P)).then_inc(vec_in, 16)
            sp.dma_start(st_rows, state_pool.rearrange("l b s c -> (l b s) c")).then_inc(st_in, 16)
            sp.dma_start(const32, c32).then_inc(st_in, 16)
            sp.dma_start(mask_rows, cmask).then_inc(st_in, 16)
            sp.dma_start(relb, rel_bias).then_inc(st_in, 16)
            for n in range(4):
                sp.dma_start(wslot(n), pre_piece(n)).then_inc(w_landed[n], 16)
            sp.dma_start(wpool[:, :, :], w_pool.rearrange("l g c d -> c (l g) d")).then_inc(pool_in, 16)
            sp.dma_start(pages[0:1, :], page_table.rearrange("b n -> (b n)")[None, :]).then_inc(page_in, 16)
            piece_used = ([(ada_ps, n + 1) for n in range(4)]
                          + [(projs_ps, 1), (projs_ps, 2), (proj_ps, 13), (projs_ps, 3)]
                          + [(ada_ps, n + 1) for n in range(4, 12)])
            for n in range(4, N_PRE):
                sp.wait_ge(*piece_used[n - 4])
                sp.dma_start(wslot(n % 4), pre_piece(n)).then_inc(w_landed[n % 4], 16)
                if n == 7:
                    sp.wait_ge(bias_ev, 1)
                    sp.dma_start(scratch, bias_rows).then_inc(bias_out, 16)
                    sp.wait_ge(bias_out, 16)
                    sp.dma_start(flipped.rearrange("p a (b n) -> p (a b) n", b=2),
                                 bass.AP(scratch.tensor, 0, [[1, P], [REV, NH], [1, 2 * P]])).then_inc(bias_back, 16)
            sp.wait_ge(page_in, 16)
            sp.wait_ge(at_out_ev, HP)
            sp.wait_ge(pool_ev, NG)
            sp.wait_ge(outs, 16 * 3)

            def load_block(cache, b, j, seq):
                slot = j % SLOTS
                for pg in range(PPB):
                    at = b * PAGES + PPB * j + pg
                    phys = sp.value_load(pages[0:1, bass.ds(at, 1)], min_val=0, max_val=N_PHYS - 1)
                    if pg == 0 and not (isinstance(seq, int) and seq < SLOTS):
                        sp.wait_ge(kv_used, seq - SLOTS + 1)
                    sp.dma_start(ring[:, slot, pg, :], cache[bass.ds(phys, 1), :, :].rearrange("a p n -> (a p) n"))\
                      .then_inc(kv_landed[slot], 16)

            def load_up(b):
                sp.dma_start(wslot(UP_SLOT), wup_d[:, :, bass.ds(b * PIECE, PIECE)]).then_inc(w_landed[UP_SLOT], 16)

            def load_down(b):
                sp.dma_start(wslot(DOWN_SLOT, D), wdown_d[bass.ds(b, 1), :, :, :]
                             .rearrange("a p k n -> (a p) k n")).then_inc(w_landed[DOWN_SLOT], 16)

            for j in range(BLOCKS):
                load_block(ck, 0, j, j)
            with sp.Fori(0, LAST) as b:
                for j in range(BLOCKS):
                    load_block(ck, b + 1, j, k_seq(b + 1, j))
                    if j == 1:
                        load_up(b)
                    if j == 9:
                        load_down(b)
                for j in range(BLOCKS):
                    load_block(cv, b, j, v_seq(b, j, True))
            for j in range(BLOCKS):
                load_block(cv, LAST, j, v_seq(LAST, j, False))
                if j == 1:
                    load_up(LAST)
                if j == SLOTS:
                    load_down(LAST)
            sp.dma_start(nfb, bass.AP(norm_final.tensor, 0, [[0, P], [1, D]])).then_inc(nf_in, 16)
            for i in range(2 * (N_CH - 1)):
                if i < 2:
                    sp.wait_ge(so_ps, 1)
                else:
                    sp.wait_ge((sup_ps, sdn_ps)[i % 2], (i - 4) // 2 + 2)
                if i % 2 == 0:
                    sp.dma_start(wslot(i % 4), wup_d[:, :, i // 2 * PIECE:(i // 2 + 1) * PIECE])\
                      .then_inc(w_landed[i % 4], 16)
                else:
                    sp.dma_start(wslot(i % 4, D), wdown_d[i // 2, :, :, :]).then_inc(w_landed[i % 4], 16)
            for t in range(TT):
                sp.wait_ge(fin_y, t + 1)
                sp.dma_start(ypd[t, :, :], ybuf[t]).then_inc(y_out, 16)
            sp.wait_ge(fin_y, TT + 1)
            sp.dma_start(ysd, ybuf[TT][0:NS, :]).then_inc(y_out, 16)
            sp.wait_ge(bias_out, 16)
            sp.wait_ge(row_out, 16 * ROWS)
            sp.wait_ge(outs, 16 * 3)
            sp.wait_ge(y_out, 16 * (TT + 1))

        @block.gpsimd
        def _(pool):
            pool.memset(QBD[:, :, :, :], 0.0).then_inc(qbd_zero, 1)
            pool.dma_start(pool_sample[0, :, 0:STATE - DT, :], state_pool[0, :, DT:STATE, :]).then_inc(outs, 16)
            step = [0]

            def chain(ins):
                step[0] += 1
                ins.then_inc(win_step, 1)
                pool.wait_ge(win_step, step[0])

            pool.wait_ge(proj_ev, 12)
            pool.dma_start(vpd, v_tok).then_inc(outs, 16)
            pool.wait_ge(proj_ev, 17)
            pool.dma_start(vsd, vS[:, :]).then_inc(outs, 16)
            pool.wait_ge(pads, 1)
            pool.wait_ge(bias_out, 16)
            for g, w in enumerate(WINDOWS):
                src, sh, n = uT[:, g, :], 1, 0
                while sh < w:
                    lo = 2 * sh - 1
                    chain(pool.tensor_tensor(win[n % 2][:, lo:UP], src[:, lo:UP], src[:, lo - sh:UP - sh], ALU.add))
                    src, sh, n = win[n % 2], 2 * sh, n + 1
                other = win[n % 2]
                chain(pool.tensor_scalar(other[:, 32:UP], src[:, 32:UP], 1.0 / w, None, ALU.mult))
                chain(pool.tensor_tensor(other[:, 16:32], src[:, 16:32], inv_count[:, g, :], ALU.mult))
                chain(pool.tensor_tensor(dT[:, g, :], other[:, 16:UP], uT[:, g, 16:UP], ALU.subtract))
            pool.wait_ge(projs_ev, 3)
            L = STATE + DT
            for g, w in enumerate(WINDOWS):
                src, sh, n = uS[:, g, :, :], 1, 0
                while sh < w:
                    lo = 2 * sh - 1
                    chain(pool.tensor_tensor(winS[:, n % 2, :, lo:L], src[:, :, lo:L], src[:, :, lo - sh:L - sh],
                                             ALU.add))
                    src, sh, n = winS[:, n % 2, :, :], 2 * sh, n + 1
                other = winS[:, n % 2, :, :]
                chain(pool.tensor_scalar(other[:, :, STATE:L], src[:, :, STATE:L], 1.0 / w, None, ALU.mult))
                chain(pool.tensor_tensor(dS[:, g, :].rearrange("p (b t) -> p b t", b=DB), other[:, :, STATE:L],
                                         uS[:, g, :, STATE:L], ALU.subtract))
            for t in range(TT):
                pool.wait_ge(row_ev, t + 1)
                pool.dma_start(kpd[t, :, :], rows_k[:, t, :]).then_inc(row_out, 16)
            pool.wait_ge(row_ev, ROWS)
            pool.dma_start(ksd, rows_s[:, 0, :]).then_inc(row_out, 16)
            pool.dma_start(pool_sample[0, :, STATE - DT:STATE, :], rows_s[:, 1, :]).then_inc(row_out, 16)
            pool.dma_start(pool_prompt[0, 0, :, :], rows_s[0:STATE, 2, :]).then_inc(row_out, 16)

            def take_queries(b, first=False):
                if first:
                    pool.wait_ge(projs_ev, 1)
                else:
                    pool.wait_ge(qk, UNITS * b)
                pool.tensor_copy(qcur[:, :, :], QBD[:, bass.ds(b, 1), :, :].rearrange("p a h c -> p (a h) c"))\
                    .then_inc(q_cur, 1)

            def squares(b):
                for m in range(HP):
                    pool.wait_ge(relu_ev, HP * b + m + 1)
                    pool.tensor_tensor(gT[:, m, :], gT[:, m, :], gT[:, m, :], ALU.mult).then_inc(sqr_ev, 1)

            take_queries(0, first=True)
            with pool.Fori(0, LAST) as b:
                take_queries(b + 1)
                squares(b)
            squares(LAST)

        @block.scalar
        def _(act):
            act.wait_ge(c_in, 32)
            act.activation(c_sig, c_tok, ACT.Exp, scale=-1.0).then_inc(c_exp, 1)
            for f in range(0, FT, 2):
                act.wait_ge(xt_ps, f + 1)
                act.activation(xT[:, f, :], bank(f % 4), ACT.Copy).then_inc(xt_ev_act, 1)
            act.wait_ge(xt_ev_act, FT // 2)
            act.wait_ge(xt_ev_dve, FT // 2 + 1)
            for f in range(FT):
                act.activation(hT[:, f, :], xT[:, f, :], ACT.Square).then_inc(sq_done, 1)
            act.activation(hTs[:, :, :], xTs[:, :, :], ACT.Square).then_inc(sq_done, 1)
            act.wait_ge(ms_ps, 1)
            act.wait_ge(dve_init, 2)
            act.activation(rstd[:, :], bank(7), ACT.Sqrt, bias=eps[:, 0:1], scale=1.0 / D).then_inc(root_done, 1)
            act.activation(rstds[:, :], bank(5, P, NS), ACT.Sqrt, bias=eps[:, 0:1], scale=1.0 / D)\
               .then_inc(root_done, 1)
            for g in range(17):
                act.wait_ge(proj_ps, g + 1)
                src = bank(2 + g % 2)
                if g < 4:
                    act.activation(qT[:, g, :], src, ACT.Copy, scale=SCALE).then_inc(proj_ev, 1)
                elif g < 8:
                    act.activation(kT[:, g - 4, :], src, ACT.Copy).then_inc(proj_ev, 1)
                elif g < 12:
                    act.activation(v_tok[:, g - 8, :], src, ACT.Copy).then_inc(proj_ev, 1)
                elif g == 12:
                    act.activation(vS[:, :], bank(2 + g % 2, NS), ACT.Copy).then_inc(proj_ev, 1)
                else:
                    if g == 13:
                        act.wait_ge(pads, 1)
                    act.activation(uT[:, g - 13, 16:UP], src, ACT.Copy).then_inc(proj_ev, 1)

            def attention_out(hp):
                act.activation(mixT[:, hp, :], bank(4 + hp % 2), ACT.Copy).then_inc(at_out_ev, 1)

            for a in range(NH * TT):
                n = (a % TT + 1) * P
                act.wait_ge(at_max, a + 1)
                act.activation(logits[:, a % 2, 0:n], logits[:, a % 2, 0:n], ACT.Exp, bias=stat[:, a % 2:a % 2 + 1],
                               accum_out=stat[:, 2 + a % 2:3 + a % 2]).then_inc(at_exp, 1)
                act.wait_ge(at_pT, a + 1)
                if a >= 2:
                    act.wait_ge(at_out, a - 1)
                act.activation(pT[:, a % 2, 0:n], bank(a % 2, P, n), ACT.Copy).then_inc(at_pT_ev, 1)
                if a > 2 * TT and a % (2 * TT) == 1:
                    act.wait_ge(at_out, a - 1)
                    attention_out(a // (2 * TT) - 1)
            act.wait_ge(at_out, NH * TT)
            attention_out(HP - 1)
            for g in range(NG):
                act.wait_ge(pool_ps, g + 1)
                act.activation(mixT[:, HP + g, :], bank(6 + g % 2), ACT.Copy,
                               scale=vecs[:, VEC_POOL + g:VEC_POOL + g + 1]).then_inc(pool_ev, 1)
            act.wait_ge(row_out, 16 * ROWS)
            for f in range(FT):
                act.wait_ge(out_ev, f + 1)
                act.activation(hT[:, f, :], xT[:, f, :], ACT.Square).then_inc(sq2_done, 1)
            act.wait_ge(ms2_ps, 1)
            act.activation(rstd[:, :], bank(7), ACT.Sqrt, bias=eps[:, 0:1], scale=1.0 / D).then_inc(root2_done, 1)

            def keys_out(b, n, first=False):
                j, pg, u = n // PPB, n % PPB, n // QUADS
                if pg == 0:
                    act.wait_ge(kt_ps, BLOCKS * b + j + 1)
                else:
                    act.wait_ge(kv_used, (j if first else k_seq(b, j)) + 1)
                if n % QUADS == 0 and not (first and u < 2):
                    act.wait_ge(qk, UNITS * b + u - 1)
                act.activation(ktb[:, u % 2, :, n % QUADS * P:(n % QUADS + 1) * P],
                               bank(pg).rearrange("p (h n) -> p h n", h=HP), ACT.Copy).then_inc(kt_ev, 1)

            def exps(b):
                act.wait_ge(fin_dve, FD * b + 3)
                act.activation(probs, probs, ACT.Exp, accum_out=rowsum[:, 0:1]).then_inc(fin_exp, 1)

            def probs_out(b, half):
                act.wait_ge(fin_pe, FP * b + 4 + half)
                act.activation(probsT[:, 512 * half:512 * half + 512], bank(7), ACT.Copy).then_inc(pT_out, 1)

            def relu(b, m):
                act.wait_ge(up_ps, HP * b + m + 1)
                act.activation(gT[:, m, :], bank(5 + m % 2), ACT.Relu).then_inc(relu_ev, 1)

            for n in range(PAGES):
                keys_out(0, n, first=True)
            with act.Fori(0, LAST) as b:
                for n in range(PAGES):
                    keys_out(b + 1, n)
                    if n in (8, 16, 24):
                        relu(b, n // 8 - 1)
                    if n == 11:
                        exps(b)
                    if n == 18:
                        probs_out(b, 0)
                    if n == 21:
                        probs_out(b, 1)
                relu(b, HP - 1)
            relu(LAST, 0)
            exps(LAST)
            relu(LAST, 1)
            probs_out(LAST, 0)
            relu(LAST, 2)
            probs_out(LAST, 1)
            relu(LAST, 3)

            act.wait_ge(so_ev, 1)
            act.activation(hTs[:, :, :], xTs[:, :, :], ACT.Square).then_inc(ssq, 1)
            act.wait_ge(sms_ps, 1)
            act.activation(rstds[:, :], bank(1, P, NS), ACT.Sqrt, bias=eps[:, 0:1], scale=1.0 / D).then_inc(sroot, 1)

            def final_norm(t):
                n = P if t < TT else NS
                act.wait_ge(fin_ps, t + 1)
                act.activation(junk[0:n, :], PS[0:n, 4 + 2 * (t % 2):6 + 2 * (t % 2), :].rearrange("p a b -> p (a b)"),
                               ACT.Square, accum_out=fstat[0:n, t, 0:1]).then_inc(fin_ss, 1)
                act.wait_ge(fin_ss, t + 1)
                act.activation(fstat[0:n, t, 1:2], fstat[0:n, t, 0:1], ACT.Sqrt, bias=eps[0:n, 0:1], scale=1.0 / D)\
                   .then_inc(fin_root, 1)

            for i in range(N_CH):
                act.wait_ge(sup_fold, i + 1)
                if i >= 2:
                    act.wait_ge(sdn_ps, i - 1)
                act.activation(gS[:, i % 2, :, :].rearrange("p a b -> p (a b)"), bank(1, P, HP * NS), ACT.Relu)\
                   .then_inc(srelu, 1)
                if 1 <= i <= TT:
                    final_norm(i - 1)
            final_norm(TT)

        @block.vector
        def _(dve):
            steps = [0]

            def link(ins):
                steps[0] += 1
                ins.then_inc(dve_chain, 1)
                dve.wait_ge(dve_chain, steps[0])

            dve.memset(ones[:, :], 1.0).then_inc(dve_init, 1)
            dve.memset(eps[:, :], EPS).then_inc(dve_init, 1)
            dve.memset(cT[:, :, :], 0.0).then_inc(dve_init, 1)
            dve.memset(own[:, :, :], NEG).then_inc(dve_init, 1)
            dve.memset(penalty[:, :], 0.0).then_inc(dve_init, 1)
            dve.wait_ge(c_exp, 1)
            link(dve.tensor_scalar(c_sig, c_sig, 1.0, None, ALU.add))
            link(dve.reciprocal(c_sig, c_sig))
            dve.tensor_tensor(c_sig, c_sig, c_tok, ALU.mult).then_inc(c_ready, 1)
            link(dve.memset(relrows, 0.0))
            dve.wait_ge(st_in, 64)
            for t in range(DT):
                dve.tensor_copy(relx[:, t, QUADS - 1, :, t], relb)
            for g in range(QUADS):
                over = relb[:, :, None].to_broadcast([32, NH, DT])
                if g < QUADS - 1:
                    dve.tensor_copy(relx[:, DT, g, :, :], over)
                last = dve.tensor_copy(relx[:, DT + 1, g, :, :], over)
            last.then_inc(relx_ready, 1)
            for f in range(1, FT, 2):
                dve.wait_ge(xt_ps, f + 1)
                dve.tensor_copy(xT[:, f, :], bank(f % 4)).then_inc(xt_ev_dve, 1)
            dve.wait_ge(xt_ps, FT + 1)
            dve.tensor_copy(xTs[:, :, :].rearrange("p a b -> p (a b)"), bank(4, P, FT * NS)).then_inc(xt_ev_dve, 1)
            dve.memset(uT[:, :, 0:16], 0.0).then_inc(pads, 1)
            dve.wait_ge(small_ps, 1)
            dve.wait_ge(dve_init, 3)
            dve.tensor_copy(cT[:, :, 0:1 + DB], bank(5, P, FT * (1 + DB)).rearrange("p (f c) -> p f c", f=FT))\
               .then_inc(small_ev, 1)
            dve.tensor_copy(vecs[:, :], bank(5, P, VECS, 128)).then_inc(small_ev, 1)
            dve.tensor_copy(uS[:, :, :, 0:STATE], bank(6, P, NG * DB * STATE)
                            .rearrange("p (g b s) -> p g b s", g=NG, b=DB)).then_inc(small_ev, 1)
            dve.wait_ge(bias_ps, 1)
            dve.tensor_tensor(bias_rows, bank(6, NH, REV), mask_rows, ALU.add).then_inc(bias_ev, 1)
            dve.wait_ge(bias_ps, 2)
            dve.tensor_copy(farb[:, :], bank(4, P, NH)).then_inc(bias_ev, 1)
            dve.tensor_copy(farr[:, :], bank(4, P, 1, 16)).then_inc(bias_ev, 1)
            dve.tensor_copy(lastr[:, :], bank(4, P, P, P)).then_inc(bias_ev, 1)
            dve.tensor_copy(ownb[:, :], bank(4, HT, NS, 64)).then_inc(bias_ev, 1)

            def ada_out(p):
                dve.wait_ge(ada_part, p + 1)
                if p:
                    dve.wait_ge(ada_ps, p)
                dve.tensor_copy(ada_sums, bank(p % 2 if p < 4 else 7)).then_inc(ada_copied, 1)

            def modulation(p):
                dve.wait_ge(ada_ps, p + 1)
                dve.tensor_tensor(mods[:, 4 * p:4 * p + 4, :],
                                  bank(2 if p < 4 else 7, P, 4 * (1 + DB)).rearrange("p (m c) -> p m c", m=4),
                                  vecs[:, 4 * p:4 * p + 4][:, :, None].to_broadcast([P, 4, 1 + DB]), ALU.add)\
                   .then_inc(ada_ev, 1)

            def weighted(which, scale, vec):
                link(dve.tensor_scalar(mod_a[:, which, :, :], mods[:, scale:scale + FT, :], 1.0, None, ALU.add))
                link(dve.tensor_tensor(mod_a[:, which, :, :], mod_a[:, which, :, :],
                                       vecs[:, vec:vec + FT][:, :, None].to_broadcast([P, FT, 1 + DB]), ALU.mult))

            def per_token(table):
                return table[:, :, 1:1 + DB][:, :, :, None].to_broadcast([P, FT, DB, DT])

            def split(tile):
                return tile[:, :, :].rearrange("p f (b t) -> p f b t", b=DB)

            def modulate_sample(which, shift):
                link(dve.tensor_tensor(hTs[:, :, :], xTs[:, :, :], rstds[:, None, :].to_broadcast([P, FT, NS]), ALU.mult))
                link(dve.tensor_tensor(split(hTs), split(hTs), per_token(mod_a[:, which, :, :]), ALU.mult))
                return dve.tensor_tensor(split(hTs), split(hTs), per_token(mods[:, shift:shift + FT, :]), ALU.add)

            def modulate_prompt(which, shift, ready):
                for f in range(FT):
                    link(dve.tensor_tensor(hT[:, f, :], xT[:, f, :], rstd[:, :], ALU.mult))
                    dve.tensor_scalar(hT[:, f, :], hT[:, f, :], mod_a[:, which, f, 0:1], mods[:, shift + f, 0:1],
                                      ALU.mult, ALU.add).then_inc(ready, 1)

            dve.wait_ge(root_done, 2)
            link(dve.reciprocal(rstd[:, :], rstd[:, :]))
            link(dve.reciprocal(rstds[:, :], rstds[:, :]))
            for p in range(4):
                ada_out(p)
                if p:
                    modulation(p - 1)
            modulation(3)
            dve.wait_ge(ada_ev, 4)
            weighted(0, SC1, VEC_MIX)
            dve.wait_ge(xt_ev_act, FT // 2)
            modulate_sample(0, SH1).then_inc(h_ready, 1)
            modulate_prompt(0, SH1, h_ready)

            dve.wait_ge(projs_ps, 1)
            dve.wait_ge(qbd_zero, 1)
            for hp in range(HP):
                for half in range(2):
                    r, c = slice(HD * half, HD * half + HD), 2 * DT * hp + DT * half
                    last = dve.tensor_scalar(QBD[r, :, hp, c:c + DT],
                                             PS[r, 4, hp * NS:(hp + 1) * NS].rearrange("p (b t) -> p b t", b=DB),
                                             SCALE, None, ALU.mult)
                    if (hp, half) != (HP - 1, 1):
                        link(last)
            last.then_inc(projs_ev, 1)
            dve.wait_ge(projs_ps, 2)
            dve.tensor_copy(kTs[:, :, :].rearrange("p a b -> p (a b)"), bank(5, P, HP * NS)).then_inc(projs_ev, 1)
            dve.wait_ge(projs_ps, 3)
            link(dve.tensor_copy(uS[:, :, :, STATE:STATE + DT],
                                 bank(6, P, NG * NS).rearrange("p (g b t) -> p g b t", g=NG, b=DB)))
            dve.tensor_copy(uSn[:, :, :].rearrange("p a b -> p (a b)"), bank(6, P, NG * NS)).then_inc(projs_ev, 1)
            dve.wait_ge(own_ps, 1)
            dve.wait_ge(bias_ev, 5)
            dve.wait_ge(dve_init, 5)
            link(dve.tensor_tensor(own[0:HT, :, :], bank(7, HT, DB * NS).rearrange("p (b c) -> p b c", b=DB),
                                   ownb[:, None, :].to_broadcast([HT, DB, NS]), ALU.add))
            dve.tensor_tensor(own[0:HT, :, :], own[0:HT, :, :], const32[:, C32["ownmask"][0]:C32["ownmask"][1]]
                              .rearrange("p (b c) -> p b c", b=DB), ALU.add).then_inc(own_ev, 1)

            def logits_in(a):
                h, i = a // TT, a % TT
                n, near = (i + 1) * P, P if i == 0 else 2 * P
                dve.wait_ge(at_scores, a + 1)
                if a >= 2:
                    dve.wait_ge(at_pT, a - 1)
                src = bank(2 + a % 2)
                if n > near:
                    dve.tensor_scalar(logits[:, a % 2, 0:n - near], src[:, 0:n - near], farb[:, h:h + 1], None,
                                      ALU.add).then_inc(dve_chain, 1)
                    steps[0] += 1
                link(dve.tensor_tensor(logits[:, a % 2, n - near:n], src[:, n - near:n], nearb[:, h, 2 * P - near:2 * P],
                                       ALU.add))
                dve.tensor_reduce(stat[:, a % 2:a % 2 + 1], logits[:, a % 2, 0:n], AX.X, ALU.max, negate=True)\
                   .then_inc(at_max, 1)

            def normalize(a):
                n = (a % TT + 1) * P
                dve.wait_ge(at_exp, a + 1)
                link(dve.reciprocal(stat[:, 2 + a % 2:3 + a % 2], stat[:, 2 + a % 2:3 + a % 2]))
                dve.tensor_scalar(logits[:, a % 2, 0:n], logits[:, a % 2, 0:n], stat[:, 2 + a % 2:3 + a % 2], None,
                                  ALU.mult).then_inc(at_norm, 1)

            def rows(r):
                dve.wait_ge(row_ps, r + 1)
                if r < TT:
                    dve.tensor_copy(rows_k[:, r, :], bank(6)).then_inc(row_ev, 1)
                else:
                    n = NS if r < TT + 2 else STATE
                    dve.tensor_copy(rows_s[0:n, r - TT, :], bank(6, n)).then_inc(row_ev, 1)

            for i in range(4):
                dve.wait_ge(near_ps, i + 1)
                dve.tensor_copy(scn[:, 512 * i:512 * i + 512], bank(4 + i % 2)).then_inc(near_ev, 1)
            dve.wait_ge(near_ev, 4)
            logits_in(0)
            for a in range(NH * TT):
                if a + 1 < NH * TT:
                    logits_in(a + 1)
                normalize(a)
                h = a // TT
                if a % TT == 1 and h:
                    modulation(3 + h)
                if a % TT == TT - 1:
                    if h < ROWS:
                        rows(h)
                    ada_out(4 + h)
            modulation(3 + NH)
            dve.wait_ge(pools_ps, 1)
            dve.tensor_tensor(mixS[:, HP:FT, :], bank(5, P, NG * NS).rearrange("p (g n) -> p g n", g=NG),
                              vecs[:, VEC_POOL:VEC_POOL + NG][:, :, None].to_broadcast([P, NG, NS]), ALU.mult)\
               .then_inc(pools_ev, 1)
            dve.wait_ge(ada_ev, 12)
            weighted(1, SC2, VEC_MLP)
            for m in range(FT):
                dve.wait_ge(out_ps, m + 1)
                dve.scalar_tensor_tensor(xT[:, m, :], bank(2 + m % 2), mods[:, G1 + m, 0:1], xT[:, m, :],
                                         ALU.mult, ALU.add).then_inc(out_ev, 1)
            dve.wait_ge(root2_done, 1)
            link(dve.reciprocal(rstd[:, :], rstd[:, :]))
            modulate_prompt(1, SH2, h2_ready)

            def scores_out(b, half):
                dve.wait_ge(qk, UNITS * b + 4 * (half + 1))
                src = bank(2 + half)
                lo, mid, hi = 512 * half, 512 * half + (384 if half else 512), 512 * half + 512
                dve.tensor_reduce(gsum[:, 4 * half:4 * half + 4], src.rearrange("p (u n) -> p u n", n=P), AX.X, ALU.add)
                ins = dve.tensor_scalar(sc[:, lo:mid], src[:, 0:mid - lo], farr[:, 0:1], None, ALU.add)
                if half:
                    ins = dve.tensor_tensor(sc[:, mid:hi], src[:, mid - lo:512], lastr[:, :], ALU.add)
                ins.then_inc(sc_in, 1)
                dve.wait_ge(sc_in, 2 * b + half + 1)
                dve.tensor_reduce(tops[:, 4 * half:4 * half + 4], sc[:, lo:hi].rearrange("p (u n) -> p u n", n=P),
                                  AX.X, ALU.max).then_inc(sc_ev, 1)

            def fchain(ins, b, k):
                ins.then_inc(fin_chain, 1)
                dve.wait_ge(fin_chain, FC * b + k)

            def split_sums(b):
                dve.wait_ge(sc_ev, 2 * b + 2)
                dve.tensor_tensor(gsplit[:, :, :], gsum[:, :, None].to_broadcast([P, UNITS, PPB]),
                                  own_pair[:, None, :].to_broadcast([P, UNITS, PPB]), ALU.mult).then_inc(fin_dve, 1)

            def rank_blocks(b):
                dve.tensor_copy(owncur[:, :], own[:, bass.ds(b, 1), :].rearrange("p a c -> p (a c)"))
                dve.wait_ge(fin_pe, FP * b + 1)
                fchain(dve.tensor_copy(gate[:, :], bank(7, P, BLOCKS)), b, 1)
                over_n = gate[:, None, :].to_broadcast([P, BLOCKS, BLOCKS])
                over_m = gate[:, :, None].to_broadcast([P, BLOCKS, BLOCKS])
                dve.tensor_reduce(tops[:, UNITS:UNITS + 1], owncur[:, :], AX.X, ALU.max)
                fchain(dve.tensor_tensor(cmpb, over_n, over_m, ALU.is_equal), b, 2)
                fchain(dve.tensor_tensor(cmpb, cmpb, lower, ALU.mult), b, 3)
                fchain(dve.tensor_tensor(cmpa, over_n, over_m, ALU.is_gt), b, 4)
                fchain(dve.tensor_tensor(cmpa, cmpa, cmpb, ALU.add), b, 5)
                fchain(dve.tensor_reduce(rank[:, :, :].rearrange("p u g -> p (u g)"), cmpa, AX.X, ALU.add), b, 6)
                fchain(dve.tensor_scalar(rank[:, :, :], rank[:, :, :], float(TOPK), NEG, ALU.is_ge, ALU.mult), b, 7)
                fchain(dve.tensor_tensor(rank[:, :, :], rank[:, :, :], own_pair[:, None, :]
                                         .to_broadcast([P, UNITS, PPB]), ALU.mult), b, 8)
                fchain(dve.tensor_reduce(penalty[:, 0:UNITS], rank[:, :, :], AX.X, ALU.add), b, 9)
                fchain(dve.tensor_tensor(shift[:, :], tops[:, :], penalty[:, :], ALU.add), b, 10)
                fchain(dve.tensor_reduce(rowmax[:, 0:1], shift[:, :], AX.X, ALU.max), b, 11)
                dve.tensor_scalar(quadmax[:, :], own_quad, rowmax[:, 0:1], None, ALU.mult).then_inc(fin_dve, 1)

            def less_max(b):
                dve.wait_ge(fin_pe, FP * b + 2)
                fchain(dve.tensor_reduce(rowmax[:, 1:2], bank(7, P, QUADS), AX.X, ALU.max), b, 12)
                fchain(dve.tensor_scalar(shift[:, :], penalty[:, :], rowmax[:, 1:2], None, ALU.subtract), b, 13)
                dve.tensor_tensor(probs[:, 0:UNITS * P].rearrange("p (u n) -> p u n", n=P),
                                  sc.rearrange("p (u n) -> p u n", n=P),
                                  shift[:, 0:UNITS, None].to_broadcast([P, UNITS, P]), ALU.add)
                dve.tensor_scalar(probs[:, UNITS * P:], owncur[:, :], shift[:, UNITS:UNITS + 1], None, ALU.add)\
                   .then_inc(fin_dve, 1)

            def take_total(b):
                dve.wait_ge(fin_pe, FP * b + 3)
                fchain(dve.reciprocal(rden[:, :], bank(7, P, 1)), b, 14)
                dve.tensor_copy(probsT[0:NS, UNITS * P:], bank(7, NS, HT, P)).then_inc(fin_dve, 1)

            def down_out(b, m):
                dve.wait_ge(dn_ps, FT * b + m + 1)
                dve.scalar_tensor_tensor(xT[:, m, :], bank(5 + m % 2), mods[:, G2 + m, 0:1], xT[:, m, :],
                                         ALU.mult, ALU.add).then_inc(dn_ev, 1)

            def own_heads(b):
                dve.wait_ge(pv, b + 1)
                dve.scalar_tensor_tensor(heads_out.rearrange("p (h d) -> p h d", h=NH),
                                         bank(4).rearrange("p (h d) -> p h d", h=NH), rden[:, 0:1],
                                         own_head[:, :, None].to_broadcast([P, NH, HD]), ALU.mult, ALU.mult)\
                   .then_inc(fin_dve, 1)

            def attention_sample(b):
                dve.wait_ge(fin_pe, FP * (b + 1))
                dve.tensor_copy(mixS[:, 0:HP, bass.ds(DT * b, DT)], bank(7, P, HP * DT)
                                .rearrange("p (h t) -> p h t", h=HP)).then_inc(at_s, 1)

            def sequence_end(b):
                for m in range(FT):
                    down_out(b, m)
                    if m == FT - 3:
                        own_heads(b)
                attention_sample(b)

            for half in range(2):
                scores_out(0, half)
            with dve.Fori(0, LAST) as b:
                split_sums(b)
                rank_blocks(b)
                less_max(b)
                take_total(b)
                for half in range(2):
                    scores_out(b + 1, half)
                sequence_end(b)
            split_sums(LAST)
            rank_blocks(LAST)
            less_max(LAST)
            take_total(LAST)
            sequence_end(LAST)

            dve.wait_ge(so_ps, 1)
            dve.tensor_copy(folded, PS[:, 0:2, :]).then_inc(so_copied, 1)
            dve.wait_ge(so_fold, 1)
            link(dve.tensor_tensor(split(tmpS), bank(2, P, FT * NS).rearrange("p (f b t) -> p f b t", f=FT, b=DB),
                                   per_token(mods[:, G1:G1 + FT, :]), ALU.mult))
            dve.tensor_tensor(xTs[:, :, :], xTs[:, :, :], tmpS[:, :, :], ALU.add).then_inc(so_ev, 1)
            dve.wait_ge(so_ev, 1)
            dve.wait_ge(sroot, 1)
            link(dve.reciprocal(rstds[:, :], rstds[:, :]))
            modulate_sample(1, SH2).then_inc(h2s_ready, 1)

            def final_out(t):
                n = P if t < TT else NS
                dve.wait_ge(fin_root, t + 1)
                if t == 0:
                    dve.wait_ge(nf_in, 16)
                link(dve.reciprocal(fstat[0:n, t, 1:2], fstat[0:n, t, 1:2]))
                src = PS[0:n, 4 + 2 * (t % 2):6 + 2 * (t % 2), :].rearrange("p a b -> p (a b)")
                dve.scalar_tensor_tensor(ybuf[t][0:n, :], src, fstat[0:n, t, 1:2], nfb[0:n, :],
                                         ALU.mult, ALU.mult).then_inc(fin_y, 1)

            for i in range(N_CH):
                dve.wait_ge(sup_ps, i + 1)
                dve.tensor_copy(up_sums, bank(0)).then_inc(sup_copied, 1)
                dve.wait_ge(srelu, i + 1)
                dve.tensor_tensor(gS[:, i % 2, :, :], gS[:, i % 2, :, :], gS[:, i % 2, :, :], ALU.mult)\
                   .then_inc(ssqr, 1)
                if 1 <= i <= TT:
                    final_out(i - 1)
            dve.wait_ge(sdn_ps, N_CH)
            dve.tensor_copy(folded, PS[:, 2:4, :]).then_inc(sdn_copied, 1)
            dve.wait_ge(sdn_fold, 1)
            link(dve.tensor_tensor(split(tmpS), bank(1, P, FT * NS).rearrange("p (f b t) -> p f b t", f=FT, b=DB),
                                   per_token(mods[:, G2:G2 + FT, :]), ALU.mult))
            dve.tensor_tensor(xTs[:, :, :], xTs[:, :, :], tmpS[:, :, :], ALU.add).then_inc(xs_done, 1)
            final_out(TT)

        @block.tensor
        def _(pe):
            def mm(out, lhsT, rhs, start=True, stop=True, **kw):
                return pe.matmul(out, lhsT, rhs, start=start, stop=stop, **kw)

            def quarter(i, g, lhsT, rhs, start, stop, n=512, off=0):
                return mm(PS[HT * g:HT * g + HT, i, off:off + n], lhsT, rhs, start, stop, tile_position=(0, HT * g),
                          skip_group_check=True)

            pe.wait_ge(cst_in, 16)
            pe.wait_ge(x_in, 32)
            for f in range(FT):
                if f >= 4:
                    pe.wait_ge((xt_ev_act, xt_ev_dve)[f % 2], (f - 4) // 2 + 1)
                for t in range(TT):
                    last = pe.transpose(bank(f % 4, P, P, t * P), x_tok[:, t, f * P:(f + 1) * P], ident)
                last.then_inc(xt_ps, 1)
            for f in range(FT):
                last = pe.transpose(bank(4, P, NS, f * NS), xs_tok[:, f * P:(f + 1) * P], ident[0:NS, 0:NS])
            last.then_inc(xt_ps, 1)
            pe.wait_ge(c_ready, 1)
            for f in range(FT):
                pe.transpose(bank(5, P, 1 + DB, f * (1 + DB)), c_sig[:, f * P:(f + 1) * P], ident[0:1 + DB, 0:1 + DB])
            pe.wait_ge(vec_in, 64)
            pe.transpose(bank(5, P, VECS, 128), vec_rows, ident[0:VECS, 0:VECS])
            pe.wait_ge(st_in, 64)
            for g in range(NG):
                last = pe.transpose(bank(6, P, DB * STATE, g * DB * STATE), st_rows[:, g * P:(g + 1) * P],
                                    ident[0:DB * STATE, 0:DB * STATE])
            last.then_inc(small_ps, 1)
            pe.wait_ge(small_ev, 3)
            pe.wait_ge(xt_ev_dve, FT // 2 + 1)
            lo, hi = C32["rev"]
            mm(bank(6, NH, REV), relb, const32[:, lo:lo + REV]).then_inc(bias_ps, 1)
            pe.wait_ge(relx_ready, 1)
            lo, hi = C32["far"]
            far = const32[:, lo:hi]
            mm(bank(4, P, NH), far, relb)
            mm(bank(4, P, 1, 16), relrows[:, DT + 1, :], far[:, 0:1])
            for t in range(DT):
                lo = C32["own"][0] + t * NS
                mm(bank(4, HT, NS, 64), relrows[:, t, P - HT:P], const32[:, lo:lo + NS], t == 0, t == DT - 1)
            for t in range(DT):
                lo = C32["last"][0] + t * P
                mm(bank(4, P, P, P), relrows[:, t, :], const32[:, lo:lo + P], t == 0, False)
            mm(bank(4, P, P, P), relrows[:, DT, :], far, False, True).then_inc(bias_ps, 1)

            def mean_squares(dst, tile, done, first):
                for f in range(FT):
                    pe.wait_ge(done, first + f + 1)
                    last = mm(dst, ones[:, :], tile[:, f, :], f == 0, f == FT - 1)
                return last

            pe.wait_ge(dve_init, 2)
            mean_squares(bank(7), hT, sq_done, 0)
            pe.wait_ge(sq_done, FT + 1)
            for f in range(FT):
                last = mm(bank(5, P, NS), ones[:, :], hTs[:, f, :], f == 0, f == FT - 1)
            last.then_inc(ms_ps, 1)

            def w_ready(n):
                pe.wait_ge(w_landed[n % 4], 16 * (n // 4 + 1))

            def modulation(p, n):
                w_ready(n)
                if p == 4:
                    pe.wait_ge(own_ev, 1)
                elif p >= 2:
                    pe.wait_ge(ada_copied, p - 1) if p < 4 else pe.wait_ge(ada_ev, p)
                for k in range(FT):
                    last = quarter(p % 2 if p < 4 else 7, k % QUADS, cT[:, k, :], wslot(n % 4)[:, k, :],
                                   k < QUADS, k >= QUADS)
                last.then_inc(ada_part, 1)

            def fold_modulation(p):
                pe.wait_ge(ada_copied, p + 1)
                if p == 0:
                    pe.wait_ge(xt_ev_act, FT // 2)
                elif p < 4:
                    pe.wait_ge(ada_ev, p)
                for m in range(4):
                    last = mm(bank(2 if p < 4 else 7, P, 1 + DB, m * (1 + DB)), ada_sums[:, m * P:(m + 1) * P],
                              same_row[:, 0:1 + DB])
                last.then_inc(ada_ps, 1)

            pe.wait_ge(xt_ev_act, FT // 2)
            for p in range(4):
                modulation(p, p)
                if p:
                    fold_modulation(p - 1)
            fold_modulation(3)

            def project(g, dst, weights, tile, done, ready):
                for k in range(FT):
                    if ready:
                        pe.wait_ge(h_ready, k + 2)
                    last = mm(dst, weights[:, k, :], tile[:, k, :], k == 0, k == FT - 1)
                if done is not None:
                    last.then_inc(done, 1)

            def proj_bank(g):
                if g >= 2:
                    pe.wait_ge(proj_ev, g - 1)
                return 2 + g % 2

            for n, first, dst in ((4, 0, 4), (5, 4, 5), (6, 8, None), (7, 13, 6)):
                w_ready(n)
                if n == 6:
                    for t in range(TT + 1):
                        tile = hT[:, :, t * P:(t + 1) * P] if t < TT else hTs
                        out = bank(proj_bank(8 + t), P if t < TT else NS)
                        for k in range(FT):
                            last = mm(out, tile[:, k, :], wslot(n % 4)[:, k, :], k == 0, k == FT - 1)
                        last.then_inc(proj_ps, 1)
                    continue
                if n == 4:
                    pe.wait_ge(bias_ev, 5)
                    pe.wait_ge(ada_ev, 4)
                if n == 5:
                    pe.wait_ge(root_done, 2)
                for m in range(4):
                    weights = wslot(n % 4)[:, :, m * P:(m + 1) * P]
                    out = bank(proj_bank(first + m))
                    project(first + m, out, weights, hT, proj_ps, n == 4 and m == 0)
                    pe.wait_ge(h_ready, 1)
                    project(first + m, bank(dst, P, NS, m * NS), weights, hTs, projs_ps if m == 3 else None, False)

            pe.wait_ge(projs_ev, 2)
            pe.wait_ge(root_done, 2)
            for b in range(DB):
                for hp in range(HP):
                    last = mm(bank(7, HT, NS, b * NS), QBD[:, b, hp, :], kTs[:, hp, :], hp == 0, hp == HP - 1)
            last.then_inc(own_ps, 1)

            def scores(a):
                h, i = a // TT, a % TT
                r, hp = slice(HD * (h % 2), HD * (h % 2) + HD), h // 2
                if a >= 2:
                    pe.wait_ge(at_max, a - 1)
                mm(bank(2 + a % 2, P, (i + 1) * P), qT[r, hp, i * P:(i + 1) * P], kT[r, hp, 0:(i + 1) * P])\
                    .then_inc(at_scores, 1)

            def turn_probs(a):
                pe.wait_ge(at_norm, a + 1)
                if a >= 2:
                    pe.wait_ge(at_pT_ev, a - 1)
                for kt in range(a % TT + 1):
                    last = pe.transpose(bank(a % 2, P, P, kt * P), logits[:, a % 2, kt * P:(kt + 1) * P], ident)
                last.then_inc(at_pT, 1)

            def weigh(a):
                h, i = a // TT, a % TT
                r, hp = slice(HD * (h % 2), HD * (h % 2) + HD), h // 2
                pe.wait_ge(at_pT_ev, a + 1)
                if hp >= 2:
                    pe.wait_ge(at_out_ev, hp - 1)
                for kt in range(i + 1):
                    last = mm(PS[r, 4 + hp % 2, i * P:(i + 1) * P], v_tok[:, kt, HD * h:HD * h + HD],
                              pT[:, a % 2, kt * P:(kt + 1) * P], kt == 0, kt == i)
                last.then_inc(at_out, 1)

            def rows(r):
                pe.wait_ge(row_ev, r) if r else pe.wait_ge(projs_ev, 3)
                for c in range(HP):
                    if r < TT:
                        src, n = kT[:, c, r * P:(r + 1) * P], P
                    elif r == TT:
                        src, n = kTs[:, c, :], NS
                    elif r == TT + 1:
                        src, n = uSn[:, c, :], NS
                    else:
                        src, n = uT[:, c, UP - STATE:UP], STATE
                    last = pe.transpose(bank(6, n, P, c * P), src, ident)
                last.then_inc(row_ps, 1)

            pe.wait_ge(bias_back, 16)
            for i in range(4):
                if i >= 2:
                    pe.wait_ge(near_ev, i - 1)
                mm(bank(4 + i % 2), flip, flipped[:, i, :]).then_inc(near_ps, 1)
            pe.wait_ge(near_ev, 4)
            pe.wait_ge(proj_ev, 17)
            pe.wait_ge(ada_ev, 4)
            scores(0)
            for a in range(NH * TT):
                if a + 1 < NH * TT:
                    scores(a + 1)
                turn_probs(a)
                if a >= 1:
                    weigh(a - 1)
                h = a // TT
                if a % TT == 1 and h:
                    fold_modulation(3 + h)
                if a % TT == TT - 1:
                    if h < ROWS:
                        rows(h)
                    modulation(4 + h, 8 + h)
            weigh(NH * TT - 1)
            fold_modulation(3 + NH)

            pe.wait_ge(pool_in, 16)
            pe.wait_ge(win_step, WIN_STEPS)
            pe.wait_ge(row_ev, ROWS)
            pe.wait_ge(ada_ev, 12)
            for g in range(NG):
                if g >= 2:
                    pe.wait_ge(pool_ev, g - 1)
                mm(bank(6 + g % 2), wpool[:, g, :], dT[:, g, :]).then_inc(pool_ps, 1)
            pe.wait_ge(at_out_ev, HP)
            for g in range(NG):
                last = mm(bank(5, P, NS, g * NS), wpool[:, g, :], dS[:, g, :])
            last.then_inc(pools_ps, 1)

            pe.wait_ge(pool_ev, NG)
            pe.wait_ge(at_max, NH * TT)
            for m in range(FT):
                if m % 4 == 0:
                    w_ready(16 + m // 4)
                if m >= 2:
                    pe.wait_ge(out_ev, m - 1)
                for k in range(FT):
                    last = mm(bank(2 + m % 2), wslot(m // 4)[:, k, m % 4 * P:(m % 4 + 1) * P], mixT[:, k, :],
                              k == 0, k == FT - 1)
                last.then_inc(out_ps, 1)
            mean_squares(bank(7), hT, sq2_done, 0).then_inc(ms2_ps, 1)

            def turn_keys(b, n, known):
                j, pg = n // PPB, n % PPB
                slot = j % SLOTS
                if pg == 0:
                    pe.wait_ge(kv_landed[slot], k_landed(b, j) if not known else 16 * PPB * (j // SLOTS + 1))
                if not (known and n < 2):
                    pe.wait_ge(kt_ev, PAGES * b + n - 1)
                for hp in range(HP):
                    last = pe.transpose(bank(pg, P, P, hp * P), ring[:, slot, pg, hp * P:(hp + 1) * P], ident)
                last.then_inc(kt_ps if pg == 0 else kv_used, 1)

            def score_keys(b, u, known):
                pe.wait_ge(kt_ev, PAGES * b + QUADS * (u + 1))
                if u == 0:
                    pe.wait_ge(q_cur, b + 1)
                half = u // 4
                if u % 4 == 0 and not known:
                    pe.wait_ge(sc_ev, 2 * b + half - 1)
                for hp in range(HP):
                    for g in range(QUADS):
                        last = quarter(2 + half, g, qcur[:, hp, :], ktb[:, u % 2, hp, g * P:(g + 1) * P],
                                       hp == 0, hp == HP - 1, P, u % 4 * P)
                last.then_inc(qk, 1)

            def add_sums(b):
                pe.wait_ge(fin_dve, FD * b + 1)
                mm(bank(7, P, BLOCKS), same_row, gsplit[:, :, :].rearrange("p u g -> p (u g)")).then_inc(fin_pe, 1)

            def spread_max(b):
                pe.wait_ge(fin_dve, FD * b + 2)
                mm(bank(7, P, QUADS), same_row, quadmax[:, :]).then_inc(fin_pe, 1)

            def total(b):
                pe.wait_ge(fin_exp, b + 1)
                mm(bank(7, P, 1), same_row, rowsum[:, :])
                pe.transpose(bank(7, NS, P, P), probs[:, UNITS * P:], ident).then_inc(fin_pe, 1)

            def turn_probs(b, half):
                if half == 0:
                    pe.wait_ge(fin_dve, FD * b + 4)
                else:
                    pe.wait_ge(pT_out, 2 * b + 1)
                for u in range(4):
                    lo = (4 * half + u) * P
                    last = pe.transpose(bank(7, P, P, u * P), probs[:, lo:lo + P], ident)
                last.then_inc(fin_pe, 1)

            def up(b, n):
                m, k = n // FT, n % FT
                if n == 0:
                    pe.wait_ge(w_landed[UP_SLOT], 16 * (PRE_USES + b + 1))
                if m >= 2 and k == 0:
                    pe.wait_ge(relu_ev, HP * b + m - 1)
                ins = mm(bank(5 + m % 2), wslot(UP_SLOT)[:, k, m * P:(m + 1) * P], hT[:, k, :], k == 0, k == FT - 1)
                if k == FT - 1:
                    ins.then_inc(up_ps, 1)

            def down(b, m):
                if m == 0:
                    pe.wait_ge(w_landed[DOWN_SLOT], 16 * (PRE_USES + b + 1))
                    pe.wait_ge(sqr_ev, HP * (b + 1))
                if m >= 2:
                    pe.wait_ge(dn_ev, FT * b + m - 1)
                for k in range(HP):
                    last = mm(bank(5 + m % 2), wslot(DOWN_SLOT, D)[:, k, m * P:(m + 1) * P], gT[:, k, :],
                              k == 0, k == HP - 1)
                last.then_inc(dn_ps, 1)

            def weigh_values(b, more):
                pe.wait_ge(pT_out, 2 * b + 2)
                for u in range(UNITS):
                    for g in range(QUADS):
                        n = QUADS * u + g
                        j, pg = n // PPB, n % PPB
                        if pg == 0:
                            pe.wait_ge(kv_landed[j % SLOTS], v_landed(b, j, more))
                        last = quarter(4, g, probsT[:, n * HT:(n + 1) * HT], ring[:, j % SLOTS, pg, :], u == 0,
                                       u == UNITS - 1 and g > 0)
                    last.then_inc(kv_used, PPB)
                    if u < FT - 2:
                        down(b, u)
                quarter(4, 0, probsT[0:NS, UNITS * P:], vS[:, :], False, True).then_inc(pv, 1)
                down(b, FT - 2)
                down(b, FT - 1)
                pe.wait_ge(fin_dve, FD * (b + 1))
                for hp in range(HP):
                    last = mm(bank(7, P, DT, hp * DT), heads_out[:, hp * P:(hp + 1) * P], own_token)
                last.then_inc(fin_pe, 1)

            pe.wait_ge(at_pT_ev, NH * TT)
            pe.wait_ge(out_ev, FT)
            for n in range(PAGES):
                turn_keys(0, n, True)
                if n % QUADS == QUADS - 1 and n > QUADS:
                    score_keys(0, n // QUADS - 1, True)
            score_keys(0, UNITS - 1, True)
            pe.wait_ge(h2_ready, FT)
            pe.wait_ge(root2_done, 1)
            pe.wait_ge(pools_ev, 1)
            with pe.Fori(0, LAST) as b:
                for n in range(PAGES):
                    turn_keys(b + 1, n, False)
                    if n % QUADS == QUADS - 1 and n > QUADS:
                        score_keys(b + 1, n // QUADS - 1, False)
                    if n == 0:
                        add_sums(b)
                    if n == 5:
                        spread_max(b)
                    if n == 13:
                        total(b)
                    if n == 17:
                        turn_probs(b, 0)
                    if n == 20:
                        turn_probs(b, 1)
                    up(b, n)
                score_keys(b + 1, UNITS - 1, False)
                weigh_values(b, True)
            add_sums(LAST)
            for n in range(HP * FT):
                up(LAST, n)
                if n == 7:
                    spread_max(LAST)
                if n == 15:
                    total(LAST)
                if n == 19:
                    turn_probs(LAST, 0)
                if n == 25:
                    turn_probs(LAST, 1)
            weigh_values(LAST, False)

            pe.wait_ge(at_s, DB)
            for c in range(D // PIECE):
                for k in range(FT):
                    last = quarter(c, k % QUADS, mixS[:, k, :], wslot(c)[:, k, :], k < QUADS, k >= QUADS)
            last.then_inc(so_ps, 1)

            def fold(dst, src, m):
                return mm(bank(dst, P, NS, m * NS), src[:, m * P:(m + 1) * P], same_row[:, 0:NS])

            folded_flat = folded.rearrange("p a n -> p (a n)")
            pe.wait_ge(so_copied, 1)
            for m in range(FT):
                last = fold(2, folded_flat, m)
            last.then_inc(so_fold, 1)
            pe.wait_ge(ssq, 1)
            for f in range(FT):
                last = mm(bank(1, P, NS), ones[:, :], hTs[:, f, :], f == 0, f == FT - 1)
            last.then_inc(sms_ps, 1)

            def final_rows(t):
                pe.wait_ge(dn_ev, FT * N_CH) if t < TT else pe.wait_ge(xs_done, 1)
                if t >= 2:
                    pe.wait_ge(fin_y, t - 1)
                for f in range(FT):
                    if t < TT:
                        src, n = xT[:, f, t * P:(t + 1) * P], P
                    else:
                        src, n = xTs[:, f, :], NS
                    last = pe.transpose(bank(4 + 2 * (t % 2) + f // 4, n, P, f % 4 * P), src, ident)
                last.then_inc(fin_ps, 1)

            def tail_landed(i, half):
                if i == 0:
                    slot, uses = (UP_SLOT, DOWN_SLOT)[half], PRE_USES + N_CH
                else:
                    n = 2 * (i - 1) + half
                    slot = n % 4
                    uses = (5 if slot < 2 else PRE_USES + N_CH) + n // 4 + 1
                pe.wait_ge(w_landed[slot], 16 * uses)
                return slot

            pe.wait_ge(h2s_ready, 1)
            for i in range(N_CH):
                slot = tail_landed(i, 0)
                for k in range(FT):
                    last = quarter(0, k % QUADS, hTs[:, k, :], wslot(slot)[:, k, :], k < QUADS, k >= QUADS)
                last.then_inc(sup_ps, 1)
                pe.wait_ge(sup_copied, i + 1)
                for m in range(HP):
                    last = fold(1, up_sums, m)
                last.then_inc(sup_fold, 1)
                slot = tail_landed(i, 1)
                pe.wait_ge(ssqr, i + 1)
                for c in range(D // PIECE):
                    for k in range(HP):
                        last = quarter(2 + c, k, gS[:, i % 2, k, :], wslot(slot, D)[:, k, c * PIECE:(c + 1) * PIECE],
                                       i == 0, i == N_CH - 1)
                last.then_inc(sdn_ps, 1)
                if 1 <= i <= TT:
                    final_rows(i - 1)
            pe.wait_ge(sdn_copied, 1)
            for m in range(FT):
                last = fold(1, folded_flat, m)
            last.then_inc(sdn_fold, 1)
            final_rows(TT)


_INS = ["x_prompt", "x_sample", "cache_k", "cache_v", "state_pool", "page_table", "c_prompt", "c_sample", "w_ada",
        "b_ada", "norm_mix", "w_in", "rel_bias", "w_pool", "pool_scale", "w_out", "norm_mlp", "w_up", "w_down",
        "norm_final"]
_OUTS = [(1, S, D), (DB, DT, D), (1, 1, S, NH, HD), (1, 1, S, NH, HD), (1, 1, STATE, AW), (1, DB, DT, NH, HD),
         (1, DB, DT, NH, HD), (1, DB, STATE, AW)]


def kernel(**inputs):
    import numpy as _np
    import concourse.bacc as _bacc
    from concourse import mybir as _mybir
    from concourse.bass_utils import run_bass_kernel_spmd as _run

    nc = _bacc.Bacc("TRN2", target_bir_lowering=False, num_devices=1)
    arrays, args = {}, []
    host = [(name, _np.ascontiguousarray(inputs[name])) for name in _INS]
    host += list(zip(("shape_c128", "shape_c32", "shape_cmask"), shape_constants()))
    for name, a in host:
        arrays[f"in_{name}_dram"] = a
        args.append(nc.dram_tensor(f"in_{name}_dram", a.shape, _mybir.dt.from_np(a.dtype), kind="ExternalInput").ap())
    for i, shape in enumerate(_OUTS):
        args.append(nc.dram_tensor(f"out_{i}_dram", shape, F32, kind="ExternalOutput").ap())
    decoder_step(nc, *args)
    r = _run(nc, [arrays], core_ids=[0])
    return tuple(r.results[0][f"out_{i}_dram"] for i in range(len(_OUTS)))
```

```python
import math
from contextlib import ExitStack

import numpy as np

import concourse.bass as bass
from concourse import mybir

F32 = mybir.dt.float32
F32R = mybir.dt.float32r
I32 = mybir.dt.int32
ALU = mybir.AluOpType
ACT = mybir.ActivationFunctionType
AX = mybir.AxisListType

P = 128
D = 1024
FT = D // P
S = 512
TT = S // P
DB, DT = 8, 4
NS = DB * DT
NH, HD = 8, 64
AW = NH * HD
HP = AW // P
NG = 4
WINDOWS = (2, 4, 8, 16)
STATE = 15
FF = 4096
PAGES = 32
BLOCKS = 16
PPB = 2
TOPK = 3
HT = NH * DT
NMOD = 6 * FT
SH1, SC1, G1, SH2, SC2, G2 = (i * FT for i in range(6))
EPS = 1e-6
NEG = -1e30
SCALE = HD ** -0.5
PIECE = 512
SLOTS = 4
VEC_MIX, VEC_MLP, VEC_POOL, VECS = NMOD, NMOD + FT, NMOD + 2 * FT, NMOD + 2 * FT + NG
REV = 2 * P + P - 1
C32 = {}
_at = 0
for _name, _n in (("ownmask", DB * NS), ("rev", REV + 1), ("far", P), ("last", DT * P), ("own", DT * NS)):
    C32[_name] = (_at, _at + _n)
    _at += _n
C32_W = _at
QUADS = P // HT
UNITS = PAGES // QUADS
C128 = {}
_at = 0
for _name, _n in (("ident", P), ("inv_count", NG * 16), ("flip", P), ("same_row", P), ("head", NH), ("token", DT),
                  ("pair", 2), ("quad", QUADS), ("lower", BLOCKS * BLOCKS)):
    C128[_name] = (_at, _at + _n)
    _at += _n
C128_W = _at


def bucket(n):
    n = max(n, 0)
    if n < 16:
        return n
    return min(16 + int(math.log(n / 16) / math.log(8) * 16), 31)


def shape_constants():
    c128 = np.zeros((P, C128_W), np.float32)
    part = {name: c128[:, lo:hi] for name, (lo, hi) in C128.items()}
    part["ident"][:] = np.eye(P)
    part["flip"][:] = np.eye(P)[::-1]
    for g, w in enumerate(WINDOWS):
        part["inv_count"][:, 16 * g:16 * g + 16] = 1.0 / np.minimum(np.arange(16) + 1, w)
    for p in range(P):
        part["same_row"][p, p % HT::HT] = 1.0
        part["head"][p, p % HT // DT] = 1.0
        part["token"][p, p % DT] = 1.0
        part["pair"][p, p // HT // PPB] = 1.0
        part["quad"][p, p // HT] = 1.0
    for n in range(BLOCKS):
        part["lower"][:, n * BLOCKS:n * BLOCKS + n] = 1.0
    c32 = np.zeros((32, C32_W), np.float32)
    cmask = np.zeros((NH, REV), np.float32)
    o = C32["rev"][0]
    for i in range(REV):
        rel = 2 * P - 1 - i
        if rel >= 0:
            c32[bucket(rel), o + i] = 1.0
        else:
            cmask[:, i] = NEG
    c32[31, C32["far"][0]:C32["far"][1]] = 1.0
    o = C32["last"][0]
    for t in range(DT):
        for key in range(P):
            c32[bucket(P + t - key), o + t * P + key] = 1.0
    o = C32["own"][0]
    for t in range(DT):
        for r in range(NS):
            c32[bucket(t - r % DT), o + t * NS + r] = 1.0
    o = C32["ownmask"][0]
    for row in range(HT):
        for b in range(DB):
            for key in range(NS):
                if key // DT != b or key % DT > row % DT:
                    c32[row, o + b * NS + key] = NEG
    return c128, c32, cmask


def decoder_step(nc, x_prompt, x_sample, cache_k, cache_v, state_pool, page_table, c_prompt, c_sample, w_ada, b_ada,
                 norm_mix, w_in, rel_bias, w_pool, pool_scale, w_out, norm_mlp, w_up, w_down, norm_final,
                 c128, c32, cmask,
                 y_prompt, y_sample, k_prompt, v_prompt, pool_prompt, k_sample, v_sample, pool_sample):
    ctx = ExitStack()
    with ctx:
        def sb(name, shape, dt=F32):
            return ctx.enter_context(nc.sbuf_tensor(name, shape, dt))

        def sem(name):
            return ctx.enter_context(nc.semaphore(name))

        def shared(suffix, dt, stack):
            sizes = (("hT", [P, FT, S]), ("gT", [P, HP, S]), ("kT", [P, HP, S]), ("rwT", [P, 2 * FT * S]),
                     ("W", [P, 4, 4096]), ("mixT", [P, FT, S]))
            return [stack.enter_context(nc.sbuf_tensor(name + suffix, shape, dt)) for name, shape in sizes]

        with ExitStack() as plain:
            hT, gT, kT, rw, W, mixT = shared("", F32, plain)
        h_lo, g_hi, g_lo, rw_split, W_split, first_hi = shared("_split", F32R, ctx)
        k_pages = rw_split[:, 0:FT * S].rearrange("p (s g n) -> p s g n", s=SLOTS, g=PPB)
        ident_r = sb("ident_r", [P, P], F32R)
        h_hi = rw_split[:, FT * S:2 * FT * S].rearrange("p (f n) -> p f n", f=FT)
        cst = sb("cst", [P, C128_W])

        def const(name):
            return cst[:, C128[name][0]:C128[name][1]]

        ident, flip = const("ident"), const("flip")
        inv_count = const("inv_count").rearrange("p (g c) -> p g c", g=NG)
        same_row, own_head, own_token = const("same_row"), const("head"), const("token")
        own_pair, own_quad = const("pair"), const("quad")
        lower = const("lower").rearrange("p (n m) -> p n m", n=BLOCKS)
        ones = sb("ones", [P, P])
        eps = sb("eps", [P, 1])
        pages = sb("pages", [1, DB * PAGES], I32)
        xT = sb("xT", [P, FT, S])
        ring = rw[:, 0:FT * S].rearrange("p (s g n) -> p s g n", s=SLOTS, g=PPB)
        ktb = mixT[:, :, :].rearrange("p (u h) n -> p u h n", u=2)
        up_sums = kT[:, 2, :]
        scn = sb("scn", [P, NH * 2 * P])
        nearb = scn[:, :].rearrange("p (h n) -> p h n", h=NH)
        sc = scn[:, 0:UNITS * P]
        nfb = scn[:, D:2 * D]
        smp = sb("smp", [P, 2, UNITS * P + NS])
        probs, probsT = smp[:, 0, :], smp[:, 1, :]
        QBD = sb("QBD", [P, DB, HP, HT])
        qcur = sb("qcur", [P, HP, HT])
        xTs = sb("xTs", [P, FT, NS])
        hTs = sb("hTs", [P, FT, NS])
        mixS = sb("mixS", [P, FT, NS])
        kTs = sb("kTs", [P, HP, NS])
        vS = sb("vS", [NS, AW])
        uS = sb("uS", [P, NG, DB, STATE + DT])
        uSn = sb("uSn", [P, NG, NS])
        mods = sb("mods", [P, NMOD, 1 + DB])
        vecs = sb("vecs", [P, VECS])
        cT = sb("cT", [P, FT, HT])
        rstd = sb("rstd", [P, S])
        heads_out = rstd[:, :]
        rstds = sb("rstds", [P, NS])
        farb = sb("farb", [P, NH])
        farr = sb("farr", [P, 1])
        lastr = sb("lastr", [P, P])
        own = sb("own", [P, DB, NS])
        owncur = sb("owncur", [P, NS])
        ownb = sb("ownb", [HT, NS])
        gsum = sb("gsum", [P, UNITS])
        gsplit = sb("gsplit", [P, UNITS, PPB])
        tops = sb("tops", [P, UNITS + 1])
        penalty = sb("penalty", [P, UNITS + 1])
        shift = sb("shift", [P, UNITS + 1])
        gate = sb("gate", [P, BLOCKS])
        cmps = sb("cmps", [P, 2 * BLOCKS * BLOCKS])
        cmpa, cmpb = (cmps[:, i * 256:(i + 1) * 256].rearrange("p (n m) -> p n m", n=BLOCKS) for i in range(2))
        rank = sb("rank", [P, UNITS, PPB])
        wpool = sb("wpool", [P, NG, P])
        rowmax = sb("rowmax", [P, 2])
        quadmax = sb("quadmax", [P, QUADS])
        rowsum = sb("rowsum", [P, 1])
        rden = sb("rden", [P, 1])
        stat = sb("stat", [P, 6])
        mod_a = sb("mod_a", [P, 2, FT, 1 + DB])
        gS = sb("gS", [P, 2, HP, NS])
        tmpS = gS[:, :, :, :].rearrange("p a m n -> p (a m) n")
        fstat = sb("fstat", [P, TT + 1, 2])

        LB = 3
        x_tok = mixT[:, :, :].rearrange("p a b -> p (a b)").rearrange("p (t d) -> p t d", t=TT)
        xs_tok = probs[0:NS, 0:D]
        flipped = gT
        folded = rw[:, 0:D].rearrange("p (a n) -> p a n", a=2)
        sample_sums = rw[:, 2560:3072]
        c_tok = rw[0:1 + DB, 0:D]
        c_sig = rw[0:1 + DB, D:2 * D]
        vec_rows = rw[0:VECS, 2 * D:2 * D + P]
        st_rows = rw[0:DB * STATE, 2304:2304 + AW]
        const32 = rw[0:32, 3072:3072 + C32_W]
        bias_rows = rw[0:NH, 4864:4864 + REV]
        mask_rows = rw[0:NH, 5376:5376 + REV]
        relb = rw[0:32, 5888:5888 + NH]
        relx = rw[0:32, 6144:6144 + 6 * P].rearrange("p (s g h t) -> p s g h t", s=6, g=QUADS, h=NH)
        relrows = rw[0:32, 6144:6144 + 6 * P].rearrange("p (s r) -> p s r", s=6)
        ada_sums = [rw[:, 7168:7168 + PIECE], rstd[:, :]]
        qT = gT
        v_tok = rw[:, 0:2048].rearrange("p (t n) -> p t n", t=TT)
        logits = rw[:, 2048:3584].rearrange("p (a n) -> p a n", a=LB)
        pT = rw[:, 3584:4608].rearrange("p (a n) -> p a n", a=2)
        dT = rw[:, 4608:6656].rearrange("p (g n) -> p g n", g=NG)
        UP = S + 16
        win = [rw[:, 6656:6656 + UP], rw[:, 6656 + UP:6656 + 2 * UP]]
        rows_k = hT[:, 0:TT, :]
        uT = smp[:, :, :].rearrange("p a b -> p (a b)")[:, 0:NG * UP].rearrange("p (g n) -> p g n", g=NG)
        winS = cmps[:, 0:2 * DB * (STATE + DT)].rearrange("p (a b s) -> p a b s", a=2, b=DB)
        dS = sb("dS", [P, NG, NS])
        rows_s = hT[0:NS, TT:TT + 3, :]
        junk = rw[:, 2 * D:3 * D]
        ybuf = [rw[:, (3 + i) * D:(4 + i) * D] for i in range(TT + 1)]
        PS = ctx.enter_context(nc.psum_tensor("PS", [P, 8, 512], F32))

        def bank(i, parts=P, n=512, off=0):
            return PS[0:parts, i, off:off + n]

        def sems(names):
            return [sem(n) for n in names.split()]

        x_in, c_in, vec_in, cst_in, st_in, pool_in, page_in, nf_in = sems(
            "x_in c_in vec_in cst_in st_in pool_in page_in nf_in")
        w_landed = [sem(f"w_landed{i}") for i in range(4)]
        up_landed = [sem(f"up_landed{i}") for i in range(4)]
        tail_landed = [sem(f"tail_landed{i}") for i in range(6)]
        kv_landed = [sem(f"kv_landed{i}") for i in range(SLOTS)]
        bias_out, bias_back, row_out, outs, y_out = sems("bias_out bias_back row_out outs y_out")
        kv_used = sem("kv_used")
        dve_init, qbd_zero, pads, c_exp, c_ready = sems("dve_init qbd_zero pads c_exp c_ready")
        relx_ready, ada_part, ada_copied, ident_ready = sems("relx_ready ada_part ada_copied ident_ready")
        small_ps, small_ev, xt_ps, xt_ev_act, xt_ev_dve = sems("small_ps small_ev xt_ps xt_ev_act xt_ev_dve")
        sq_done, ms_ps, root_done = sems("sq_done ms_ps root_done")
        ada_ps, ada_ev, bias_ps, bias_ev, h_ready = sems("ada_ps ada_ev bias_ps bias_ev h_ready")
        proj_ps, proj_ev, projs_ps, projs_ev = sems("proj_ps proj_ev projs_ps projs_ev")
        near_ps, near_ev = sems("near_ps near_ev")
        hs_ready = sem("hs_ready")
        h_raw, h_high, in_high, in_low, samp_part, samp_copied = sems(
            "h_raw h_high in_high in_low samp_part samp_copied")
        own_ps, own_ev, row_ps, row_ev = sems("own_ps own_ev row_ps row_ev")
        win_step, pool_ps, pool_ev, pools_ps, pools_ev = sems(
            "win_step pool_ps pool_ev pools_ps pools_ev")
        at_scores, at_max, at_exp, at_norm, at_pT, at_pT_ev, at_out, at_out_ev = sems(
            "at_scores at_max at_exp at_norm at_pT at_pT_ev at_out at_out_ev")
        out_ps, out_ev, sq2_done, ms2_ps, root2_done, h2_ready = sems(
            "out_ps out_ev sq2_done ms2_ps root2_done h2_ready")
        dve_chain = sem("dve_chain")
        kt_ps, kt_ev, qk, sc_in, sc_ev, q_cur = sems("kt_ps kt_ev qk sc_in sc_ev q_cur")
        fin_pe, fin_dve, fin_exp, fin_chain, pT_out, pv, at_s = sems("fin_pe fin_dve fin_exp fin_chain pT_out pv at_s")
        up_ps, relu_ev, sqr_ev, dn_ps, dn_ev = sems("up_ps relu_ev sqr_ev dn_ps dn_ev")
        h2_raw, h2_high, g_high, g_low = sems("h2_raw h2_high g_high g_low")
        up_high, up_low, dn_high, dn_low = sems("up_high up_low dn_high dn_low")
        so_ps, so_ev, ssq, sms_ps, sroot, h2s_ready = sems("so_ps so_ev ssq sms_ps sroot h2s_ready")
        so_copied, so_fold, sup_copied, sup_fold, sdn_copied, sdn_fold = sems(
            "so_copied so_fold sup_copied sup_fold sdn_copied sdn_fold")
        sup_ps, srelu, ssqr, sdn_ps, xs_done = sems("sup_ps srelu ssqr sdn_ps xs_done")
        fin_ps, fin_ss, fin_root, fin_y = sems("fin_ps fin_ss fin_root fin_y")

        scratch = nc.dram_tensor("bias_scratch", [NH, REV], F32, kind="Internal").ap()
        block = ctx.enter_context(nc.Block())

        wada = w_ada.rearrange("l (k p) n -> (l p) k n", p=P)
        win_d = w_in.rearrange("l (k p) n -> (l p) k n", p=P)
        wout_d = w_out.rearrange("l (k p) n -> (l p) k n", p=P)
        wup_d = w_up.rearrange("l (k p) n -> (l p) k n", p=P)
        wdown_d = w_down.rearrange("l (c k p) n -> (l c) p k n", p=P, k=PIECE // P)
        ck = cache_k.rearrange("l n p h d -> (l n) p (h d)")
        cv = cache_v.rearrange("l n p h d -> (l n) p (h d)")
        kpd = k_prompt.rearrange("a b (t p) h d -> (a b t) p (h d)", p=P)
        vpd = v_prompt.rearrange("a b (t p) h d -> p (a b t) (h d)", p=P)
        ksd = k_sample.rearrange("a b t h d -> (a b t) (h d)")
        vsd = v_sample.rearrange("a b t h d -> (a b t) (h d)")
        ypd = y_prompt.rearrange("b (t p) d -> (b t) p d", p=P)
        ysd = y_sample.rearrange("b t d -> (b t) d")

        PRE_SLOT = [0, 1, 2, 3, 0, 2, 0, 2] + [1, 0, 3, 2] * 2 + [1, 0]
        N_PRE = 18
        UP_SLOT, DOWN_SLOT = 2, 3
        UP_HIGH, DOWN_HIGH = 0, 1
        PARTS = 4
        PRE_USES = PRE_SLOT.count(DOWN_SLOT)
        N_CH = FF // PIECE

        def pre_piece(n):
            if n < 4:
                return wada[:, :, n * PIECE:(n + 1) * PIECE]
            if n < 8:
                return win_d[:, :, (n - 4) * PIECE:(n - 3) * PIECE]
            if n < 16:
                return wada[:, :, (n - 4) * PIECE:(n - 3) * PIECE]
            return wout_d[:, :, (n - 16) * PIECE:(n - 15) * PIECE]

        def wslot(s, cols=PIECE):
            return W[:, s, :].rearrange("p (k n) -> p k n", n=cols)

        def pre_landed(n):
            return w_landed[PRE_SLOT[n]], 16 * PRE_SLOT[:n + 1].count(PRE_SLOT[n])

        LAST = DB - 1

        def k_seq(b, j):
            return 2 * BLOCKS * b - BLOCKS + j

        def v_seq(b, j, more):
            return 2 * BLOCKS * b + (2 * BLOCKS if more else BLOCKS) + j

        ROUNDS = BLOCKS // SLOTS

        def k_landed(b, j):
            return 16 * PPB * (ROUNDS * (2 * b - 1) + j // SLOTS + 1)

        def v_landed(b, j, more):
            return 16 * PPB * (ROUNDS * (2 * b + (2 if more else 1)) + j // SLOTS + 1)

        tail_slots = [mixT[:, :, :].rearrange("p a b -> p (a b)"), W[:, UP_HIGH, :], W[:, UP_SLOT, :],
                      hT[:, :, :].rearrange("p a b -> p (a b)"), W[:, DOWN_HIGH, :], W[:, DOWN_SLOT, :]]
        TAIL_SLOTS = len(tail_slots)

        def tail_place(n):
            return n if n < 4 else (0, 1, 4, 5, 2, 3)[(n - 4) % TAIL_SLOTS]

        N_TAIL = 2 + 2 * N_CH

        def tail_lands(n):
            at = tail_place(n)
            return tail_landed[at], 16 * [tail_place(i) for i in range(n + 1)].count(at)

        def tail_slot(n, cols=PIECE):
            return tail_slots[tail_place(n)].rearrange("p (k n) -> p k n", n=cols)

        def part(slot, q, memory=W):
            if slot in (UP_SLOT, UP_HIGH):
                return memory[:, slot, :].rearrange("p (k n) -> p k n", n=PIECE)[:, :, q * P:(q + 1) * P]
            return memory[:, slot, 1024 * q:1024 * q + 1024]

        def rows_part(slot, q, memory=W):
            return memory[:, slot, 1024 * q:1024 * q + 1024]

        def split_slot(s, cols=PIECE):
            return W_split[:, s, :].rearrange("p (k n) -> p k n", n=cols)

        ROWS = TT + 3
        FD, FP = 5, 6
        FC = 14
        UP_PASSES = HP * FT * 3
        UP_PAGES = 30
        LATE_UP = 40
        WIN_STEPS = 2 * sum(range(1, NG + 1)) + NG * 5

        @block.sync
        def _(sp):
            sp.dma_start(c_tok[0:1, :], c_prompt).then_inc(c_in, 16)
            sp.dma_start(c_tok[1:1 + DB, :], c_sample).then_inc(c_in, 16)
            sp.dma_start(cst[:, :], c128).then_inc(cst_in, 16)
            sp.dma_start(x_tok, x_prompt.rearrange("b (t p) d -> p (b t) d", p=P)).then_inc(x_in, 16)
            sp.dma_start(xs_tok, x_sample.rearrange("b t d -> (b t) d")).then_inc(x_in, 16)
            for lo, hi, src in ((0, NMOD, b_ada), (VEC_MIX, VEC_MLP, norm_mix), (VEC_MLP, VEC_POOL, norm_mlp),
                                (VEC_POOL, VECS, pool_scale)):
                sp.dma_start(vec_rows[lo:hi, :], src.rearrange("l (k p) -> (l k) p", p=P)).then_inc(vec_in, 16)
            sp.dma_start(st_rows, state_pool.rearrange("l b s c -> (l b s) c")).then_inc(st_in, 16)
            sp.dma_start(const32, c32).then_inc(st_in, 16)
            sp.dma_start(mask_rows, cmask).then_inc(st_in, 16)
            sp.dma_start(relb, rel_bias).then_inc(st_in, 16)
            for n in range(4):
                sp.dma_start(wslot(n), pre_piece(n)).then_inc(w_landed[n], 16)
            sp.dma_start(wpool[:, :, :], w_pool.rearrange("l g c d -> c (l g) d")).then_inc(pool_in, 16)
            sp.dma_start(pages[0:1, :], page_table.rearrange("b n -> (b n)")[None, :]).then_inc(page_in, 16)
            sp.wait_ge(bias_ev, 1)
            sp.dma_start(scratch, bias_rows).then_inc(bias_out, 16)
            sp.wait_ge(bias_out, 16)
            sp.dma_start(flipped[:, :, :].rearrange("p a (b n) -> p (a b) n", b=2),
                         bass.AP(scratch.tensor, 0, [[1, P], [REV, NH], [1, 2 * P]])).then_inc(bias_back, 16)
            piece_used = ([(ada_part, 1), (ada_part, 3), (proj_ps, 4), (proj_ps, 8), (proj_ps, 12), (proj_ps, 12),
                           (proj_ps, 16), (proj_ps, 16)] + [(ada_part, n - 7) for n in range(12, N_PRE)])
            for n in range(4, N_PRE):
                sp.wait_ge(*piece_used[n - 4])
                sp.dma_start(wslot(PRE_SLOT[n]), pre_piece(n)).then_inc(w_landed[PRE_SLOT[n]], 16)
            sp.wait_ge(page_in, 16)

            def load_block(cache, b, j, seq):
                slot = j % SLOTS
                _, phys = nc.values_load_multi_w_load_instructions(pages[0:1, bass.ds(b * PAGES + PPB * j, PPB)],
                                                                   engines=[mybir.EngineType.SP])
                if not (isinstance(seq, int) and seq < SLOTS):
                    sp.wait_ge(kv_used, seq - SLOTS + 1)
                for pg in range(PPB):
                    sp.dma_start(ring[:, slot, pg, :], cache[bass.ds(phys[pg], 1), :, :].rearrange("a p n -> (a p) n"))\
                      .then_inc(kv_landed[slot], 16)

            def load_up(b, m):
                sp.dma_start(wslot(UP_SLOT)[:, :, m * P:(m + 1) * P], wup_d[:, :, bass.ds(b * PIECE + m * P, P)])\
                  .then_inc(up_landed[m], 16)

            def load_down(b):
                sp.dma_start(wslot(DOWN_SLOT, D), wdown_d[bass.ds(b, 1), :, :, :]
                             .rearrange("a p k n -> (a p) k n")).then_inc(w_landed[DOWN_SLOT], 16)

            sp.wait_ge(ada_part, 12)
            for m in range(HP):
                load_up(0, m)
            sp.wait_ge(at_out_ev, HP)
            sp.wait_ge(outs, 16 * 3)
            for j in range(BLOCKS):
                load_block(ck, 0, j, j)
            with sp.Fori(0, LAST) as b:
                for j in range(BLOCKS):
                    load_block(ck, b + 1, j, k_seq(b + 1, j))
                    if j == SLOTS:
                        load_down(b)
                    if j in (8, 12, 15):
                        m = (8, 12, 15).index(j)
                        sp.wait_ge(up_ps, HP * b + m + 1)
                        load_up(b + 1, m)
                for j in range(BLOCKS):
                    load_block(cv, b, j, v_seq(b, j, True))
                    if j == 2:
                        sp.wait_ge(up_ps, HP * (b + 1))
                        load_up(b + 1, HP - 1)
            sp.dma_start(nfb, bass.AP(norm_final.tensor, 0, [[0, P], [1, D]])).then_inc(nf_in, 16)

            def load_tail(n):
                i = n // 2 - 1
                landed = tail_landed[tail_place(n)]
                if n < 2:
                    sp.dma_start(tail_slot(n), wout_d[:, :, n * PIECE:(n + 1) * PIECE]).then_inc(landed, 16)
                elif n % 2 == 0:
                    sp.dma_start(tail_slot(n), wup_d[:, :, i * PIECE:(i + 1) * PIECE]).then_inc(landed, 16)
                else:
                    sp.dma_start(tail_slot(n, D), wdown_d[i, :, :, :]).then_inc(landed, 16)

            for j in range(BLOCKS):
                load_block(cv, LAST, j, v_seq(LAST, j, False))
                if j == SLOTS - 1:
                    sp.wait_ge(dn_ps, FT * LAST)
                    load_down(LAST)
                    sp.wait_ge(qk, UNITS * DB)
                    load_tail(0)
            sp.wait_ge(up_ps, HP * DB)
            for n in (1, 2, 3):
                load_tail(n)
            sp.wait_ge(so_ps, 1)
            load_tail(4)
            load_tail(5)
            sp.wait_ge(dn_ps, FT * DB)
            for n in range(6, N_TAIL):
                if n >= 8:
                    sp.wait_ge((sup_ps, sdn_ps)[n % 2], (n - TAIL_SLOTS) // 2)
                load_tail(n)
            for t in range(TT):
                sp.wait_ge(fin_y, t + 1)
                sp.dma_start(ypd[t, :, :], ybuf[t]).then_inc(y_out, 16)
            sp.wait_ge(fin_y, TT + 1)
            sp.dma_start(ysd, ybuf[TT][0:NS, :]).then_inc(y_out, 16)
            sp.wait_ge(bias_out, 16)
            sp.wait_ge(row_out, 16 * ROWS)
            sp.wait_ge(outs, 16 * 3)
            sp.wait_ge(y_out, 16 * (TT + 1))

        @block.gpsimd
        def _(pool):
            pool.memset(QBD[:, :, :, :], 0.0).then_inc(qbd_zero, 1)
            pool.dma_start(pool_sample[0, :, 0:STATE - DT, :], state_pool[0, :, DT:STATE, :]).then_inc(outs, 16)
            step = [0]

            def chain(ins):
                step[0] += 1
                ins.then_inc(win_step, 1)
                pool.wait_ge(win_step, step[0])

            def stream_low(high, high_done, ready):
                for f in range(FT):
                    pool.wait_ge(high_done, f + 1)
                    pool.tensor_tensor(h_lo[:, f, :], hT[:, f, :], high[:, f, :], ALU.subtract).then_inc(ready, 1)

            stream_low(first_hi, h_high, h_ready)
            pool.wait_ge(proj_ev, 12)
            pool.dma_start(vpd, v_tok).then_inc(outs, 16)
            pool.wait_ge(proj_ev, 16)
            pool.wait_ge(projs_ev, 3)
            pool.dma_start(vsd, vS[:, :]).then_inc(outs, 16)
            pool.wait_ge(pads, 1)
            pool.wait_ge(bias_out, 16)
            for g, w in enumerate(WINDOWS):
                src, sh, n = uT[:, g, :], 1, 0
                while sh < w:
                    lo = 2 * sh - 1
                    chain(pool.tensor_tensor(win[n % 2][:, lo:UP], src[:, lo:UP], src[:, lo - sh:UP - sh], ALU.add))
                    src, sh, n = win[n % 2], 2 * sh, n + 1
                other = win[n % 2]
                chain(pool.tensor_scalar(other[:, 32:UP], src[:, 32:UP], 1.0 / w, None, ALU.mult))
                chain(pool.tensor_tensor(other[:, 16:32], src[:, 16:32], inv_count[:, g, :], ALU.mult))
                chain(pool.tensor_tensor(dT[:, g, :], other[:, 16:UP], uT[:, g, 16:UP], ALU.subtract))
            pool.wait_ge(projs_ev, 4)
            L = STATE + DT
            for g, w in enumerate(WINDOWS):
                src, sh, n = uS[:, g, :, :], 1, 0
                while sh < w:
                    lo = 2 * sh - 1
                    chain(pool.tensor_tensor(winS[:, n % 2, :, lo:L], src[:, :, lo:L], src[:, :, lo - sh:L - sh],
                                             ALU.add))
                    src, sh, n = winS[:, n % 2, :, :], 2 * sh, n + 1
                other = winS[:, n % 2, :, :]
                chain(pool.tensor_scalar(other[:, :, STATE:L], src[:, :, STATE:L], 1.0 / w, None, ALU.mult))
                chain(pool.tensor_tensor(dS[:, g, :].rearrange("p (b t) -> p b t", b=DB), other[:, :, STATE:L],
                                         uS[:, g, :, STATE:L], ALU.subtract))
            for t in range(TT):
                pool.wait_ge(row_ev, t + 1)
                pool.dma_start(kpd[t, :, :], rows_k[:, t, :]).then_inc(row_out, 16)
            pool.wait_ge(row_ev, ROWS)
            pool.dma_start(ksd, rows_s[:, 0, :]).then_inc(row_out, 16)
            pool.dma_start(pool_sample[0, :, STATE - DT:STATE, :], rows_s[:, 1, :]).then_inc(row_out, 16)
            pool.dma_start(pool_prompt[0, 0, :, :], rows_s[0:STATE, 2, :]).then_inc(row_out, 16)

            def take_queries(b, first=False):
                if first:
                    pool.wait_ge(projs_ev, 1)
                else:
                    pool.wait_ge(qk, UNITS * b)
                pool.tensor_copy(qcur[:, :, :], QBD[:, bass.ds(b, 1), :, :].rearrange("p a h c -> p (a h) c"))\
                    .then_inc(q_cur, 1)

            def squares(b):
                for m in range(HP):
                    pool.wait_ge(relu_ev, HP * b + m + 1)
                    pool.tensor_tensor(kT[:, m, :], kT[:, m, :], kT[:, m, :], ALU.mult).then_inc(sqr_ev, 1)
                    pool.wait_ge(sqr_ev, HP * b + m + 1)
                    pool.wait_ge(g_high, HP * b + m + 1)
                    pool.tensor_tensor(g_lo[:, m, :], kT[:, m, :], g_hi[:, m, :], ALU.subtract)\
                        .then_inc(g_low, 1)

            take_queries(0, first=True)
            stream_low(h_hi, h2_high, h2_ready)
            with pool.Fori(0, LAST) as b:
                take_queries(b + 1)
                squares(b)
            squares(LAST)

        @block.scalar
        def _(act):
            act.wait_ge(c_in, 32)
            act.activation(c_sig, c_tok, ACT.Exp, scale=-1.0).then_inc(c_exp, 1)
            for f in range(0, FT, 2):
                act.wait_ge(xt_ps, f + 1)
                act.activation(xT[:, f, :], bank(f % 4), ACT.Copy).then_inc(xt_ev_act, 1)
            act.wait_ge(xt_ev_act, FT // 2)
            act.wait_ge(xt_ev_dve, FT // 2 + 1)
            for f in range(FT):
                act.activation(hT[:, f, :], xT[:, f, :], ACT.Square).then_inc(sq_done, 1)
            act.activation(hTs[:, :, :], xTs[:, :, :], ACT.Square).then_inc(sq_done, 1)
            act.wait_ge(ms_ps, 1)
            act.wait_ge(dve_init, 2)
            act.activation(rstd[:, :], bank(7), ACT.Sqrt, bias=eps[:, 0:1], scale=1.0 / D).then_inc(root_done, 1)
            act.activation(rstds[:, :], bank(5, P, NS), ACT.Sqrt, bias=eps[:, 0:1], scale=1.0 / D)\
               .then_inc(root_done, 1)

            def in_weights_high(i):
                n = 4 + i
                act.wait_ge(*pre_landed(n))
                if i < 2:
                    act.wait_ge(ada_part, 2 * i + 2)
                for q in range(PARTS):
                    act.activation(rows_part(PRE_SLOT[n] + 1, q, W_split), rows_part(PRE_SLOT[n], q), ACT.Copy)\
                       .then_inc(in_high, 1)

            for i in range(4):
                act.wait_ge(near_ps, i + 1)
                act.activation(scn[:, 512 * i:512 * i + 512], bank(6 + i % 2), ACT.Copy).then_inc(near_ev, 1)
            for f in range(FT):
                act.wait_ge(h_raw, f + 1)
                act.activation(first_hi[:, f, :], hT[:, f, :], ACT.Copy).then_inc(h_high, 1)
            in_weights_high(0)
            in_weights_high(1)
            for g in range(16):
                act.wait_ge(proj_ps, g + 1)
                src = bank(2 + g % 2)
                if g < 4:
                    act.activation(qT[:, g, :], src, ACT.Copy, scale=SCALE).then_inc(proj_ev, 1)
                elif g < 8:
                    act.activation(kT[:, g - 4, :], src, ACT.Copy).then_inc(proj_ev, 1)
                elif g < 12:
                    act.activation(v_tok[:, g - 8, :], src, ACT.Copy).then_inc(proj_ev, 1)
                else:
                    if g == 12:
                        act.wait_ge(pads, 1)
                    act.activation(uT[:, g - 12, 16:UP], src, ACT.Copy).then_inc(proj_ev, 1)
                if g == 5:
                    in_weights_high(2)
                if g == 9:
                    in_weights_high(3)

            def attention_out(hp):
                act.activation(mixT[:, hp, :], bank(4 + hp % 2), ACT.Copy).then_inc(at_out_ev, 1)

            def exponentials(a):
                n, s = (a % TT + 1) * P, a % LB
                act.wait_ge(at_max, a + 1)
                act.activation(logits[:, s, 0:n], logits[:, s, 0:n], ACT.Exp, bias=stat[:, s:s + 1],
                               accum_out=stat[:, LB + s:LB + s + 1]).then_inc(at_exp, 1)

            exponentials(0)
            for a in range(NH * TT):
                n = (a % TT + 1) * P
                if a + 1 < NH * TT:
                    exponentials(a + 1)
                act.wait_ge(at_pT, a + 1)
                if a >= 2:
                    act.wait_ge(at_out, a - 1)
                act.activation(pT[:, a % 2, 0:n], bank(a % 2, P, n), ACT.Copy).then_inc(at_pT_ev, 1)
                if a > 2 * TT and a % (2 * TT) == 1:
                    act.wait_ge(at_out, a - 1)
                    attention_out(a // (2 * TT) - 1)
            act.wait_ge(at_out, NH * TT)
            attention_out(HP - 1)
            for g in range(NG):
                act.wait_ge(pool_ps, g + 1)
                act.activation(mixT[:, HP + g, :], bank(6 + g % 2), ACT.Copy,
                               scale=vecs[:, VEC_POOL + g:VEC_POOL + g + 1]).then_inc(pool_ev, 1)
            act.wait_ge(row_out, 16 * ROWS)
            for f in range(FT):
                act.wait_ge(out_ev, f + 1)
                act.activation(hT[:, f, :], xT[:, f, :], ACT.Square).then_inc(sq2_done, 1)
            act.wait_ge(ms2_ps, 1)
            act.activation(rstd[:, :], bank(7), ACT.Sqrt, bias=eps[:, 0:1], scale=1.0 / D).then_inc(root2_done, 1)

            def keys_out(b, n, first=False):
                j, pg, u = n // PPB, n % PPB, n // QUADS
                if pg == 0:
                    act.wait_ge(kt_ps, BLOCKS * b + j + 1)
                else:
                    act.wait_ge(kv_used, (j if first else k_seq(b, j)) + 1)
                if n % QUADS == 0 and not (first and u < 2):
                    act.wait_ge(qk, UNITS * b + u - 1)
                act.activation(ktb[:, u % 2, :, n % QUADS * P:(n % QUADS + 1) * P],
                               bank(pg).rearrange("p (h n) -> p h n", h=HP), ACT.Copy).then_inc(kt_ev, 1)

            def exps(b):
                act.wait_ge(fin_dve, FD * b + 3)
                act.activation(probs, probs, ACT.Exp, accum_out=rowsum[:, 0:1]).then_inc(fin_exp, 1)

            def probs_out(b, half):
                act.wait_ge(fin_pe, FP * b + 4 + half)
                act.activation(probsT[:, 512 * half:512 * half + 512], bank(7), ACT.Copy).then_inc(pT_out, 1)

            def relu(b, m):
                act.wait_ge(up_ps, HP * b + m + 1)
                act.activation(kT[:, m, :], bank(5 + m % 2), ACT.Relu).then_inc(relu_ev, 1)

            def hidden_high(b, m):
                act.wait_ge(sqr_ev, HP * b + m + 1)
                act.activation(g_hi[:, m, :], kT[:, m, :], ACT.Copy).then_inc(g_high, 1)

            def weights_high(b, q, slot, high, done):
                if slot == UP_SLOT:
                    act.wait_ge(up_landed[q], 16 * (b + 1))
                if slot == DOWN_SLOT and q == 0:
                    act.wait_ge(w_landed[slot], 16 * (PRE_USES + b + 1))
                act.activation(part(high, q, W_split), part(slot, q), ACT.Copy).then_inc(done, 1)

            for n in range(PAGES):
                keys_out(0, n, first=True)
                if n % 2 == 1 and n < 2 * FT:
                    f = n // 2
                    act.wait_ge(h2_raw, f + 1)
                    act.activation(h_hi[:, f, :], hT[:, f, :], ACT.Copy).then_inc(h2_high, 1)
                if n in (17, 19, 21, 23):
                    weights_high(0, (n - 17) // 2, UP_SLOT, UP_HIGH, up_high)
            with act.Fori(0, LAST) as b:
                for n in range(PAGES):
                    keys_out(b + 1, n)
                    if n in (9, 16, 24, 31):
                        relu(b, (9, 16, 24, 31).index(n))
                    if n in (11, 18, 26):
                        hidden_high(b, (11, 18, 26).index(n))
                    if n == 12:
                        exps(b)
                    if n == 19:
                        probs_out(b, 0)
                    if n == 23:
                        probs_out(b, 1)
                    if n in (17, 19, 22, 25):
                        weights_high(b, (17, 19, 22, 25).index(n), DOWN_SLOT, DOWN_HIGH, dn_high)
                hidden_high(b, HP - 1)
                for q in range(PARTS):
                    weights_high(b + 1, q, UP_SLOT, UP_HIGH, up_high)
            relu(LAST, 0)
            hidden_high(LAST, 0)
            exps(LAST)
            relu(LAST, 1)
            probs_out(LAST, 0)
            probs_out(LAST, 1)
            hidden_high(LAST, 1)
            for q in range(PARTS):
                weights_high(LAST, q, DOWN_SLOT, DOWN_HIGH, dn_high)
            relu(LAST, 2)
            hidden_high(LAST, 2)
            relu(LAST, 3)
            hidden_high(LAST, 3)

            act.wait_ge(so_ev, 1)
            act.activation(hTs[:, :, :], xTs[:, :, :], ACT.Square).then_inc(ssq, 1)
            act.wait_ge(sms_ps, 1)
            act.activation(rstds[:, :], bank(1, P, NS), ACT.Sqrt, bias=eps[:, 0:1], scale=1.0 / D).then_inc(sroot, 1)

            def final_norm(t):
                n = P if t < TT else NS
                act.wait_ge(fin_ps, t + 1)
                act.activation(junk[0:n, :], PS[0:n, 4 + 2 * (t % 2):6 + 2 * (t % 2), :].rearrange("p a b -> p (a b)"),
                               ACT.Square, accum_out=fstat[0:n, t, 0:1]).then_inc(fin_ss, 1)
                act.wait_ge(fin_ss, t + 1)
                act.activation(fstat[0:n, t, 1:2], fstat[0:n, t, 0:1], ACT.Sqrt, bias=eps[0:n, 0:1], scale=1.0 / D)\
                   .then_inc(fin_root, 1)

            for i in range(N_CH):
                act.wait_ge(sup_fold, i + 1)
                if i >= 2:
                    act.wait_ge(sdn_ps, i - 1)
                act.activation(gS[:, i % 2, :, :].rearrange("p a b -> p (a b)"), bank(1, P, HP * NS), ACT.Relu)\
                   .then_inc(srelu, 1)
                if 1 <= i <= TT:
                    final_norm(i - 1)
            final_norm(TT)

        @block.vector
        def _(dve):
            steps = [0]

            def link(ins):
                steps[0] += 1
                ins.then_inc(dve_chain, 1)
                dve.wait_ge(dve_chain, steps[0])

            dve.memset(ones[:, :], 1.0).then_inc(dve_init, 1)
            dve.memset(eps[:, :], EPS).then_inc(dve_init, 1)
            dve.memset(cT[:, :, :], 0.0).then_inc(dve_init, 1)
            dve.wait_ge(cst_in, 16)
            dve.tensor_copy(ident_r[:, :], ident).then_inc(ident_ready, 1)
            dve.memset(own[:, :, :], NEG).then_inc(dve_init, 1)
            dve.memset(penalty[:, :], 0.0).then_inc(dve_init, 1)
            dve.wait_ge(c_exp, 1)
            link(dve.tensor_scalar(c_sig, c_sig, 1.0, None, ALU.add))
            link(dve.reciprocal(c_sig, c_sig))
            dve.tensor_tensor(c_sig, c_sig, c_tok, ALU.mult).then_inc(c_ready, 1)
            link(dve.memset(relrows, 0.0))
            dve.wait_ge(st_in, 64)
            for t in range(DT):
                dve.tensor_copy(relx[:, t, QUADS - 1, :, t], relb)
            for g in range(QUADS):
                over = relb[:, :, None].to_broadcast([32, NH, DT])
                if g < QUADS - 1:
                    dve.tensor_copy(relx[:, DT, g, :, :], over)
                last = dve.tensor_copy(relx[:, DT + 1, g, :, :], over)
            last.then_inc(relx_ready, 1)
            for f in range(1, FT, 2):
                dve.wait_ge(xt_ps, f + 1)
                dve.tensor_copy(xT[:, f, :], bank(f % 4)).then_inc(xt_ev_dve, 1)
            dve.wait_ge(xt_ps, FT + 1)
            dve.tensor_copy(xTs[:, :, :].rearrange("p a b -> p (a b)"), bank(4, P, FT * NS)).then_inc(xt_ev_dve, 1)
            dve.memset(uT[:, :, 0:16], 0.0).then_inc(pads, 1)
            dve.wait_ge(small_ps, 1)
            dve.wait_ge(dve_init, 3)
            dve.tensor_copy(cT[:, :, 0:1 + DB], bank(5, P, FT * (1 + DB)).rearrange("p (f c) -> p f c", f=FT))\
               .then_inc(small_ev, 1)
            dve.tensor_copy(vecs[:, :], bank(5, P, VECS, 128)).then_inc(small_ev, 1)
            dve.tensor_copy(uS[:, :, :, 0:STATE], bank(6, P, NG * DB * STATE)
                            .rearrange("p (g b s) -> p g b s", g=NG, b=DB)).then_inc(small_ev, 1)
            dve.wait_ge(bias_ps, 1)
            dve.tensor_tensor(bias_rows, bank(6, NH, REV), mask_rows, ALU.add).then_inc(bias_ev, 1)
            dve.wait_ge(bias_ps, 2)
            dve.tensor_copy(farb[:, :], bank(4, P, NH)).then_inc(bias_ev, 1)
            dve.tensor_copy(farr[:, :], bank(4, P, 1, 16)).then_inc(bias_ev, 1)
            dve.tensor_copy(lastr[:, :], bank(4, P, P, P)).then_inc(bias_ev, 1)
            dve.tensor_copy(ownb[:, :], bank(4, HT, NS, 64)).then_inc(bias_ev, 1)

            def ada_out(p):
                dve.wait_ge(ada_part, p + 1)
                if p:
                    dve.wait_ge(ada_ps, p)
                dve.tensor_copy(ada_sums[p >= 4], bank(p % 2 if p < 4 else 7)).then_inc(ada_copied, 1)

            def modulation(p):
                dve.wait_ge(ada_ps, p + 1)
                dve.tensor_tensor(mods[:, 4 * p:4 * p + 4, :],
                                  bank(2 if p < 4 else 7, P, 4 * (1 + DB)).rearrange("p (m c) -> p m c", m=4),
                                  vecs[:, 4 * p:4 * p + 4][:, :, None].to_broadcast([P, 4, 1 + DB]), ALU.add)\
                   .then_inc(ada_ev, 1)

            def weighted(which, scale, vec):
                link(dve.tensor_scalar(mod_a[:, which, :, :], mods[:, scale:scale + FT, :], 1.0, None, ALU.add))
                link(dve.tensor_tensor(mod_a[:, which, :, :], mod_a[:, which, :, :],
                                       vecs[:, vec:vec + FT][:, :, None].to_broadcast([P, FT, 1 + DB]), ALU.mult))

            def per_token(table):
                return table[:, :, 1:1 + DB][:, :, :, None].to_broadcast([P, FT, DB, DT])

            def split(tile):
                return tile[:, :, :].rearrange("p f (b t) -> p f b t", b=DB)

            def modulate_sample(which, shift):
                link(dve.tensor_tensor(hTs[:, :, :], xTs[:, :, :], rstds[:, None, :].to_broadcast([P, FT, NS]), ALU.mult))
                link(dve.tensor_tensor(split(hTs), split(hTs), per_token(mod_a[:, which, :, :]), ALU.mult))
                return dve.tensor_tensor(split(hTs), split(hTs), per_token(mods[:, shift:shift + FT, :]), ALU.add)

            def modulate_prompt(which, shift, raw):
                for f in range(FT):
                    link(dve.tensor_tensor(hT[:, f, :], xT[:, f, :], rstd[:, :], ALU.mult))
                    dve.tensor_scalar(hT[:, f, :], hT[:, f, :], mod_a[:, which, f, 0:1], mods[:, shift + f, 0:1],
                                      ALU.mult, ALU.add).then_inc(raw, 1)

            dve.wait_ge(root_done, 2)
            link(dve.reciprocal(rstd[:, :], rstd[:, :]))
            link(dve.reciprocal(rstds[:, :], rstds[:, :]))
            for p in range(4):
                ada_out(p)
                if p:
                    modulation(p - 1)
            modulation(3)
            dve.wait_ge(ada_ev, 4)
            weighted(0, SC1, VEC_MIX)
            dve.wait_ge(xt_ev_act, FT // 2)
            modulate_sample(0, SH1).then_inc(hs_ready, 1)
            modulate_prompt(0, SH1, h_raw)

            def sample_sums_out(i):
                dve.wait_ge(samp_part, i + 1)
                if i:
                    dve.wait_ge(projs_ps, i)
                dve.tensor_copy(sample_sums, bank(4)).then_inc(samp_copied, 1)

            def in_weights_low(i):
                for q in range(PARTS):
                    dve.wait_ge(in_high, PARTS * i + q + 1)
                    dve.tensor_tensor(rows_part(PRE_SLOT[4 + i], q, W_split), rows_part(PRE_SLOT[4 + i], q),
                                      rows_part(PRE_SLOT[4 + i] + 1, q, W_split), ALU.subtract).then_inc(in_low, 1)

            sample_sums_out(0)
            in_weights_low(0)
            dve.wait_ge(projs_ps, 1)
            dve.wait_ge(qbd_zero, 1)
            for hp in range(HP):
                for half in range(2):
                    r, c = slice(HD * half, HD * half + HD), 2 * DT * hp + DT * half
                    last = dve.tensor_scalar(QBD[r, :, hp, c:c + DT],
                                             PS[r, 5, hp * NS:(hp + 1) * NS].rearrange("p (b t) -> p b t", b=DB),
                                             SCALE, None, ALU.mult)
                    if (hp, half) != (HP - 1, 1):
                        link(last)
            last.then_inc(projs_ev, 1)
            sample_sums_out(1)
            in_weights_low(1)
            dve.wait_ge(projs_ps, 2)
            dve.tensor_copy(kTs[:, :, :].rearrange("p a b -> p (a b)"), bank(5, P, HP * NS, P)).then_inc(projs_ev, 1)
            sample_sums_out(2)
            in_weights_low(2)
            dve.wait_ge(projs_ps, 3)
            dve.tensor_copy(vS[:, :], bank(7, NS)).then_inc(projs_ev, 1)
            sample_sums_out(3)
            in_weights_low(3)
            dve.wait_ge(projs_ps, 4)
            link(dve.tensor_copy(uS[:, :, :, STATE:STATE + DT],
                                 bank(6, P, NG * NS).rearrange("p (g b t) -> p g b t", g=NG, b=DB)))
            dve.tensor_copy(uSn[:, :, :].rearrange("p a b -> p (a b)"), bank(6, P, NG * NS)).then_inc(projs_ev, 1)
            dve.wait_ge(own_ps, 1)
            dve.wait_ge(bias_ev, 5)
            dve.wait_ge(dve_init, 5)
            link(dve.tensor_tensor(own[0:HT, :, :], bank(7, HT, DB * NS).rearrange("p (b c) -> p b c", b=DB),
                                   ownb[:, None, :].to_broadcast([HT, DB, NS]), ALU.add))
            dve.tensor_tensor(own[0:HT, :, :], own[0:HT, :, :], const32[:, C32["ownmask"][0]:C32["ownmask"][1]]
                              .rearrange("p (b c) -> p b c", b=DB), ALU.add).then_inc(own_ev, 1)

            def logits_in(a):
                h, i = a // TT, a % TT
                n, near = (i + 1) * P, P if i == 0 else 2 * P
                s = a % LB
                dve.wait_ge(at_scores, a + 1)
                if a >= LB:
                    dve.wait_ge(at_pT, a - LB + 1)
                src = bank(2 + a % 2)
                if n > near:
                    dve.tensor_scalar(logits[:, s, 0:n - near], src[:, 0:n - near], farb[:, h:h + 1], None,
                                      ALU.add).then_inc(dve_chain, 1)
                    steps[0] += 1
                link(dve.tensor_tensor(logits[:, s, n - near:n], src[:, n - near:n], nearb[:, h, 2 * P - near:2 * P],
                                       ALU.add))
                dve.tensor_reduce(stat[:, s:s + 1], logits[:, s, 0:n], AX.X, ALU.max, negate=True).then_inc(at_max, 1)

            def normalize(a):
                n, s = (a % TT + 1) * P, a % LB
                dve.wait_ge(at_exp, a + 1)
                link(dve.reciprocal(stat[:, LB + s:LB + s + 1], stat[:, LB + s:LB + s + 1]))
                dve.tensor_scalar(logits[:, s, 0:n], logits[:, s, 0:n], stat[:, LB + s:LB + s + 1], None,
                                  ALU.mult).then_inc(at_norm, 1)

            def rows(r):
                dve.wait_ge(row_ps, r + 1)
                if r < TT:
                    dve.tensor_copy(rows_k[:, r, :], bank(6)).then_inc(row_ev, 1)
                else:
                    n = NS if r < TT + 2 else STATE
                    dve.tensor_copy(rows_s[0:n, r - TT, :], bank(6, n)).then_inc(row_ev, 1)

            dve.wait_ge(near_ev, 4)
            logits_in(0)
            logits_in(1)
            for a in range(NH * TT):
                normalize(a)
                if a + 2 < NH * TT:
                    logits_in(a + 2)
                h = a // TT
                if a % TT == 1 and h:
                    modulation(3 + h)
                if a % TT == TT - 1:
                    if h < ROWS:
                        rows(h)
                    ada_out(4 + h)
            modulation(3 + NH)
            dve.wait_ge(pools_ps, 1)
            dve.tensor_tensor(mixS[:, HP:FT, :], bank(5, P, NG * NS).rearrange("p (g n) -> p g n", g=NG),
                              vecs[:, VEC_POOL:VEC_POOL + NG][:, :, None].to_broadcast([P, NG, NS]), ALU.mult)\
               .then_inc(pools_ev, 1)
            dve.wait_ge(ada_ev, 12)
            weighted(1, SC2, VEC_MLP)
            for m in range(FT):
                dve.wait_ge(out_ps, m + 1)
                dve.scalar_tensor_tensor(xT[:, m, :], bank(2 + m % 2), mods[:, G1 + m, 0:1], xT[:, m, :],
                                         ALU.mult, ALU.add).then_inc(out_ev, 1)
            dve.wait_ge(root2_done, 1)
            link(dve.reciprocal(rstd[:, :], rstd[:, :]))
            modulate_prompt(1, SH2, h2_raw)

            def weights_low(b, q, slot, high, high_done, done):
                dve.wait_ge(high_done, PARTS * b + q + 1)
                dve.tensor_tensor(part(slot, q, W_split), part(slot, q), part(high, q, W_split), ALU.subtract)\
                   .then_inc(done, 1)

            def up_weights_low(b, q):
                weights_low(b, q, UP_SLOT, UP_HIGH, up_high, up_low)

            def down_weights_low(b, q):
                weights_low(b, q, DOWN_SLOT, DOWN_HIGH, dn_high, dn_low)

            def scores_out(b, half):
                dve.wait_ge(qk, UNITS * b + 4 * (half + 1))
                src = bank(2 + half)
                lo, mid, hi = 512 * half, 512 * half + (384 if half else 512), 512 * half + 512
                dve.tensor_reduce(gsum[:, 4 * half:4 * half + 4], src.rearrange("p (u n) -> p u n", n=P), AX.X, ALU.add)
                ins = dve.tensor_scalar(sc[:, lo:mid], src[:, 0:mid - lo], farr[:, 0:1], None, ALU.add)
                if half:
                    ins = dve.tensor_tensor(sc[:, mid:hi], src[:, mid - lo:512], lastr[:, :], ALU.add)
                ins.then_inc(sc_in, 1)
                dve.wait_ge(sc_in, 2 * b + half + 1)
                dve.tensor_reduce(tops[:, 4 * half:4 * half + 4], sc[:, lo:hi].rearrange("p (u n) -> p u n", n=P),
                                  AX.X, ALU.max).then_inc(sc_ev, 1)

            def fchain(ins, b, k):
                ins.then_inc(fin_chain, 1)
                dve.wait_ge(fin_chain, FC * b + k)

            def split_sums(b):
                dve.wait_ge(sc_ev, 2 * b + 2)
                dve.tensor_tensor(gsplit[:, :, :], gsum[:, :, None].to_broadcast([P, UNITS, PPB]),
                                  own_pair[:, None, :].to_broadcast([P, UNITS, PPB]), ALU.mult).then_inc(fin_dve, 1)

            def rank_blocks(b):
                dve.tensor_copy(owncur[:, :], own[:, bass.ds(b, 1), :].rearrange("p a c -> p (a c)"))
                dve.wait_ge(fin_pe, FP * b + 1)
                fchain(dve.tensor_copy(gate[:, :], bank(7, P, BLOCKS)), b, 1)
                over_n = gate[:, None, :].to_broadcast([P, BLOCKS, BLOCKS])
                over_m = gate[:, :, None].to_broadcast([P, BLOCKS, BLOCKS])
                dve.tensor_reduce(tops[:, UNITS:UNITS + 1], owncur[:, :], AX.X, ALU.max)
                fchain(dve.tensor_tensor(cmpb, over_n, over_m, ALU.is_equal), b, 2)
                fchain(dve.tensor_tensor(cmpb, cmpb, lower, ALU.mult), b, 3)
                fchain(dve.tensor_tensor(cmpa, over_n, over_m, ALU.is_gt), b, 4)
                fchain(dve.tensor_tensor(cmpa, cmpa, cmpb, ALU.add), b, 5)
                fchain(dve.tensor_reduce(rank[:, :, :].rearrange("p u g -> p (u g)"), cmpa, AX.X, ALU.add), b, 6)
                fchain(dve.tensor_scalar(rank[:, :, :], rank[:, :, :], float(TOPK), NEG, ALU.is_ge, ALU.mult), b, 7)
                fchain(dve.tensor_tensor(rank[:, :, :], rank[:, :, :], own_pair[:, None, :]
                                         .to_broadcast([P, UNITS, PPB]), ALU.mult), b, 8)
                fchain(dve.tensor_reduce(penalty[:, 0:UNITS], rank[:, :, :], AX.X, ALU.add), b, 9)
                fchain(dve.tensor_tensor(shift[:, :], tops[:, :], penalty[:, :], ALU.add), b, 10)
                fchain(dve.tensor_reduce(rowmax[:, 0:1], shift[:, :], AX.X, ALU.max), b, 11)
                dve.tensor_scalar(quadmax[:, :], own_quad, rowmax[:, 0:1], None, ALU.mult).then_inc(fin_dve, 1)

            def less_max(b):
                dve.wait_ge(fin_pe, FP * b + 2)
                fchain(dve.tensor_reduce(rowmax[:, 1:2], bank(7, P, QUADS), AX.X, ALU.max), b, 12)
                fchain(dve.tensor_scalar(shift[:, :], penalty[:, :], rowmax[:, 1:2], None, ALU.subtract), b, 13)
                dve.tensor_tensor(probs[:, 0:UNITS * P].rearrange("p (u n) -> p u n", n=P),
                                  sc.rearrange("p (u n) -> p u n", n=P),
                                  shift[:, 0:UNITS, None].to_broadcast([P, UNITS, P]), ALU.add)
                dve.tensor_scalar(probs[:, UNITS * P:], owncur[:, :], shift[:, UNITS:UNITS + 1], None, ALU.add)\
                   .then_inc(fin_dve, 1)

            def take_total(b):
                dve.wait_ge(fin_pe, FP * b + 3)
                fchain(dve.reciprocal(rden[:, :], bank(7, P, 1)), b, 14)
                dve.tensor_copy(probsT[0:NS, UNITS * P:], bank(7, NS, HT, P)).then_inc(fin_dve, 1)

            def down_out(b, m):
                dve.wait_ge(dn_ps, FT * b + m + 1)
                dve.scalar_tensor_tensor(xT[:, m, :], bank(5 + m % 2), mods[:, G2 + m, 0:1], xT[:, m, :],
                                         ALU.mult, ALU.add).then_inc(dn_ev, 1)

            def own_heads(b):
                dve.wait_ge(pv, b + 1)
                dve.scalar_tensor_tensor(heads_out.rearrange("p (h d) -> p h d", h=NH),
                                         bank(4).rearrange("p (h d) -> p h d", h=NH), rden[:, 0:1],
                                         own_head[:, :, None].to_broadcast([P, NH, HD]), ALU.mult, ALU.mult)\
                   .then_inc(fin_dve, 1)

            def attention_sample(b):
                dve.wait_ge(fin_pe, FP * (b + 1))
                dve.tensor_copy(mixS[:, 0:HP, bass.ds(DT * b, DT)], bank(7, P, HP * DT)
                                .rearrange("p (h t) -> p h t", h=HP)).then_inc(at_s, 1)

            def sequence_end(b):
                for m in range(FT):
                    down_out(b, m)
                    if 1 <= m <= PARTS:
                        up_weights_low(b + 1, m - 1)
                    if m == FT - 3:
                        own_heads(b)
                    if m == FT - 2:
                        attention_sample(b)

            scores_out(0, 0)
            for q in range(PARTS):
                up_weights_low(0, q)
            scores_out(0, 1)
            with dve.Fori(0, LAST) as b:
                split_sums(b)
                rank_blocks(b)
                less_max(b)
                take_total(b)
                for half in range(2):
                    down_weights_low(b, 2 * half)
                    down_weights_low(b, 2 * half + 1)
                    scores_out(b + 1, half)
                sequence_end(b)
            split_sums(LAST)
            rank_blocks(LAST)
            less_max(LAST)
            take_total(LAST)
            for q in range(PARTS):
                down_weights_low(LAST, q)
            own_heads(LAST)
            down_out(LAST, 0)
            attention_sample(LAST)
            down_out(LAST, 1)

            dve.wait_ge(so_ps, 1)
            dve.tensor_copy(folded, PS[:, 0:2, :]).then_inc(so_copied, 1)
            down_out(LAST, 2)
            dve.wait_ge(so_fold, 1)
            link(dve.tensor_tensor(split(tmpS), bank(2, P, FT * NS).rearrange("p (f b t) -> p f b t", f=FT, b=DB),
                                   per_token(mods[:, G1:G1 + FT, :]), ALU.mult))
            dve.tensor_tensor(xTs[:, :, :], xTs[:, :, :], tmpS[:, :, :], ALU.add).then_inc(so_ev, 1)
            down_out(LAST, 3)
            dve.wait_ge(so_ev, 1)
            dve.wait_ge(sroot, 1)
            link(dve.reciprocal(rstds[:, :], rstds[:, :]))
            modulate_sample(1, SH2).then_inc(h2s_ready, 1)
            for m in range(4, FT):
                down_out(LAST, m)

            def final_out(t):
                n = P if t < TT else NS
                dve.wait_ge(fin_root, t + 1)
                if t == 0:
                    dve.wait_ge(nf_in, 16)
                link(dve.reciprocal(fstat[0:n, t, 1:2], fstat[0:n, t, 1:2]))
                src = PS[0:n, 4 + 2 * (t % 2):6 + 2 * (t % 2), :].rearrange("p a b -> p (a b)")
                dve.scalar_tensor_tensor(ybuf[t][0:n, :], src, fstat[0:n, t, 1:2], nfb[0:n, :],
                                         ALU.mult, ALU.mult).then_inc(fin_y, 1)

            for i in range(N_CH):
                dve.wait_ge(sup_ps, i + 1)
                dve.tensor_copy(up_sums, bank(0)).then_inc(sup_copied, 1)
                dve.wait_ge(srelu, i + 1)
                dve.tensor_tensor(gS[:, i % 2, :, :], gS[:, i % 2, :, :], gS[:, i % 2, :, :], ALU.mult)\
                   .then_inc(ssqr, 1)
                if 1 <= i <= TT:
                    final_out(i - 1)
            dve.wait_ge(sdn_ps, N_CH)
            dve.tensor_copy(folded, PS[:, 2:4, :]).then_inc(sdn_copied, 1)
            dve.wait_ge(sdn_fold, 1)
            link(dve.tensor_tensor(split(tmpS), bank(1, P, FT * NS).rearrange("p (f b t) -> p f b t", f=FT, b=DB),
                                   per_token(mods[:, G2:G2 + FT, :]), ALU.mult))
            dve.tensor_tensor(xTs[:, :, :], xTs[:, :, :], tmpS[:, :, :], ALU.add).then_inc(xs_done, 1)
            final_out(TT)

        @block.tensor
        def _(pe):
            def mm(out, lhsT, rhs, start=True, stop=True, **kw):
                return pe.matmul(out, lhsT, rhs, start=start, stop=stop, **kw)

            def quarter(i, g, lhsT, rhs, start, stop, n=512, off=0):
                return mm(PS[HT * g:HT * g + HT, i, off:off + n], lhsT, rhs, start, stop, tile_position=(0, HT * g),
                          skip_group_check=True)

            pe.wait_ge(cst_in, 16)
            pe.wait_ge(x_in, 32)
            for f in range(FT):
                if f >= 4:
                    pe.wait_ge((xt_ev_act, xt_ev_dve)[f % 2], (f - 4) // 2 + 1)
                for t in range(TT):
                    last = pe.transpose(bank(f % 4, P, P, t * P), x_tok[:, t, f * P:(f + 1) * P], ident)
                last.then_inc(xt_ps, 1)
            for f in range(FT):
                last = pe.transpose(bank(4, P, NS, f * NS), xs_tok[:, f * P:(f + 1) * P], ident[0:NS, 0:NS])
            last.then_inc(xt_ps, 1)
            pe.wait_ge(c_ready, 1)
            for f in range(FT):
                pe.transpose(bank(5, P, 1 + DB, f * (1 + DB)), c_sig[:, f * P:(f + 1) * P], ident[0:1 + DB, 0:1 + DB])
            pe.wait_ge(vec_in, 64)
            pe.transpose(bank(5, P, VECS, 128), vec_rows, ident[0:VECS, 0:VECS])
            pe.wait_ge(st_in, 64)
            for g in range(NG):
                last = pe.transpose(bank(6, P, DB * STATE, g * DB * STATE), st_rows[:, g * P:(g + 1) * P],
                                    ident[0:DB * STATE, 0:DB * STATE])
            last.then_inc(small_ps, 1)
            pe.wait_ge(small_ev, 3)
            pe.wait_ge(xt_ev_dve, FT // 2 + 1)
            lo, hi = C32["rev"]
            mm(bank(6, NH, REV), relb, const32[:, lo:lo + REV]).then_inc(bias_ps, 1)
            pe.wait_ge(relx_ready, 1)
            lo, hi = C32["far"]
            far = const32[:, lo:hi]
            mm(bank(4, P, NH), far, relb)
            mm(bank(4, P, 1, 16), relrows[:, DT + 1, :], far[:, 0:1])
            for t in range(DT):
                lo = C32["own"][0] + t * NS
                mm(bank(4, HT, NS, 64), relrows[:, t, P - HT:P], const32[:, lo:lo + NS], t == 0, t == DT - 1)
            for t in range(DT):
                lo = C32["last"][0] + t * P
                mm(bank(4, P, P, P), relrows[:, t, :], const32[:, lo:lo + P], t == 0, False)
            mm(bank(4, P, P, P), relrows[:, DT, :], far, False, True).then_inc(bias_ps, 1)

            def mean_squares(dst, tile, done, first):
                for f in range(FT):
                    pe.wait_ge(done, first + f + 1)
                    last = mm(dst, ones[:, :], tile[:, f, :], f == 0, f == FT - 1)
                return last

            pe.wait_ge(dve_init, 2)
            mean_squares(bank(7), hT, sq_done, 0)
            pe.wait_ge(sq_done, FT + 1)
            for f in range(FT):
                last = mm(bank(5, P, NS), ones[:, :], hTs[:, f, :], f == 0, f == FT - 1)
            last.then_inc(ms_ps, 1)

            def w_ready(n):
                pe.wait_ge(*pre_landed(n))

            def modulation(p, n):
                w_ready(n)
                if p == 4:
                    pe.wait_ge(own_ev, 1)
                elif p >= 2:
                    pe.wait_ge(ada_copied, p - 1) if p < 4 else pe.wait_ge(ada_ev, p)
                for k in range(FT):
                    last = quarter(p % 2 if p < 4 else 7, k % QUADS, cT[:, k, :], wslot(PRE_SLOT[n])[:, k, :],
                                   k < QUADS, k >= QUADS)
                last.then_inc(ada_part, 1)

            def fold_modulation(p):
                pe.wait_ge(ada_copied, p + 1)
                if p == 0:
                    pe.wait_ge(xt_ev_act, FT // 2)
                elif p < 4:
                    pe.wait_ge(ada_ev, p)
                for m in range(4):
                    last = mm(bank(2 if p < 4 else 7, P, 1 + DB, m * (1 + DB)), ada_sums[p >= 4][:, m * P:(m + 1) * P],
                              same_row[:, 0:1 + DB])
                last.then_inc(ada_ps, 1)

            pe.wait_ge(xt_ev_act, FT // 2)
            for p in range(4):
                modulation(p, p)
                if p:
                    fold_modulation(p - 1)
            fold_modulation(3)

            pe.wait_ge(bias_back, 16)
            pe.wait_ge(small_ev, 3)
            pe.wait_ge(bias_ev, 1)
            pe.wait_ge(root_done, 1)
            for i in range(4):
                if i >= 2:
                    pe.wait_ge(near_ev, i - 1)
                mm(bank(6 + i % 2), flip, flipped[:, i, :]).then_inc(near_ps, 1)

            def three_pass(out, w_hi, w_lo, x_hi, x_lo, term, start, stop):
                w, x = ((w_hi, x_hi), (w_hi, x_lo), (w_lo, x_hi))[term]
                return mm(out, w, x, start and term == 0, stop and term == 2)

            def fold_sample(i):
                pe.wait_ge(samp_copied, i + 1)
                if i == 2:
                    mm(bank(7, NS), same_row[:, 0:NS], sample_sums).then_inc(projs_ps, 1)
                    return
                for m in range(4):
                    last = mm(bank((5, 5, 7, 6)[i], P, NS, (i == 1) * P + m * NS), sample_sums[:, m * P:(m + 1) * P],
                              same_row[:, 0:NS])
                last.then_inc(projs_ps, 1)

            pe.wait_ge(hs_ready, 1)
            pe.wait_ge(bias_ev, 5)
            pe.wait_ge(root_done, 2)
            pe.wait_ge(near_ev, 4)
            pe.wait_ge(ada_ev, 4)
            def project_sample(i):
                w_ready(4 + i)
                for k in range(FT):
                    last = quarter(4, k % QUADS, hTs[:, k, :], wslot(PRE_SLOT[4 + i])[:, k, :], k < QUADS, k >= QUADS)
                last.then_inc(samp_part, 1)

            project_sample(0)
            for i in range(4):
                slot = PRE_SLOT[4 + i]
                low, high = split_slot(slot), split_slot(slot + 1)
                for m in range(4):
                    g = 4 * i + m
                    if g >= 2:
                        pe.wait_ge(proj_ev, g - 1)
                    tile = slice(m * P, (m + 1) * P)
                    for k in range(FT):
                        if m == 0 and k % 2 == 0:
                            pe.wait_ge(in_low, PARTS * i + k // 2 + 1)
                        if g == 0:
                            pe.wait_ge(h_ready, k + 1)
                        for term in range(3):
                            if i == 2:
                                last = three_pass(bank(2 + g % 2), first_hi[:, k, tile], h_lo[:, k, tile],
                                                  high[:, k, :], low[:, k, :], term, k == 0, k == FT - 1)
                            else:
                                last = three_pass(bank(2 + g % 2), high[:, k, tile], low[:, k, tile],
                                                  first_hi[:, k, :], h_lo[:, k, :], term, k == 0, k == FT - 1)
                    last.then_inc(proj_ps, 1)
                    if m == 1:
                        fold_sample(i)
                    if m == 2 and i < 3:
                        project_sample(i + 1)

            pe.wait_ge(projs_ev, 2)
            pe.wait_ge(root_done, 2)
            for b in range(DB):
                for hp in range(HP):
                    last = mm(bank(7, HT, NS, b * NS), QBD[:, b, hp, :], kTs[:, hp, :], hp == 0, hp == HP - 1)
            last.then_inc(own_ps, 1)

            def scores(a):
                h, i = a // TT, a % TT
                r, hp = slice(HD * (h % 2), HD * (h % 2) + HD), h // 2
                if a >= 2:
                    pe.wait_ge(at_max, a - 1)
                mm(bank(2 + a % 2, P, (i + 1) * P), qT[r, hp, i * P:(i + 1) * P], kT[r, hp, 0:(i + 1) * P])\
                    .then_inc(at_scores, 1)

            def turn_probs(a):
                pe.wait_ge(at_norm, a + 1)
                if a >= 2:
                    pe.wait_ge(at_pT_ev, a - 1)
                for kt in range(a % TT + 1):
                    last = pe.transpose(bank(a % 2, P, P, kt * P), logits[:, a % LB, kt * P:(kt + 1) * P], ident)
                last.then_inc(at_pT, 1)

            def weigh(a):
                h, i = a // TT, a % TT
                r, hp = slice(HD * (h % 2), HD * (h % 2) + HD), h // 2
                pe.wait_ge(at_pT_ev, a + 1)
                if hp >= 2:
                    pe.wait_ge(at_out_ev, hp - 1)
                for kt in range(i + 1):
                    last = mm(PS[r, 4 + hp % 2, i * P:(i + 1) * P], v_tok[:, kt, HD * h:HD * h + HD],
                              pT[:, a % 2, kt * P:(kt + 1) * P], kt == 0, kt == i)
                last.then_inc(at_out, 1)

            def rows(r):
                pe.wait_ge(row_ev, r) if r else pe.wait_ge(projs_ev, 4)
                for c in range(HP):
                    if r < TT:
                        src, n = kT[:, c, r * P:(r + 1) * P], P
                    elif r == TT:
                        src, n = kTs[:, c, :], NS
                    elif r == TT + 1:
                        src, n = uSn[:, c, :], NS
                    else:
                        src, n = uT[:, c, UP - STATE:UP], STATE
                    last = pe.transpose(bank(6, n, P, c * P), src, ident)
                last.then_inc(row_ps, 1)

            pe.wait_ge(proj_ev, 16)
            pe.wait_ge(ada_ev, 4)
            scores(0)
            scores(1)
            for a in range(NH * TT):
                if a + 2 < NH * TT:
                    scores(a + 2)
                turn_probs(a)
                if a >= 1:
                    weigh(a - 1)
                h = a // TT
                if a % TT == 1 and h:
                    fold_modulation(3 + h)
                if a % TT == TT - 1:
                    if h < ROWS:
                        rows(h)
                    modulation(4 + h, 8 + h)
            weigh(NH * TT - 1)
            fold_modulation(3 + NH)

            pe.wait_ge(pool_in, 16)
            pe.wait_ge(win_step, WIN_STEPS)
            pe.wait_ge(row_ev, ROWS)
            pe.wait_ge(ada_ev, 12)
            for g in range(NG):
                if g >= 2:
                    pe.wait_ge(pool_ev, g - 1)
                mm(bank(6 + g % 2), wpool[:, g, :], dT[:, g, :]).then_inc(pool_ps, 1)
            pe.wait_ge(at_out_ev, HP)
            for g in range(NG):
                last = mm(bank(5, P, NS, g * NS), wpool[:, g, :], dS[:, g, :])
            last.then_inc(pools_ps, 1)

            pe.wait_ge(pool_ev, NG)
            pe.wait_ge(at_max, NH * TT)
            for m in range(FT):
                if m % 4 == 0:
                    w_ready(16 + m // 4)
                if m >= 2:
                    pe.wait_ge(out_ev, m - 1)
                for k in range(FT):
                    last = mm(bank(2 + m % 2), wslot(PRE_SLOT[16 + m // 4])[:, k, m % 4 * P:(m % 4 + 1) * P], mixT[:, k, :],
                              k == 0, k == FT - 1)
                last.then_inc(out_ps, 1)
            mean_squares(bank(7), hT, sq2_done, 0).then_inc(ms2_ps, 1)

            def turn_keys(b, n, known):
                j, pg = n // PPB, n % PPB
                slot = j % SLOTS
                if pg == 0:
                    pe.wait_ge(kv_landed[slot], k_landed(b, j) if not known else 16 * PPB * (j // SLOTS + 1))
                if not (known and n < 2):
                    pe.wait_ge(kt_ev, PAGES * b + n - 1)
                for hp in range(HP):
                    last = pe.transpose(bank(pg, P, P, hp * P).bitcast(F32R), k_pages[:, slot, pg, hp * P:(hp + 1) * P],
                                        ident_r[:, :])
                last.then_inc(kt_ps if pg == 0 else kv_used, 1)

            def score_keys(b, u, known):
                pe.wait_ge(kt_ev, PAGES * b + QUADS * (u + 1))
                if u == 0:
                    pe.wait_ge(q_cur, b + 1)
                half = u // 4
                if u % 4 == 0 and not known:
                    pe.wait_ge(sc_ev, 2 * b + half - 1)
                for hp in range(HP):
                    for g in range(QUADS):
                        last = quarter(2 + half, g, qcur[:, hp, :], ktb[:, u % 2, hp, g * P:(g + 1) * P],
                                       hp == 0, hp == HP - 1, P, u % 4 * P)
                last.then_inc(qk, 1)

            def add_sums(b):
                pe.wait_ge(fin_dve, FD * b + 1)
                mm(bank(7, P, BLOCKS), same_row, gsplit[:, :, :].rearrange("p u g -> p (u g)")).then_inc(fin_pe, 1)

            def spread_max(b):
                pe.wait_ge(fin_dve, FD * b + 2)
                mm(bank(7, P, QUADS), same_row, quadmax[:, :]).then_inc(fin_pe, 1)

            def total(b):
                pe.wait_ge(fin_exp, b + 1)
                mm(bank(7, P, 1), same_row, rowsum[:, :])
                pe.transpose(bank(7, NS, P, P), probs[:, UNITS * P:], ident).then_inc(fin_pe, 1)

            def turn_probs(b, half):
                if half == 0:
                    pe.wait_ge(fin_dve, FD * b + 4)
                else:
                    pe.wait_ge(pT_out, 2 * b + 1)
                for u in range(4):
                    lo = (4 * half + u) * P
                    last = pe.transpose(bank(7, P, P, u * P), probs[:, lo:lo + P], ident)
                last.then_inc(fin_pe, 1)

            def up(b, first, end):
                for i in range(first, end):
                    m, k, term = i // (3 * FT), i % (3 * FT) // 3, i % 3
                    if i % (3 * FT) == 0:
                        pe.wait_ge(up_low, PARTS * b + m + 1)
                    if m >= 2 and i % (3 * FT) == 0:
                        pe.wait_ge(relu_ev, HP * b + m - 1)
                    cols = slice(m * P, (m + 1) * P)
                    ins = three_pass(bank(5 + m % 2), split_slot(UP_HIGH)[:, k, cols], split_slot(UP_SLOT)[:, k, cols],
                                     h_hi[:, k, :], h_lo[:, k, :], term, k == 0, k == FT - 1)
                    if i % (3 * FT) == 3 * FT - 1:
                        ins.then_inc(up_ps, 1)

            def down(b, m):
                if m == 0:
                    pe.wait_ge(dn_low, PARTS * (b + 1))
                    pe.wait_ge(g_low, HP * (b + 1))
                if m >= 2:
                    pe.wait_ge(dn_ev, FT * b + m - 1)
                cols = slice(m * P, (m + 1) * P)
                for k in range(HP):
                    for term in range(3):
                        last = three_pass(bank(5 + m % 2), split_slot(DOWN_HIGH, D)[:, k, cols],
                                          split_slot(DOWN_SLOT, D)[:, k, cols], g_hi[:, k, :], g_lo[:, k, :], term,
                                          k == 0, k == HP - 1)
                last.then_inc(dn_ps, 1)

            def weigh_values(b, more):
                pe.wait_ge(pT_out, 2 * b + 2)
                for u in range(UNITS):
                    for g in range(QUADS):
                        n = QUADS * u + g
                        j, pg = n // PPB, n % PPB
                        if pg == 0:
                            pe.wait_ge(kv_landed[j % SLOTS], v_landed(b, j, more))
                        last = quarter(4, g, probsT[:, n * HT:(n + 1) * HT], ring[:, j % SLOTS, pg, :], u == 0,
                                       u == UNITS - 1 and g > 0)
                    last.then_inc(kv_used, PPB)
                    if more and 1 <= u < FT - 1:
                        down(b, u - 1)
                    if not more and u < LATE_UP // 8:
                        up(b, UP_PASSES - LATE_UP + 8 * u, UP_PASSES - LATE_UP + 8 * u + 8)
                quarter(4, 0, probsT[0:NS, UNITS * P:], vS[:, :], False, True).then_inc(pv, 1)
                down(b, FT - 2 if more else 0)
                pe.wait_ge(fin_dve, FD * (b + 1))
                for hp in range(HP):
                    last = mm(bank(7, P, DT, hp * DT), heads_out[:, hp * P:(hp + 1) * P], own_token)
                last.then_inc(fin_pe, 1)
                down(b, FT - 1 if more else 1)

            pe.wait_ge(at_pT_ev, NH * TT)
            pe.wait_ge(out_ev, FT)
            pe.wait_ge(ident_ready, 1)
            for n in range(PAGES):
                turn_keys(0, n, True)
                if n % QUADS == QUADS - 1 and n > QUADS:
                    score_keys(0, n // QUADS - 1, True)
            score_keys(0, UNITS - 1, True)
            pe.wait_ge(h2_ready, FT)
            pe.wait_ge(root2_done, 1)
            pe.wait_ge(pools_ev, 1)
            with pe.Fori(0, LAST) as b:
                for n in range(PAGES):
                    turn_keys(b + 1, n, False)
                    if n % QUADS == QUADS - 1 and n > QUADS:
                        score_keys(b + 1, n // QUADS - 1, False)
                    if n == 1:
                        add_sums(b)
                    if n == 5:
                        spread_max(b)
                    if n == 15:
                        total(b)
                    if n == 18:
                        turn_probs(b, 0)
                    if n == 22:
                        turn_probs(b, 1)
                    if 1 <= n <= UP_PAGES:
                        up(b, UP_PASSES * (n - 1) // UP_PAGES, UP_PASSES * n // UP_PAGES)
                score_keys(b + 1, UNITS - 1, False)
                weigh_values(b, True)
            add_sums(LAST)
            for n in range((UP_PASSES - LATE_UP) // 8):
                up(LAST, 8 * n, 8 * n + 8)
                if n == 2:
                    spread_max(LAST)
                if n == 4:
                    total(LAST)
                if n == 5:
                    turn_probs(LAST, 0)
                if n == 6:
                    turn_probs(LAST, 1)
            weigh_values(LAST, False)

            def piece_landed(n):
                pe.wait_ge(*tail_lands(n))

            pe.wait_ge(at_s, DB)
            for c in range(D // PIECE):
                piece_landed(c)
                for k in range(FT):
                    last = quarter(c, k % QUADS, mixS[:, k, :], tail_slot(c)[:, k, :], k < QUADS, k >= QUADS)
            last.then_inc(so_ps, 1)

            def fold(dst, src, m):
                return mm(bank(dst, P, NS, m * NS), src[:, m * P:(m + 1) * P], same_row[:, 0:NS])

            down(LAST, 2)
            folded_flat = folded.rearrange("p a n -> p (a n)")
            pe.wait_ge(so_copied, 1)
            for m in range(FT):
                last = fold(2, folded_flat, m)
            last.then_inc(so_fold, 1)
            down(LAST, 3)
            pe.wait_ge(ssq, 1)
            for f in range(FT):
                last = mm(bank(1, P, NS), ones[:, :], hTs[:, f, :], f == 0, f == FT - 1)
            last.then_inc(sms_ps, 1)
            for m in range(4, FT):
                down(LAST, m)

            def final_rows(t):
                pe.wait_ge(dn_ev, FT * N_CH) if t < TT else pe.wait_ge(xs_done, 1)
                if t >= 2:
                    pe.wait_ge(fin_y, t - 1)
                for f in range(FT):
                    if t < TT:
                        src, n = xT[:, f, t * P:(t + 1) * P], P
                    else:
                        src, n = xTs[:, f, :], NS
                    last = pe.transpose(bank(4 + 2 * (t % 2) + f // 4, n, P, f % 4 * P), src, ident)
                last.then_inc(fin_ps, 1)

            pe.wait_ge(h2s_ready, 1)
            for i in range(N_CH):
                piece_landed(2 + 2 * i)
                for k in range(FT):
                    last = quarter(0, k % QUADS, hTs[:, k, :], tail_slot(2 + 2 * i)[:, k, :], k < QUADS, k >= QUADS)
                last.then_inc(sup_ps, 1)
                pe.wait_ge(sup_copied, i + 1)
                for m in range(HP):
                    last = fold(1, up_sums, m)
                last.then_inc(sup_fold, 1)
                piece_landed(3 + 2 * i)
                pe.wait_ge(ssqr, i + 1)
                for c in range(D // PIECE):
                    for k in range(HP):
                        last = quarter(2 + c, k, gS[:, i % 2, k, :],
                                       tail_slot(3 + 2 * i, D)[:, k, c * PIECE:(c + 1) * PIECE], i == 0, i == N_CH - 1)
                last.then_inc(sdn_ps, 1)
                if 1 <= i <= TT:
                    final_rows(i - 1)
            pe.wait_ge(sdn_copied, 1)
            for m in range(FT):
                last = fold(1, folded_flat, m)
            last.then_inc(sdn_fold, 1)
            final_rows(TT)


_INS = ["x_prompt", "x_sample", "cache_k", "cache_v", "state_pool", "page_table", "c_prompt", "c_sample", "w_ada",
        "b_ada", "norm_mix", "w_in", "rel_bias", "w_pool", "pool_scale", "w_out", "norm_mlp", "w_up", "w_down",
        "norm_final"]
_OUTS = [(1, S, D), (DB, DT, D), (1, 1, S, NH, HD), (1, 1, S, NH, HD), (1, 1, STATE, AW), (1, DB, DT, NH, HD),
         (1, DB, DT, NH, HD), (1, DB, STATE, AW)]


def kernel(**inputs):
    import numpy as _np
    import concourse.bacc as _bacc
    from concourse import mybir as _mybir
    from concourse.bass_utils import run_bass_kernel_spmd as _run

    nc = _bacc.Bacc("TRN2", target_bir_lowering=False, num_devices=1)
    arrays, args = {}, []
    host = [(name, _np.ascontiguousarray(inputs[name])) for name in _INS]
    host += list(zip(("shape_c128", "shape_c32", "shape_cmask"), shape_constants()))
    for name, a in host:
        arrays[f"in_{name}_dram"] = a
        args.append(nc.dram_tensor(f"in_{name}_dram", a.shape, _mybir.dt.from_np(a.dtype), kind="ExternalInput").ap())
    for i, shape in enumerate(_OUTS):
        args.append(nc.dram_tensor(f"out_{i}_dram", shape, F32, kind="ExternalOutput").ap())
    decoder_step(nc, *args)
    r = _run(nc, [arrays], core_ids=[0])
    return tuple(r.results[0][f"out_{i}_dram"] for i in range(len(_OUTS)))
```
